# Optimizing a Trainium2 kernel written in Bass

```python
import math
import jax, jax.numpy as jnp
from jax import lax
import numpy as np

D_MODEL = 1024
BATCH = 1
SEQ = 256
DEPTH = 2

CHUNK = 64
Q_BLOCK = 128
ROPE_THETA = 10000.0
EPS = 1e-6

HG_HEADS = 4
HG_DIM = 128
HG_WIDTH = HG_HEADS * HG_DIM
AT_HEADS = 8
AT_KV_HEADS = 2
AT_DIM = 64
AT_WIDTH = AT_HEADS * AT_DIM
KV_WIDTH = AT_KV_HEADS * AT_DIM
IDX_HEADS = 4
IDX_DIM = 64
TOPK_MAX = 256
EVEN_IN = 4 * HG_WIDTH + AT_WIDTH + 2 * KV_WIDTH + IDX_HEADS * IDX_DIM + IDX_DIM + IDX_HEADS
MIX_WIDTH = HG_WIDTH + AT_WIDTH

SSM_INNER = 2 * D_MODEL
SSM_HEAD_DIM = 64
SSM_HEADS = SSM_INNER // SSM_HEAD_DIM
SSM_GROUPS = 4
SSM_STATE = 128
SSM_CONV = 4
SSM_CONV_CH = SSM_INNER + 2 * SSM_GROUPS * SSM_STATE
ODD_IN = SSM_INNER + SSM_CONV_CH + SSM_HEADS

MOE_GROUPS = 4
MOE_PER_GROUP = 8
MOE_EXPERTS = MOE_GROUPS * MOE_PER_GROUP
MOE_TOPK = 2
MOE_FF = 512

N_EVEN = (DEPTH + 1) // 2
N_ODD = DEPTH // 2

kernel_name = "hybrid_hgrn2_dsa_mamba2_hmoe"

def _offsets(sizes):
    out, acc = [], 0
    for s in sizes[:-1]:
        acc += s
        out.append(acc)
    return out

def rmsnorm(x, g):
    xf = x.astype(jnp.float32)
    y = xf * lax.rsqrt(jnp.mean(xf * xf, axis=-1, keepdims=True) + EPS)
    return (y * g.astype(jnp.float32)).astype(x.dtype)

def rope(x, pos):
    half = x.shape[-1] // 2
    inv = jnp.exp(-math.log(ROPE_THETA) * jnp.arange(half, dtype=jnp.float32) / half)
    ang = pos.astype(jnp.float32)[:, None] * inv[None, :]
    cos = jnp.cos(ang)[:, None, :]
    sin = jnp.sin(ang)[:, None, :]
    xf = x.astype(jnp.float32)
    x1, x2 = xf[..., :half], xf[..., half:]
    return jnp.concatenate([x1 * cos - x2 * sin, x2 * cos + x1 * sin], axis=-1).astype(x.dtype)

def hgrn2_scan(q, k, v, logf):
    B, S, H, K = q.shape
    V = v.shape[-1]
    n = S // CHUNK

    def to_chunks(a):
        return a.astype(jnp.float32).reshape(B, n, CHUNK, H, a.shape[-1]).transpose(1, 0, 3, 2, 4)

    qc, kc, vc, gc = to_chunks(q), to_chunks(k), to_chunks(v), to_chunks(logf)
    causal = jnp.tril(jnp.ones((CHUNK, CHUNK), dtype=bool))

    def step(state, inp):
        qi, ki, vi, gi = inp
        b = jnp.cumsum(gi, axis=2)
        diff = b[:, :, :, None, :] - b[:, :, None, :, :]
        decay = jnp.exp(jnp.where(causal[:, :, None], diff, -jnp.inf))
        attn = jnp.einsum('bhtk,bhsk,bhtsk->bhts', qi, ki, decay)
        o = jnp.einsum('bhts,bhsv->bhtv', attn, vi)
        o = o + jnp.einsum('bhtk,bhkv->bhtv', qi * jnp.exp(b), state)
        b_last = b[:, :, -1:, :]
        state = state * jnp.exp(b_last)[:, :, 0, :, None] + jnp.einsum(
            'bhsk,bhsv->bhkv', ki * jnp.exp(b_last - b), vi)
        return state, o

    state0 = jnp.zeros((B, H, K, V), jnp.float32)
    _, o = lax.scan(step, state0, (qc, kc, vc, gc))
    return o.transpose(1, 0, 3, 2, 4).reshape(B, S, H, V)

def dsa_attention(q, k, v, iq, ik, iw):
    B, S = q.shape[0], q.shape[1]
    topk = min(TOPK_MAX, S // 4)
    nb = S // Q_BLOCK
    grp = AT_HEADS // AT_KV_HEADS
    key_chunk = jnp.arange(S) // CHUNK
    ikf = ik.astype(jnp.float32)

    def blk(args):
        qb, iqb, iwb, qchunk = args
        sc = jnp.einsum('bqhd,bsd->bqhs', iqb.astype(jnp.float32), ikf) * (IDX_DIM ** -0.5)
        score = jnp.einsum('bqh,bqhs->bqs', iwb.astype(jnp.float32), jax.nn.relu(sc))
        adm = key_chunk[None, :] <= qchunk[:, None]
        score = jnp.where(adm[None], score, -jnp.inf)
        _, idx = lax.top_k(score, topk)
        valid = key_chunk[idx] <= qchunk[None, :, None]
        ks = jax.vmap(lambda a, i: a[i])(k, idx)
        vs = jax.vmap(lambda a, i: a[i])(v, idx)
        qg = qb.reshape(B, Q_BLOCK, AT_KV_HEADS, grp, AT_DIM).astype(jnp.float32)
        s = jnp.einsum('bqhgd,bqnhd->bqhgn', qg, ks.astype(jnp.float32)) * (AT_DIM ** -0.5)
        s = jnp.where(valid[:, :, None, None, :], s, -jnp.inf)
        p = jax.nn.softmax(s, axis=-1)
        o = jnp.einsum('bqhgn,bqnhd->bqhgd', p, vs.astype(jnp.float32))
        return o.reshape(B, Q_BLOCK, AT_WIDTH).astype(q.dtype)

    qb = q.reshape(B, nb, Q_BLOCK, AT_HEADS, AT_DIM).transpose(1, 0, 2, 3, 4)
    iqb = iq.reshape(B, nb, Q_BLOCK, IDX_HEADS, IDX_DIM).transpose(1, 0, 2, 3, 4)
    iwb = iw.reshape(B, nb, Q_BLOCK, IDX_HEADS).transpose(1, 0, 2, 3)
    qchunks = key_chunk.reshape(nb, Q_BLOCK)
    out = lax.map(blk, (qb, iqb, iwb, qchunks))
    return out.transpose(1, 0, 2, 3).reshape(B, S, AT_WIDTH)

def even_mixer(h, w_in, lb, hg_norm, q_norm, k_norm, w_out, pos):
    B, S, _ = h.shape
    sizes = [HG_WIDTH] * 4 + [AT_WIDTH, KV_WIDTH, KV_WIDTH, IDX_HEADS * IDX_DIM, IDX_DIM, IDX_HEADS]
    proj = h @ w_in
    hq, hf, hi, hg, aq, ak, av, iq, ik, iw = jnp.split(proj, _offsets(sizes), axis=-1)
    hf32 = hf.astype(jnp.float32)
    lb32 = lb.astype(jnp.float32)
    f = lb32 + (1.0 - lb32) * jax.nn.sigmoid(hf32)
    kk = (1.0 - lb32) * jax.nn.sigmoid(-hf32)
    hshape = (B, S, HG_HEADS, HG_DIM)
    o_h = hgrn2_scan(hq.reshape(hshape), kk.reshape(hshape), hi.reshape(hshape), jnp.log(f).reshape(hshape))
    o_h = rmsnorm(o_h, hg_norm.reshape(HG_HEADS, HG_DIM)) * jax.nn.silu(hg.reshape(hshape).astype(jnp.float32))
    o_h = o_h.reshape(B, S, HG_WIDTH).astype(h.dtype)
    q = rope(rmsnorm(aq.reshape(B, S, AT_HEADS, AT_DIM), q_norm), pos)
    k = rope(rmsnorm(ak.reshape(B, S, AT_KV_HEADS, AT_DIM), k_norm), pos)
    v = av.reshape(B, S, AT_KV_HEADS, AT_DIM)
    iq = rope(iq.reshape(B, S, IDX_HEADS, IDX_DIM), pos)
    ik = rope(ik.reshape(B, S, 1, IDX_DIM), pos)[:, :, 0]
    o_a = dsa_attention(q, k, v, iq, ik, iw)
    o = jnp.concatenate([o_h, o_a], axis=-1)
    return o @ w_out

def causal_conv(x, w, b):
    C = x.shape[-1]
    y = lax.conv_general_dilated(x, w[:, None, :].astype(x.dtype), window_strides=(1,),
                                 padding=[(SSM_CONV - 1, 0)],
                                 dimension_numbers=('NWC', 'WIO', 'NWC'),
                                 feature_group_count=C)
    return y + b

def ssd_scan(x, dt, A, Bm, Cm):
    B, S, H, P = x.shape
    G, N = Bm.shape[2], Bm.shape[3]
    R = H // G
    n = S // CHUNK
    xdt = (x.astype(jnp.float32) * dt[..., None]).reshape(B, n, CHUNK, G, R, P).transpose(1, 0, 2, 3, 4, 5)
    dA = (dt * A.astype(jnp.float32)).reshape(B, n, CHUNK, G, R).transpose(1, 0, 2, 3, 4)
    bc = Bm.astype(jnp.float32).reshape(B, n, CHUNK, G, N).transpose(1, 0, 2, 3, 4)
    cc = Cm.astype(jnp.float32).reshape(B, n, CHUNK, G, N).transpose(1, 0, 2, 3, 4)
    causal = jnp.tril(jnp.ones((CHUNK, CHUNK), dtype=bool))

    def step(state, inp):
        xi, ai, bi, ci = inp
        cum = jnp.cumsum(ai, axis=1)
        seg = cum[:, :, None] - cum[:, None, :]
        L = jnp.exp(jnp.where(causal[None, :, :, None, None], seg, -jnp.inf))
        cb = jnp.einsum('btgn,bsgn->btsg', ci, bi)
        y = jnp.einsum('btsg,btsgr,bsgrp->btgrp', cb, L, xi)
        y = y + jnp.einsum('btgn,bgrpn->btgrp', ci, state) * jnp.exp(cum)[..., None]
        to_end = jnp.exp(cum[:, -1:] - cum)
        state = state * jnp.exp(cum[:, -1])[..., None, None] + jnp.einsum(
            'bsgn,bsgr,bsgrp->bgrpn', bi, to_end, xi)
        return state, y

    state0 = jnp.zeros((B, G, R, P, N), jnp.float32)
    _, y = lax.scan(step, state0, (xdt, dA, bc, cc))
    return y.transpose(1, 0, 2, 3, 4, 5).reshape(B, S, H, P)

def odd_mixer(h, w_in, conv_w, conv_b, dt_bias, A_log, D_skip, norm_g, w_out):
    B, S, _ = h.shape
    proj = h @ w_in
    z, xBC, dt = jnp.split(proj, [SSM_INNER, SSM_INNER + SSM_CONV_CH], axis=-1)
    xBC = jax.nn.silu(causal_conv(xBC, conv_w, conv_b))
    xs, Bm, Cm = jnp.split(xBC, [SSM_INNER, SSM_INNER + SSM_GROUPS * SSM_STATE], axis=-1)
    dt = jax.nn.softplus(dt.astype(jnp.float32) + dt_bias.astype(jnp.float32))
    A = -jnp.exp(A_log.astype(jnp.float32))
    xs = xs.reshape(B, S, SSM_HEADS, SSM_HEAD_DIM)
    y = ssd_scan(xs, dt, A, Bm.reshape(B, S, SSM_GROUPS, SSM_STATE), Cm.reshape(B, S, SSM_GROUPS, SSM_STATE))
    y = y + D_skip.astype(jnp.float32)[:, None] * xs.astype(jnp.float32)
    y = y.reshape(B, S, SSM_INNER) * jax.nn.silu(z.astype(jnp.float32))
    gsz = SSM_INNER // SSM_GROUPS
    y = rmsnorm(y.reshape(B, S, SSM_GROUPS, gsz), norm_g.reshape(SSM_GROUPS, gsz))
    return y.reshape(B, S, SSM_INNER).astype(h.dtype) @ w_out

def hier_moe(h, wg, bg, we, be, w1, w3, w2):
    B, S, D = h.shape
    t = h.reshape(-1, D)
    T = t.shape[0]
    gprob = jax.nn.softmax((t @ wg).astype(jnp.float32) + bg.astype(jnp.float32), axis=-1)
    gval, gidx = lax.top_k(gprob, 1)
    elog = ((t @ we).astype(jnp.float32) + be.astype(jnp.float32)).reshape(T, MOE_GROUPS, MOE_PER_GROUP)
    elog = jnp.take_along_axis(elog, gidx[:, :, None], axis=1)[:, 0]
    eprob = jax.nn.softmax(elog, axis=-1)
    ev, ei = lax.top_k(eprob, MOE_TOPK)
    ev = ev / jnp.sum(ev, axis=-1, keepdims=True)
    weight = gval * ev
    flat = gidx * MOE_PER_GROUP + ei
    gate = jnp.sum(jax.nn.one_hot(flat, MOE_EXPERTS, dtype=jnp.float32) * weight[..., None], axis=1)
    y = jnp.zeros((T, D), jnp.float32)
    for e in range(MOE_EXPERTS):
        he = jax.nn.silu(t @ w1[e]) * (t @ w3[e])
        y = y + gate[:, e:e + 1] * (he @ w2[e]).astype(jnp.float32)
    return y.reshape(B, S, D).astype(h.dtype)

def setup_inputs(seed: int = 0) -> dict:
    key = jax.random.key(seed)
    ks = jax.random.split(key, 24)
    nrm = jax.random.normal
    f32 = jnp.float32
    D = D_MODEL
    x = nrm(ks[0], (BATCH, SEQ, D), f32)
    mix_norm = 1.0 + 0.05 * nrm(ks[1], (DEPTH, D), f32)
    ffn_norm = 1.0 + 0.05 * nrm(ks[2], (DEPTH, D), f32)
    ev_w_in = nrm(ks[3], (N_EVEN, D, EVEN_IN), f32) * D ** -0.5
    hg_lb_logits = 0.5 * nrm(ks[4], (N_EVEN + 1, HG_WIDTH), f32)
    hg_out_norm = 1.0 + 0.05 * nrm(ks[5], (N_EVEN, HG_WIDTH), f32)
    at_q_norm = 1.0 + 0.05 * nrm(ks[6], (N_EVEN, AT_DIM), f32)
    at_k_norm = 1.0 + 0.05 * nrm(ks[7], (N_EVEN, AT_DIM), f32)
    ev_w_out = nrm(ks[8], (N_EVEN, MIX_WIDTH, D), f32) * (0.5 * MIX_WIDTH ** -0.5)
    od_w_in = nrm(ks[9], (N_ODD, D, ODD_IN), f32) * D ** -0.5
    od_conv_w = nrm(ks[10], (N_ODD, SSM_CONV, SSM_CONV_CH), f32) * SSM_CONV ** -0.5
    od_conv_b = 0.02 * nrm(ks[11], (N_ODD, SSM_CONV_CH), f32)
    dt0 = jnp.exp(jax.random.uniform(ks[12], (N_ODD, SSM_HEADS), f32) * (math.log(0.1) - math.log(0.001)) + math.log(0.001))
    od_dt_bias = dt0 + jnp.log(-jnp.expm1(-dt0))
    od_A_log = jnp.log(jax.random.uniform(ks[13], (N_ODD, SSM_HEADS), f32, 1.0, 16.0))
    od_D = 1.0 + 0.1 * nrm(ks[14], (N_ODD, SSM_HEADS), f32)
    od_out_norm = 1.0 + 0.05 * nrm(ks[15], (N_ODD, SSM_INNER), f32)
    od_w_out = nrm(ks[16], (N_ODD, SSM_INNER, D), f32) * (0.5 * SSM_INNER ** -0.5)
    moe_wg = nrm(ks[17], (DEPTH, D, MOE_GROUPS), f32) * D ** -0.5
    moe_bg = 0.01 * nrm(ks[18], (DEPTH, MOE_GROUPS), f32)
    moe_we = nrm(ks[19], (DEPTH, D, MOE_EXPERTS), f32) * D ** -0.5
    moe_be = 0.01 * nrm(ks[20], (DEPTH, MOE_EXPERTS), f32)
    moe_w1 = nrm(ks[21], (DEPTH, MOE_EXPERTS, D, MOE_FF), f32) * D ** -0.5
    moe_w3 = nrm(ks[22], (DEPTH, MOE_EXPERTS, D, MOE_FF), f32) * D ** -0.5
    moe_w2 = nrm(ks[23], (DEPTH, MOE_EXPERTS, MOE_FF, D), f32) * MOE_FF ** -0.5
    return {"x": x, "mix_norm": mix_norm, "ffn_norm": ffn_norm,
            "ev_w_in": ev_w_in, "hg_lb_logits": hg_lb_logits, "hg_out_norm": hg_out_norm,
            "at_q_norm": at_q_norm, "at_k_norm": at_k_norm, "ev_w_out": ev_w_out,
            "od_w_in": od_w_in, "od_conv_w": od_conv_w, "od_conv_b": od_conv_b,
            "od_dt_bias": od_dt_bias, "od_A_log": od_A_log, "od_D": od_D,
            "od_out_norm": od_out_norm, "od_w_out": od_w_out,
            "moe_wg": moe_wg, "moe_bg": moe_bg, "moe_we": moe_we, "moe_be": moe_be,
            "moe_w1": moe_w1, "moe_w3": moe_w3, "moe_w2": moe_w2}

def reference(x, mix_norm, ffn_norm, ev_w_in, hg_lb_logits, hg_out_norm, at_q_norm, at_k_norm,
              ev_w_out, od_w_in, od_conv_w, od_conv_b, od_dt_bias, od_A_log, od_D, od_out_norm,
              od_w_out, moe_wg, moe_bg, moe_we, moe_be, moe_w1, moe_w3, moe_w2):
    pos = jnp.arange(x.shape[1], dtype=jnp.int32)
    lbs = jnp.cumsum(jax.nn.softmax(hg_lb_logits.astype(jnp.float32), axis=0), axis=0)
    for layer in range(DEPTH):
        i = layer // 2
        h = rmsnorm(x, mix_norm[layer])
        if layer % 2 == 0:
            x = x + even_mixer(h, ev_w_in[i], lbs[i], hg_out_norm[i], at_q_norm[i], at_k_norm[i],
                               ev_w_out[i], pos)
        else:
            x = x + odd_mixer(h, od_w_in[i], od_conv_w[i], od_conv_b[i], od_dt_bias[i], od_A_log[i],
                              od_D[i], od_out_norm[i], od_w_out[i])
        h = rmsnorm(x, ffn_norm[layer])
        x = x + hier_moe(h, moe_wg[layer], moe_bg[layer], moe_we[layer], moe_be[layer],
                         moe_w1[layer], moe_w3[layer], moe_w2[layer])
    return x


_drawn_inputs = setup_inputs


def setup_inputs(seed=0):
    import zlib

    import numpy as np

    out = dict(_drawn_inputs(seed))
    spreads = {}
    factors = {}
    for name, (base, spread) in spreads.items():
        noise = np.random.default_rng([zlib.crc32(name.encode()), seed]).standard_normal(out[name].shape)
        drawn = base * np.exp(spread * noise) if base else spread * noise
        out[name] = __import__('jax').numpy.asarray(drawn.astype(out[name].dtype))
    for name, factor in factors.items():
        out[name] = (out[name] * factor).astype(out[name].dtype)
    return out
```

```python
import numpy as np

D, S, P = 1024, 256, 128
KT = D // P
NT = S // P
RING = 6
UNIT = 4096
EPS = 1e-6
NEG = -1.0e30
GONE = -3.0e38
MARK = 3.0e38
HG = 4
TOPK = 64
EXPERTS, GROUP, CAP, FF = 32, 4, 32, 512
NGROUPS = EXPERTS // GROUP
ROUNDS = S // CAP
MIX_UNITS = (9, 15)
STEP_UNITS = 3 * GROUP
SSM_H, SSM_G = 32, 4
ORDER = [(0, 0), (0, 1), (1, 0), (1, 1), (1 - 1, 2), (2, 0), (2, 1), (1, 2), (3, 0), (3, 1), (2, 2), (3, 2)]
C_ID, C_M3, C_STRICT, C_ADM, C_CS, C_IOTA, C_THR = 0, 128, 512, 640, 1152, 1280, 1312
C_END = 1320
V_MIX, V_FFN, V_HG, V_LB, V_OD, V_CB, V_CW = 0, 16, 32, 36, 44, 60, 84
E_Q, E_F, E_I, E_G, E_AQ, E_AK, E_AV, E_IQ, E_IK = 0, 512, 1024, 1536, 2048, 2560, 2688, 2816, 3072


BATCHES = [(0, list(range(8))), (1, [0, 1, 4, 5]), (1, [2, 3, 6, 7])]
PE_ORDER = [("level", 0), ("unit", 5), ("level", 1), ("level", 2), ("unit", 6), ("level", 3), ("level", 4), ("attend", 0),
            ("level", 5), ("attend", 1), ("level", 6), ("attend", 2), ("level", 7), ("level", 8)]
DVE_ORDER = [("level", 0), ("keys", 0), ("level", 1), ("level", 2), ("keys", 1), ("level", 3), ("level", 4), ("attend", 0),
             ("level", 5), ("attend", 1), ("level", 6), ("attend", 2), ("level", 7), ("level", 8)]
ACT_ORDER = [("unit", 5), ("level", 1), ("level", 2), ("unit", 6), ("level", 3), ("level", 4), ("attend", 0),
             ("level", 5), ("level", 6), ("attend", 1), ("level", 7), ("attend", 2), ("level", 8)]
PAIRED = [("unit", 3), ("unit", 4)] + [x for x in PE_ORDER if x[0] != "attend"]
PAIR = {x: ((2, 3), (0, 1))[n % 2] for n, x in enumerate(PAIRED)}


def finished(expert, part):
    return ORDER.index((expert, part)) + 1


def slot_of(layer, unit):
    return (unit + 3 * layer) % RING


def build(nc, A, out):
    import concourse.bass as bass
    from concourse import mybir
    from contextlib import ExitStack

    f32, i32 = mybir.dt.float32, mybir.dt.int32
    ALU, ACT, AX = mybir.AluOpType, mybir.ActivationFunctionType, mybir.AxisListType
    ctx = ExitStack()
    with ctx:
        def sb(name, shape, dt=f32, c=ctx):
            return c.enter_context(nc.sbuf_tensor(name, shape, dt))

        def sem(name):
            return ctx.enter_context(nc.semaphore(name))

        class Chain:

            def __init__(self, eng, s, base=0):
                self.eng, self.s, self.base, self.n = eng, s, base, 0

            def put(self, ins):
                self.n += 1
                ins.then_inc(self.s, 1)

            def wait(self):
                self.eng.wait_ge(self.s, self.base + self.n)

            def link(self, ins):
                self.put(ins)
                self.wait()

        ring = sb("ring", [P, RING, UNIT])
        con = sb("con", [P, C_END])
        lvl = sb("lvl", [P, 8, P], i32)
        ones = sb("ones", [P, 256])
        zeros = sb("zeros", [P, P])
        x = sb("x", [P, NT, D])
        xn = sb("xn", [P, NT, D])
        hT = sb("hT", [P, KT, S])
        vrow = sb("vrow", [96, 256])
        vT = sb("vT", [P, 184])
        wr = sb("wr", [P, 2, KT, 36])
        br = sb("br", [P, 2, 36])
        st = sb("st", [P, 64])
        rounds = sb("rounds", [P, 4], i32)
        ident = con[:, C_ID:C_ID + P]
        mask3 = con[:, C_M3:C_M3 + 384]
        strict = con[:, C_STRICT:C_STRICT + P]
        adm = con[:, C_ADM:C_ADM + 512].rearrange("p (a s) -> p a s", a=2)
        cs = con[:, C_CS:C_CS + 128].rearrange("p (a s) -> p a s", a=2)
        iota = con[:, C_IOTA:C_IOTA + 32]
        thr = con[:, C_THR:C_THR + 8]
        bank = [ctx.enter_context(nc.psum_tensor(f"bank{i}", [P, 512], f32)) for i in range(8)]

        def at(off, n, mem):
            return mem[:, off:off + n]

        with ExitStack() as c:
            rb = sb("rb", [P, NT, 16, 64], c=c)
            ro = sb("ro", [P, NT, 16, 64], c=c)
            rt = sb("rt", [P, 4, 512], c=c)
            tt_ = sb("tt_", [P, 8, S], c=c)
            av = sb("av", [P, NT, P], c=c)
            iw = sb("iw", [P, NT, 4], c=c)
            sc = sb("sc", [P, NT, S], c=c)
            wk = sb("wk", [P, NT, S], c=c)
            mx8 = sb("mx8", [P, NT, 8], c=c)
            pr = sb("pr", [P, 1024], c=c)
            sm = sb("sm", [P, 3, 32], c=c)
            qT = sb("qT", [P, HG, S], c=c)
            kk = sb("kk", [P, HG, S], c=c)
            lb_ = sb("lb_", [P, HG, S], c=c)
            bb = sb("bb", [P, HG, S], c=c)
            vv = sb("vv", [P, NT, 512], c=c)
            gg = sb("gg", [P, NT, 512], c=c)
            aT = sb("aT", [P, NT, HG, P], c=c)
            aX = sb("aX", [P, HG, P], c=c)
            lbv = sb("lbv", [P, 40], c=c)
            qkn = sb("qkn", [P, 2, 64], c=c)
        xe = rb[:, :, :, :].rearrange("p a h d -> p (a h d)").rearrange("p (n h t) -> p n h t", n=2, h=HG)
        ee = ro[:, :, :, :].rearrange("p a h d -> p (a h d)").rearrange("p (n h t) -> p n h t", n=2, h=HG)
        pT = rt[:, 0:2, :].rearrange("p a n -> p (a n)")
        rl = rt[:, :, 0:256]
        with ExitStack() as c:
            zz = sb("zz", [P, NT, 2048], c=c)
            xs = sb("xs", [P, NT, 2048], c=c)
            xd = sb("xd", [P, NT, 2048], c=c)
            bT = sb("bT", [P, SSM_G, S], c=c)
            cT = sb("cT", [P, SSM_G, S], c=c)
            cv = sb("cv", [P, 3, 260], c=c)
            ca = sb("ca", [P, 3, S], c=c)
            lw = sb("lw", [P, 3, 384], c=c)
            dts = sb("dts", [32, 8], c=c)
            dnat = sb("dnat", [P, NT, 2, 32], c=c)
            dsk = sb("dsk", [P, 32], c=c)
            cumT = sb("cumT", [32, S], c=c)
            dtT = sb("dtT", [32, S], c=c)
        dtmp = zz[0:32, 0, :].rearrange("p (n t) -> p n t", n=8)
        xsT = xn[:, :, :].rearrange("p a d -> p (a d)").rearrange("p (n t) -> p n t", n=8)
        cbm = hT[:, :, :].rearrange("p k t -> p (k t)")[:, 0:1536].rearrange("p (g t) -> p g t", g=SSM_G)
        yT = xd[:, :, :].rearrange("p a d -> p (a d)").rearrange("p (k t) -> p k t", k=16)
        with ExitStack() as c:
            sel = sb("sel", [P, 8, CAP], c=c)
            pg = sb("pg", [P, NT, GROUP, 4, CAP], c=c)
            xT = sb("xT", [P, KT, P], c=c)
            pgT = sb("pgT", [P, GROUP, NT, P], c=c)
            sg = sb("sg", [P, 2, P], c=c)
            he = sb("he", [P, 2, P], c=c)
            heT = sb("heT", [P, 2, P], c=c)
            ys = sb("ys", [P, 2, D], c=c)
            rtab = sb("rtab", [P, ROUNDS * NGROUPS, 8], c=c)
            gtab = sb("gtab", [P, ROUNDS * NGROUPS, 8], c=c)
            lg = sb("lg", [P, NT, 36], c=c)
            gp = sb("gp", [P, NT, 16], c=c)
            gr = sb("gr", [P, NT, 16], c=c)
            ep = sb("ep", [P, NT, 40], c=c)
            er = sb("er", [P, NT, 40], c=c)
            m8 = sb("m8", [P, 4, NT, 8], c=c)
            arg = sb("arg", [P, NT, 36], c=c)
            g4 = sb("g4", [P, 4, NT, 4], c=c)
            s32 = sb("s32", [P, 4, NT, 32], c=c)
            rr = sb("rr", [P, 32], c=c)

        in_con, in_x, in_vec, ini = sem("in_con"), sem("in_x"), sem("in_vec"), sem("ini")
        in_small, in_rb, in_even, in_odd, vec_ps, vec_ok = sem("in_small"), sem("in_rb"), sem("in_even"), sem("in_odd"), sem("vec_ps"), sem("vec_ok")
        full = [[sem(f"full{l}_{s}") for s in range(RING)] for l in range(2)]
        mixed = [sem(f"mixed{l}") for l in range(2)]
        used = [sem(f"used{l}") for l in range(2)]
        var_ok, root_ok, xn_ok, hT_ps, hT_v, hT_a = (sem(n) for n in ("var_ok", "root_ok", "xn_ok", "hT_ps", "hT_v", "hT_a"))
        x_new = sem("x_new")
        dch, ach, pch = sem("dch"), sem("ach"), sem("pch")
        e_out = sem("e_out")
        rot_ok, rot_ps, rot_t = sem("rot_ok"), sem("rot_ps"), sem("rot_t")
        ix_ps, ix_rel, ix_ok, lb_in, lb_ex = sem("ix_ps"), sem("ix_rel"), sem("ix_ok"), sem("lb_in"), sem("lb_ex")
        qk_var, qk_root = sem("qk_var"), sem("qk_root")
        ql_ps, at_max, at_exp, at_tps, at_t, pv_ps, at_o = (sem(n) for n in
            ("ql_ps", "at_max", "at_exp", "at_tps", "at_t", "pv_ps", "at_o"))
        lb_ok, f_lin, f_log, k_ok, b_ok = sem("lb_ok"), sem("f_lin"), sem("f_log"), sem("k_ok"), sem("b_ok")
        ex_in, ex_out, lv_x, lv_ps, lv_ok = sem("ex_in"), sem("ex_out"), sem("lv_x"), sem("lv_ps"), sem("lv_ok")
        ho_ps, ho_var, ho_root, on_ok = sem("ho_ps"), sem("ho_var"), sem("ho_root"), sem("on_ok")
        mo_ps = [sem(f"mo_ps{l}") for l in range(2)]
        mo_t = [sem(f"mo_t{l}") for l in range(2)]
        mp_ok = [sem(f"mp_ok{l}") for l in range(2)]
        dt_b, dt_e, dt_l, dt_ok, dn_ps, dn_ok = (sem(n) for n in ("dt_b", "dt_e", "dt_l", "dt_ok", "dn_ps", "dn_ok"))
        raw_in, cv_ok, act_ok, xs_ps, xs_ok, z_ok = (sem(n) for n in ("raw_in", "cv_ok", "act_ok", "xs_ps", "xs_ok", "z_ok"))
        cb_ps, cb_ok, cu_ps, cu_ok, lx_ok, lm_ok, yy_ps, yy_ok = (sem(n) for n in
            ("cb_ps", "cb_ok", "cu_ps", "cu_ok", "lx_ok", "lm_ok", "yy_ps", "yy_ok"))
        o_var, o_root, yn_ok, al_in, al_ex = sem("o_var"), sem("o_root"), sem("yn_ok"), sem("al_in"), sem("al_ex")
        names = ("rt_ps", "rt_in", "rt_ex", "rt_sel", "rk_ps", "rt_ok", "s_ok", "pg_ok", "ga_ps", "xt_ok",
                 "pt_ps", "pt_ok", "si_ok", "he_ok", "ht_ps", "ht_ok", "yv_ok", "ya_ok", "scat", "acc", "mdc")
        M = [{n: sem(f"{n}{l}") for n in names} for l in range(2)]
        stored = sem("stored")

        w1v = A["moe_w1"].rearrange("l e (k p) f -> l e p k f", p=P)
        w3v = A["moe_w3"].rearrange("l e (k p) f -> l e p k f", p=P)
        w2v = A["moe_w2"].rearrange("l e (k p) n -> l e p k n", p=P)
        evin = A["ev_w_in"][0].rearrange("(k p) n -> p k n", p=P)
        evout = A["ev_w_out"][0].rearrange("(k p) n -> p k n", p=P)
        odin = A["od_w_in"][0].rearrange("(k p) n -> p k n", p=P)
        odout = A["od_w_out"][0].rearrange("(k p) n -> p k n", p=P)
        EVEN = [(E_AK, 512), (E_IK, 68), (E_AQ, 512), (E_F, 512), (E_Q, 512), (E_I, 512), (E_G, 512)]
        ODD = [(5120, 32), (4096, 512), (4608, 512)] + [(2048 + 512 * u, 512) for u in range(4)] + \
              [(512 * u, 512) for u in range(4)]

        def wslot(layer, unit, n):
            return ring[:, slot_of(layer, unit), 0:(UNIT // 512 if n <= 512 else 4) * n].rearrange("p (k n) -> p k n", n=n)

        def full_at(layer, unit):
            return 32 * (unit // RING + 1)

        block = ctx.enter_context(nc.Block())

        @block.sync
        def _(sp):
            def load(layer, unit, halves):
                for dst, src in halves:
                    sp.dma_start(dst, src).then_inc(full[layer][slot_of(layer, unit)], 16)

            def in_unit(layer, unit, w, c0, n):
                d = wslot(layer, unit, n)
                load(layer, unit, [(d[:, 4 * h:4 * h + 4, :], w[:, 4 * h:4 * h + 4, c0:c0 + n]) for h in range(2)])

            def out_unit(layer, unit, w, k0):
                d = wslot(layer, unit, 1024)
                load(layer, unit, [(d[:, 2 * h:2 * h + 2, :], w[:, k0 + 2 * h:k0 + 2 * h + 2, :]) for h in range(2)])

            def moe_unit(layer, j, e):
                unit = MIX_UNITS[layer] + j
                d, part = ring[:, slot_of(layer, unit), :], j % 3
                if part < 2:
                    d = d.rearrange("p (k w f) -> p k w f", k=4, w=2)
                    pairs = [(d[:, :, w, :], v[layer, bass.ds(e, 1), :, 4 * part:4 * part + 4, :]
                              .rearrange("e p k f -> (e p) k f")) for w, v in enumerate((w1v, w3v))]
                else:
                    d = d.rearrange("p (k n) -> p k n", k=4)
                    pairs = [(d[:, 2 * h:2 * h + 2, :], w2v[layer, bass.ds(e, 1), :, 2 * h:2 * h + 2, :]
                              .rearrange("e p k n -> (e p) k n")) for h in range(2)]
                load(layer, unit, pairs)

            for layer in range(2):
                for v in range(MIX_UNITS[layer]):
                    if v >= RING:
                        sp.wait_ge(mixed[layer], v - RING + 1)
                    elif layer == 1:
                        j = v + RING
                        sp.wait_ge(used[0], last_step * STEP_UNITS + finished(j // 3, j % 3))
                    if layer == 0:
                        if v < len(EVEN):
                            in_unit(0, v, evin, *EVEN[v])
                        else:
                            out_unit(0, v, evout, 4 * (v - len(EVEN)))
                    else:
                        if v < len(ODD):
                            in_unit(1, v, odin, *ODD[v])
                        else:
                            out_unit(1, v, odout, 4 * (v - len(ODD)))
                for j in range(STEP_UNITS):
                    if j < RING:
                        sp.wait_ge(mixed[layer], MIX_UNITS[layer] + j - RING + 1)
                    else:
                        sp.wait_ge(used[layer], finished((j - RING) // 3, (j - RING) % 3))
                    moe_unit(layer, j, j // 3)
                sp.wait_ge(M[layer]["rt_ok"], 1)
                last_step = sp.value_load(rounds[0:1, 2 + layer:3 + layer], min_val=NGROUPS - 1, max_val=ROUNDS * NGROUPS - 1)
                with sp.Fori(0, last_step) as i:
                    for j in range(STEP_UNITS):
                        q = (j + RING) % STEP_UNITS
                        sp.wait_ge(used[layer], (i + (0 if j < RING else 1)) * STEP_UNITS + finished(q // 3, q % 3))
                        moe_unit(layer, j, ((i + 1) % NGROUPS) * GROUP + j // 3)
            sp.wait_ge(x_new, 16)
            sp.dma_start(out[0].rearrange("(a p) d -> p a d", p=P), x[:, :, :]).then_inc(stored, 16)
            sp.wait_ge(stored, 16)

        @block.tensor
        def _(pe):
            mm, tr = nc.tensor.matmul, nc.tensor.transpose

            def loaded(layer, unit, extra=0):
                pe.wait_ge(full[layer][slot_of(layer, unit)], full_at(layer, unit) + extra)

            def norm_transposes(n):
                for b in range(4):
                    for k in (2 * b, 2 * b + 1):
                        for t in range(NT):
                            if b == 0 and k == 0:
                                pe.wait_ge(xn_ok, 2 * n + t + 1)
                            c0 = 256 * (k % 2) + P * t
                            last = tr(bank[b][:, c0:c0 + P], xn[:, t, P * k:P * k + P], ident)
                    last.then_inc(hT_ps, 1)

            def hT_ready(n):
                pe.wait_ge(hT_v, 4 * n + 4)
                pe.wait_ge(hT_a, 4 * n + 4)

            def rows_product(layer, unit, n, banks):
                w = wslot(layer, unit, n)
                for t in range(NT):
                    for k in range(KT):
                        last = mm(bank[banks[t]][:, 0:n], hT[:, k, P * t:P * t + P], w[:, k, :], start=(k == 0), stop=(k == KT - 1))
                last.then_inc(mixed[layer], 1)

            def cols_product(layer, unit, banks):
                w = wslot(layer, unit, 512)
                for c in range(4):
                    for k in range(KT):
                        last = mm(bank[banks[c // 2]][:, 256 * (c % 2):256 * (c % 2) + 256], w[:, k, P * c:P * c + P],
                                  hT[:, k, :], start=(k == 0), stop=(k == KT - 1))
                last.then_inc(mixed[layer], 1)

            def pair_free(kind, n):
                k, m = PAIRED[PAIRED.index((kind, n)) - 2]
                if k == "unit":
                    pe.wait_ge(e_out, m + 1)
                else:
                    pe.wait_ge(lv_ok, m + 1)

            pe.wait_ge(in_con, 32)
            pe.wait_ge(in_vec, 16 * 7)
            tr(bank[7][:, 0:84], vrow[0:84, 0:P], ident[0:84, 0:84])
            tr(bank[7][:, 84:180], vrow[0:96, P:2 * P], ident[0:96, 0:96]).then_inc(vec_ps, 1)

            norm_transposes(0)
            hT_ready(0)
            for u in range(4):
                loaded(0, u)
                if u >= 2:
                    pe.wait_ge(e_out, u - 1)
                if u == 3:
                    cols_product(0, u, (2, 3))
                else:
                    rows_product(0, u, EVEN[u][1], ((0, 1), (2, 3))[u % 2])
            pe.wait_ge(rot_ok, 2)
            pe.wait_ge(vec_ok, 1)
            for s_ in range(8):
                for t in range(NT):
                    src = ro[:, t, 2 * s_:2 * s_ + 2, :].rearrange("p h d -> p (h d)")
                    last = tr(bank[4 + s_ // 2][:, 256 * (s_ % 2) + P * t:256 * (s_ % 2) + P * t + P], src, ident)
                if s_ % 2:
                    last.then_inc(rot_ps, 1)
            loaded(0, 4)
            pe.wait_ge(e_out, 3)
            cols_product(0, 4, PAIR["unit", 4])
            pe.wait_ge(rot_t, 4)
            for t in range(NT):
                n = P * (t + 1)
                for h in range(4):
                    r0 = 64 * (h % 2)
                    last = mm(bank[4 + 2 * t + h % 2][:, n * (h // 2):n * (h // 2) + n], tt_[r0:r0 + 64, 5 + h // 2, P * t:P * t + P],
                              tt_[r0:r0 + 64, 7, 0:n], start=True, stop=True)
                last.then_inc(ix_ps, 1)

            def unit(u):
                loaded(0, u)
                pair_free("unit", u)
                rows_product(0, u, 512, PAIR["unit", u])

            def attend(b):
                t, heads = BATCHES[b]
                n = P * (t + 1)
                pe.wait_ge(ix_rel, 2)
                if b:
                    pe.wait_ge(at_o, b)
                for m, h in enumerate(heads):
                    r0, o = 64 * (h // 4), m % (len(heads) // 2)
                    last = mm(bank[4 + h // 4][:, n * o:n * o + n], tt_[r0:r0 + 64, h % 4, P * t:P * t + P],
                              tt_[r0:r0 + 64, 4, 0:n], start=True, stop=True)
                last.then_inc(ql_ps, 1)
                pe.wait_ge(at_exp, b + 1)
                for j in range(8):
                    last = tr(bank[6 + j // 4][:, P * (j % 4):P * (j % 4) + P], pr[:, P * j:P * j + P], ident)
                    if j % 4 == 3:
                        last.then_inc(at_tps, 1)
                pe.wait_ge(at_t, 2 * (b + 1))
                for m, h in enumerate(heads):
                    for s_ in range(t + 1):
                        j = m * (t + 1) + s_
                        last = mm(bank[4][:, 64 * m:64 * m + 64], pT[:, P * j:P * j + P], av[:, s_, 64 * (h // 4):64 * (h // 4) + 64],
                                  start=(s_ == 0), stop=(s_ == t))
                last.then_inc(pv_ps, 1)

            def level(v):
                if v == 0:
                    pe.wait_ge(k_ok, 1)
                    pe.wait_ge(e_out, 5)
                else:
                    pe.wait_ge(lv_x, v)
                pair_free("level", v)
                for t in range(NT if v < 8 else 1):
                    for h in range(HG):
                        o = bank[PAIR["level", v][t]][:, P * h:P * h + P]
                        if v == 0:
                            last = mm(o, kk[:, h, P * t:P * t + P], qT[:, h, P * t:P * t + P], start=True, stop=True)
                        else:
                            e, tq = xe[:, v % 2, h, :], t if v < 8 else 1
                            last = mm(o, e[:, P * t:P * t + P], e[:, P * tq:P * tq + P], start=True, stop=True)
                last.then_inc(lv_ps, 1)

            for kind, n in PE_ORDER:
                {"level": level, "unit": unit, "attend": attend}[kind](n)
            pe.wait_ge(e_out, 7)
            pe.wait_ge(lv_ok, 9)
            for t in range(NT):
                for h in range(HG):
                    for s_ in range(t + 1):
                        w = aX[:, h, :] if s_ < t else aT[:, t, h, :]
                        last = mm(bank[2 + t][:, P * h:P * h + P], w, vv[:, s_, P * h:P * h + P], start=(s_ == 0), stop=(s_ == t))
                last.then_inc(ho_ps, 1)

            def out_transposes(layer, src, kts):
                for b in range(kts // 2):
                    if b >= 4:
                        pe.wait_ge(mo_t[layer], b - 3)
                    for k in (2 * b, 2 * b + 1):
                        for t in range(NT):
                            c0 = 256 * (k % 2) + P * t
                            last = tr(bank[4 + b % 4][:, c0:c0 + P], src[:, t, P * k:P * k + P], ident)
                    last.then_inc(mo_ps[layer], 1)

            def out_product(layer, unit0, kts, src):
                for u in range(kts // 4):
                    loaded(layer, unit0 + u)
                    pe.wait_ge(mo_t[layer], 2 * u + 2)
                    w = wslot(layer, unit0 + u, 1024)
                    for k in range(4):
                        for t in range(NT):
                            for h in range(2):
                                last = mm(bank[2 * t + h][:, :], src[:, 4 * u + k, P * t:P * t + P], w[:, k, 512 * h:512 * h + 512],
                                          start=(u == 0 and k == 0), stop=(u == kts // 4 - 1 and k == 3))
                    last.then_inc(mixed[layer], 1)

            pe.wait_ge(on_ok, 1)
            out_transposes(0, xn, 8)
            out_product(0, len(EVEN), 8, hT)

            def moe(layer, n):
                m = M[layer]
                norm_transposes(n)
                hT_ready(n)
                pe.wait_ge(in_small, 16 * 4)
                for t in range(NT):
                    for k in range(KT):
                        last = mm(bank[4][:, 36 * t:36 * t + 36], hT[:, k, P * t:P * t + P], wr[:, layer, k, :], start=(k == 0), stop=(k == KT - 1))
                last.then_inc(m["rt_ps"], 1)
                for a in range(4):
                    mm(bank[a][:, :], zeros[:, :], xn[:, 0, 0:512], start=True, stop=False)
                pe.wait_ge(m["rt_sel"], 1)
                for t in range(NT):
                    for s_ in range(t + 1):
                        mm(bank[5][:, 32 * t:32 * t + 32], strict if s_ == t else ones[:, 0:P], s32[:, 0, s_, :], start=(s_ == 0), stop=(s_ == t))
                for s_ in range(NT):
                    last = mm(bank[5][:, 64:96], ones[:, 0:P], s32[:, 0, s_, :], start=(s_ == 0), stop=(s_ == NT - 1))
                last.then_inc(m["rk_ps"], 1)
                pe.wait_ge(m["rt_ok"], 1)
                nr = pe.value_load(rounds[0:1, layer:layer + 1], min_val=1, max_val=ROUNDS)
                base = MIX_UNITS[layer]
                with pe.Fori(0, nr * NGROUPS) as i:
                    pe.wait_ge(m["s_ok"], i + 1)
                    for k in range(KT):
                        for t in range(NT):
                            last = mm(bank[6 + k // 4][:, P * (k % 4):P * (k % 4) + P], xn[:, t, P * k:P * k + P],
                                      sel[:, 4 * t:4 * t + 4, :].rearrange("p e c -> p (e c)"), start=(t == 0), stop=(t == NT - 1))
                    last.then_inc(m["ga_ps"], 1)
                    pe.wait_ge(m["pg_ok"], i + 1)
                    for e in range(GROUP):
                        for t in range(NT):
                            c0 = 256 * (e % 2) + P * t
                            last = tr(bank[4 + e // 2][:, c0:c0 + P], pg[:, t, e, :, :].rearrange("p j c -> p (j c)"), ident)
                    last.then_inc(m["pt_ps"], 1)

                    def up(e):
                        for part in range(2):
                            u = base + 3 * e + part
                            loaded(layer, u, i * 64)
                            w = ring[:, slot_of(layer, u), :].rearrange("p (k w f) -> p k w f", k=4, w=2)
                            for k in range(4):
                                for j in range(4):
                                    last = mm(bank[4 + e % 2][32 * j:32 * j + 32, 0:256], xT[:, 4 * part + k, CAP * e:CAP * e + CAP],
                                              w[:, k, :, P * j:P * j + P], start=(part == 0 and k == 0), stop=(part == 1 and k == 3))
                            last.then_inc(used[layer], 1)

                    def turn(e):
                        pe.wait_ge(m["he_ok"], i * 4 + e + 1)
                        if e:
                            pe.wait_ge(m["yv_ok"], i * 4 + e)
                        tr(bank[6][:, 0:P], he[:, e % 2, :], ident).then_inc(m["ht_ps"], 1)

                    def down(e):
                        u = base + 3 * e + 2
                        loaded(layer, u, i * 64)
                        pe.wait_ge(m["ht_ok"], i * 4 + e + 1)
                        if e:
                            pe.wait_ge(m["ya_ok"], i * 4 + e)
                        w = ring[:, slot_of(layer, u), :].rearrange("p (k n) -> p k n", k=4)
                        for h in range(2):
                            for j in range(4):
                                last = mm(bank[6 + h][32 * j:32 * j + 32, :], heT[:, e % 2, CAP * j:CAP * j + CAP],
                                          w[:, j, 512 * h:512 * h + 512], start=True, stop=True)
                        last.then_inc(used[layer], 1)

                    def scatter(e):
                        pe.wait_ge(m["yv_ok"], i * 4 + e + 1)
                        pe.wait_ge(m["ya_ok"], i * 4 + e + 1)
                        for t in range(NT):
                            for h in range(2):
                                last = mm(bank[2 * t + h][:, :], pgT[:, e, t, :], ys[:, e % 2, 512 * h:512 * h + 512], start=False, stop=False)
                        last.then_inc(m["scat"], 1)

                    pe.wait_ge(m["xt_ok"], i * 2 + 2)
                    pe.wait_ge(m["pt_ok"], i * 2 + 2)
                    up(0); up(1); turn(0); down(0)
                    up(2); turn(1); down(1); scatter(0)
                    up(3); turn(2); down(2); scatter(1)
                    turn(3); down(3); scatter(2); scatter(3)
                for a in range(4):
                    last = mm(bank[a][:, :], zeros[:, :], xn[:, 0, 0:512], start=False, stop=True)
                last.then_inc(m["acc"], 1)

            pe.wait_ge(x_new, 4)
            moe(0, 1)

            pe.wait_ge(x_new, 8)
            norm_transposes(2)
            hT_ready(2)
            loaded(1, 0)
            w = wslot(1, 0, 32)
            for k in range(KT):
                last = mm(bank[4][0:32, 0:S], w[:, k, :], hT[:, k, :], start=(k == 0), stop=(k == KT - 1))
            last.then_inc(mixed[1], 1)

            def dt_rows():
                pe.wait_ge(dt_ok, 1)
                for t in range(NT):
                    mm(bank[5][:, 64 * t:64 * t + 32], dtT[:, P * t:P * t + P], ident[0:32, 0:32], start=True, stop=True)
                    last = mm(bank[5][:, 64 * t + 32:64 * t + 64], cumT[:, P * t:P * t + P], ident[0:32, 0:32], start=True, stop=True)
                last.then_inc(dn_ps, 1)

            def xs_rows(u):
                pe.wait_ge(act_ok, 8 + 4 * u + 4)
                pb = (4, 5) if u % 2 == 0 else (6, 7)
                if u >= 2:
                    pe.wait_ge(xs_ok, 2 * (u - 1))
                for t in range(NT):
                    for c in range(4):
                        last = tr(bank[pb[t]][:, P * c:P * c + P], xsT[:, (4 * u + c) % 8, P * t:P * t + P], ident)
                last.then_inc(xs_ps, 1)

            for u in range(1, 7):
                loaded(1, u)
                if u >= 3:
                    pe.wait_ge(raw_in, 4 * (u - 2))
                cols_product(1, u, ((2, 3), (0, 1))[u % 2])
                if u == 1:
                    dt_rows()
                if u == 3:
                    pe.wait_ge(dn_ok, 1)
                if u >= 4:
                    xs_rows(u - 4)
            for u in range(7, 11):
                loaded(1, u)
                pe.wait_ge(raw_in, 4 * min(u - 2, 6))
                if u >= 9:
                    pe.wait_ge(z_ok, 2 * (u - 8))
                rows_product(1, u, 512, ((2, 3), (0, 1))[u % 2])
                if u == 7:
                    xs_rows(3)
            pe.wait_ge(xs_ok, 8)
            for g in range(SSM_G):
                mm(bank[4 + g][:, 0:S], bT[:, g, 0:P], cT[:, g, :], start=True, stop=True)
                mm(bank[4 + g][:, S:S + P], bT[:, g, P:S], cT[:, g, P:S], start=True, stop=True).then_inc(cb_ps, 1)
            pe.wait_ge(z_ok, 8)

            def cum_rows(h):
                if h >= 4:
                    pe.wait_ge(cu_ok, h - 3)
                else:
                    pe.wait_ge(cb_ok, 4)
                mm(bank[4 + h % 4][:, 0:S], ident[0:32, h:h + 1].to_broadcast([32, P]), cumT[:, :], start=True, stop=True).then_inc(cu_ps, 1)

            def y_head(h):
                g, o = h // 8, 64 * (h % 8)
                pe.wait_ge(lm_ok, h + 1)
                if h % 8 == 0 and g >= 2:
                    pe.wait_ge(yy_ok, 2 * (g - 1))
                b = 2 * (g % 2)
                l_ = lw[:, h % 3, :]
                mm(bank[b][:, o:o + 64], l_[:, 0:P], xd[:, 0, 64 * h:64 * h + 64], start=True, stop=True)
                mm(bank[b + 1][:, o:o + 64], l_[:, P:2 * P], xd[:, 0, 64 * h:64 * h + 64], start=True, stop=False)
                mm(bank[b + 1][:, o:o + 64], l_[:, 2 * P:3 * P], xd[:, 1, 64 * h:64 * h + 64], start=False, stop=True).then_inc(yy_ps, 1)

            for h in range(3):
                cum_rows(h)
            for h in range(SSM_H):
                if h + 3 < SSM_H:
                    cum_rows(h + 3)
                y_head(h)
            pe.wait_ge(yn_ok, 1)
            out_transposes(1, xs, 16)
            out_product(1, len(ODD), 16, yT)
            pe.wait_ge(x_new, 12)
            moe(1, 3)

        @block.scalar
        def _(act):
            fn = nc.scalar.activation
            ch = Chain(act, ach)
            act.dma_start(x[:, :, :], A["x"][0].rearrange("(a p) d -> p a d", p=P)).then_inc(in_x, 16)
            act.dma_start(con[:, :], A["con"]).then_inc(in_con, 16)
            act.dma_start(lvl[:, :, :], A["lvl"]).then_inc(in_con, 16)
            rows = lambda a: a.rearrange("(r c) -> r c", c=P)
            act.dma_start(vrow[0:16, 0:P], A["mix_norm"].rearrange("l (r c) -> (l r) c", c=P)).then_inc(in_vec, 16)
            act.dma_start(vrow[16:32, 0:P], A["ffn_norm"].rearrange("l (r c) -> (l r) c", c=P)).then_inc(in_vec, 16)
            act.dma_start(vrow[32:36, 0:P], rows(A["hg_out_norm"][0])).then_inc(in_vec, 16)
            act.dma_start(vrow[36:44, 0:P], A["hg_lb_logits"].rearrange("l (r c) -> (l r) c", c=P)).then_inc(in_vec, 16)
            act.dma_start(vrow[44:60, 0:P], rows(A["od_out_norm"][0])).then_inc(in_vec, 16)
            act.dma_start(vrow[0:96, P:2 * P], A["od_conv_w"][0].rearrange("j (r c) -> (j r) c", c=P)).then_inc(in_vec, 16)
            act.dma_start(vrow[60:84, 0:P], rows(A["od_conv_b"][0])).then_inc(in_vec, 16)
            act.dma_start(qkn[:, 0, :], A["at_q_norm"].to_broadcast([P, 64])).then_inc(in_even, 16)
            act.dma_start(qkn[:, 1, :], A["at_k_norm"].to_broadcast([P, 64])).then_inc(in_even, 16)

            def norm_root(n):
                act.wait_ge(var_ok, n + 1)
                ch.link(fn(st[:, 4:6], st[:, 2:4], ACT.Ln))
                fn(st[:, 6:8], st[:, 4:6], ACT.Exp, scale=-0.5).then_inc(root_ok, 1)

            def norm_take(n, g0):
                for b in (1, 3):
                    act.wait_ge(hT_ps, 4 * n + b + 1)
                    for k in (2 * b, 2 * b + 1):
                        fn(hT[:, k, :], bank[b][:, 256 * (k % 2):256 * (k % 2) + 256], ACT.Copy, scale=vT[:, g0 + k:g0 + k + 1]).then_inc(hT_a, 1)

            norm_root(0)
            act.wait_ge(lb_in, 1)
            fn(lbv[:, 8:16], lbv[:, 0:8], ACT.Exp).then_inc(lb_ex, 1)
            act.wait_ge(vec_ok, 1)
            norm_take(0, V_MIX)
            act.wait_ge(mixed[0], 1)
            for t in range(NT):
                fn(rb[:, t, 8:10, :], bank[t][:, 0:128], ACT.Copy)
                fn(av[:, t, :], bank[t][:, 128:256], ACT.Copy)
                last = fn(rb[:, t, 10:14, :], bank[t][:, 256:512], ACT.Copy)
            last.then_inc(e_out, 1)
            act.wait_ge(mixed[0], 2)
            for t in range(NT):
                fn(rb[:, t, 14, :], bank[2 + t][:, 0:64], ACT.Copy)
                fn(rb[:, t, 15, :], bank[2 + t][:, 0:64], ACT.Copy)
                last = fn(iw[:, t, :], bank[2 + t][:, 64:68], ACT.Copy)
            last.then_inc(e_out, 1)
            act.wait_ge(mixed[0], 3)
            for t in range(NT):
                last = fn(rb[:, t, 0:8, :].rearrange("p (i v) d -> p v i d", v=2), bank[t][:, :].rearrange("p (v i d) -> p v i d", v=2, i=4), ACT.Copy)
            last.then_inc(e_out, 1)
            act.wait_ge(qk_var, 1)
            ch.link(fn(st[:, 36:56], st[:, 16:36], ACT.Ln))
            fn(st[:, 36:56], st[:, 36:56], ACT.Exp, scale=-0.5).then_inc(qk_root, 1)
            act.wait_ge(mixed[0], 4)
            for c in range(2):
                fn(lb_[:, 2 * c:2 * c + 2, :], bank[2 + c][:, :], ACT.Sigmoid)
                last = fn(kk[:, 2 * c:2 * c + 2, :], bank[2 + c][:, :], ACT.Sigmoid, scale=-1.0)
            last.then_inc(e_out, 1)
            for b in range(4):
                act.wait_ge(rot_ps, b + 1)
                fn(tt_[:, 2 * b:2 * b + 2, :], bank[4 + b][:, :], ACT.Copy).then_inc(rot_t, 1)
            act.wait_ge(mixed[0], 5)
            for c in range(2):
                last = fn(qT[:, 2 * c:2 * c + 2, :], bank[PAIR["unit", 4][c]][:, :], ACT.Copy)
            last.then_inc(e_out, 1)
            act.wait_ge(rot_ok, 2)
            for t in range(NT):
                act.wait_ge(ix_ps, t + 1)
                if t:
                    act.wait_ge(ix_ok, 1)
                n = P * (t + 1)
                for r in range(2):
                    last = fn(rl[:, r:4:2, 0:n], bank[4 + 2 * t + r][:, 0:2 * n].rearrange("p (h s) -> p h s", h=2), ACT.Relu)
                last.then_inc(ix_rel, 1)
            act.wait_ge(f_lin, 1)
            fn(lb_[:, :, :], lb_[:, :, :], ACT.Ln).then_inc(f_log, 1)

            def unit(u):
                act.wait_ge(mixed[0], u + 1)
                for t in range(NT):
                    last = fn((vv, gg)[u - 5][:, t, :], bank[PAIR["unit", u][t]][:, :], (ACT.Copy, ACT.Silu)[u - 5])
                last.then_inc(e_out, 1)

            def level(v):
                act.wait_ge(ex_in, v)
                fn(ee[:, v % 2, :, :], ee[:, v % 2, :, :], ACT.Exp).then_inc(ex_out, 1)

            def attend(b):
                t, heads = BATCHES[b]
                n = P * (t + 1)
                act.wait_ge(at_max, b + 1)
                for m in range(len(heads)):
                    last = fn(pr[:, n * m:n * m + n], pr[:, n * m:n * m + n], ACT.Exp, bias=sm[:, b, 8 + m:9 + m], accum_out=sm[:, b, 16 + m:17 + m])
                last.then_inc(at_exp, 1)
                for j in range(2):
                    act.wait_ge(at_tps, 2 * b + j + 1)
                    fn(pT[:, 512 * j:512 * j + 512], bank[6 + j][:, :], ACT.Copy).then_inc(at_t, 1)

            for kind, n in ACT_ORDER:
                {"level": level, "unit": unit, "attend": attend}[kind](n)
            act.wait_ge(ho_var, 1)
            ch.link(fn(st[:, 36:44], st[:, 16:24], ACT.Ln))
            fn(st[:, 36:44], st[:, 36:44], ACT.Exp, scale=-0.5).then_inc(ho_root, 1)

            def out_take(layer, kts, dst, gain):
                for b in range(kts // 2):
                    act.wait_ge(mo_ps[layer], b + 1)
                    for k in (2 * b, 2 * b + 1):
                        g = gain(k)
                        last = fn(dst[:, k, :], bank[4 + b % 4][:, 256 * (k % 2):256 * (k % 2) + 256], ACT.Copy,
                                  scale=1.0 if g is None else vT[:, g:g + 1])
                    last.then_inc(mo_t[layer], 1)

            out_take(0, 8, hT, lambda k: V_HG + k if k < 4 else None)

            def moe(layer, n):
                m = M[layer]
                norm_root(n)
                norm_take(n, V_FFN + 8 * layer)
                act.wait_ge(m["rt_in"], 2)
                fn(arg[:, :, :], arg[:, :, :], ACT.Exp).then_inc(m["rt_ex"], 1)
                act.wait_ge(m["rt_ok"], 1)
                nr = act.value_load(rounds[0:1, layer:layer + 1], min_val=1, max_val=ROUNDS)
                with act.Fori(0, nr * NGROUPS) as i:
                    act.wait_ge(m["pt_ps"], i + 1)
                    for b in range(2):
                        fn(pgT[:, 2 * b:2 * b + 2, :, :], bank[4 + b][:, :], ACT.Copy).then_inc(m["pt_ok"], 1)

                    def silu(e):
                        act.wait_ge(used[layer], i * STEP_UNITS + finished(e, 1))
                        fn(sg[:, e % 2, :], bank[4 + e % 2][:, 0:P], ACT.Silu).then_inc(m["si_ok"], 1)

                    def take(e):
                        act.wait_ge(used[layer], i * STEP_UNITS + finished(e, 2))
                        if e >= 2:
                            act.wait_ge(m["scat"], i * 4 + e - 1)
                        fn(ys[:, e % 2, 512:1024], bank[7][:, :], ACT.Copy).then_inc(m["ya_ok"], 1)

                    silu(0); silu(1); take(0); silu(2); take(1); silu(3); take(2); take(3)

            moe(0, 1)
            act.wait_ge(x_new, 5)
            act.dma_start(dts[:, 0:1], A["od_dt_bias"].rearrange("a h -> h a")).then_inc(in_odd, 16)
            act.dma_start(dts[:, 1:2], A["od_A_log"].rearrange("a h -> h a")).then_inc(in_odd, 16)
            act.dma_start(dsk[:, :], A["od_D"].to_broadcast([P, SSM_H])).then_inc(in_odd, 16)
            norm_root(2)
            norm_take(2, V_MIX + 8)
            act.wait_ge(in_odd, 48)
            fn(dts[:, 2:3], dts[:, 1:2], ACT.Exp).then_inc(al_ex, 1)
            act.wait_ge(dt_b, 1)
            fn(dtmp[:, 2, :], dtmp[:, 1, :], ACT.Exp).then_inc(dt_e, 1)
            act.wait_ge(dt_b, 2)
            fn(dtmp[:, 4, :], dtmp[:, 3, :], ACT.Ln).then_inc(dt_l, 1)

            def raw(c):
                u, q = 1 + c // 4, c % 4
                act.wait_ge(mixed[1], u + 1)
                if c >= 3:
                    act.wait_ge(cv_ok, c - 2)
                b = ((2, 3), (0, 1))[u % 2][q // 2]
                fn(cv[:, c % 3, 3:259], bank[b][:, 256 * (q % 2):256 * (q % 2) + 256], ACT.Copy).then_inc(raw_in, 1)

            def conv_silu(c):
                act.wait_ge(cv_ok, c + 1)
                if c >= 16:
                    act.wait_ge(xs_ps, (c - 8) // 4 - 1)
                dst = bT[:, c, :] if c < 4 else cT[:, c - 4, :] if c < 8 else xsT[:, c % 8, :]
                fn(dst, ca[:, c % 3, :], ACT.Silu).then_inc(act_ok, 1)

            for c in range(24):
                raw(c)
                if c:
                    conv_silu(c - 1)
            conv_silu(23)
            for u in range(4):
                act.wait_ge(mixed[1], 8 + u)
                for t in range(NT):
                    b = ((2, 3), (0, 1))[(u + 7) % 2][t]
                    fn(zz[:, t, 512 * u:512 * u + 512], bank[b][:, :], ACT.Silu).then_inc(z_ok, 1)
            for h in range(SSM_H):
                act.wait_ge(cu_ok, h + 1)
                fn(lw[:, h % 3, :], lw[:, h % 3, :], ACT.Exp).then_inc(lx_ok, 1)
            act.wait_ge(o_var, 1)
            ch.link(fn(st[:, 36:44], st[:, 16:24], ACT.Ln))
            fn(st[:, 36:44], st[:, 36:44], ACT.Exp, scale=-0.5).then_inc(o_root, 1)
            out_take(1, 16, yT, lambda k: V_OD + k)
            moe(1, 3)

        @block.gpsimd
        def _(pool):
            g = nc.gpsimd
            ch = Chain(pool, pch)
            for l in range(2):
                pool.dma_start(wr[:, l, :, 0:4], A["moe_wg"][l].rearrange("(k p) n -> p k n", p=P)).then_inc(in_small, 16)
                pool.dma_start(wr[:, l, :, 4:36], A["moe_we"][l].rearrange("(k p) n -> p k n", p=P)).then_inc(in_small, 16)
                pool.dma_start(br[:, l, 0:4], A["moe_bg"][l:l + 1, :].to_broadcast([P, 4])).then_inc(in_rb, 16)
                pool.dma_start(br[:, l, 4:36], A["moe_be"][l:l + 1, :].to_broadcast([P, 32])).then_inc(in_rb, 16)
            for v in range(1, 9):
                half = P >> (v - 1) if v == 8 else 64 >> (v - 1)
                if v == 8:
                    half = P
                if v == 1:
                    pool.wait_ge(b_ok, 1)
                    pool.wait_ge(rot_ps, 4)
                if v >= 3:
                    pool.wait_ge(lv_ps, v - 1)
                blk = lambda a: a.rearrange("p h (n w t) -> p (h n) w t", w=2, t=half)
                b_, e_, q_, k_, x_ = blk(bb[:, :, :]), blk(ee[:, v % 2, :, :]), blk(qT[:, :, :]), blk(kk[:, :, :]), blk(xe[:, v % 2, :, :])
                nb = b_.shape[1]
                ref = b_[:, :, 0, half - 1:half].to_broadcast([P, nb, half])
                g.tensor_tensor(e_[:, :, 0, :], ref, b_[:, :, 0, :], ALU.subtract)
                g.tensor_tensor(e_[:, :, 1, :], b_[:, :, 1, :], ref, ALU.subtract).then_inc(ex_in, 1)
                if v == 1:
                    pool.wait_ge(e_out, 5)
                    pool.wait_ge(k_ok, 1)
                pool.wait_ge(ex_out, v)
                g.tensor_tensor(x_[:, :, 0, :], k_[:, :, 0, :], e_[:, :, 0, :], ALU.mult)
                g.tensor_tensor(x_[:, :, 1, :], q_[:, :, 1, :], e_[:, :, 1, :], ALU.mult).then_inc(lv_x, 1)

        @block.vector
        def _(dve):
            v_ = nc.vector
            ch = Chain(dve, dch)
            tt, ts, stt = v_.tensor_tensor, v_.tensor_scalar, v_.scalar_tensor_tensor
            bc = lambda a, shape: a.to_broadcast(shape)

            def newton(y, y0, var, tmp):
                ch.link(tt(tmp, y0, y0, ALU.mult))
                ch.link(tt(tmp, tmp, var, ALU.mult))
                ch.link(ts(tmp, tmp, -0.5, 1.5, ALU.mult, ALU.add))
                ch.link(tt(y, y0, tmp, ALU.mult))

            def norm(n):
                for t in range(NT):
                    ch.put(v_.tensor_tensor_reduce(out=xn[:, t, :], in0=x[:, t, :], in1=x[:, t, :], scale=1.0, scalar=0.0,
                                                   op0=ALU.mult, op1=ALU.add, accum_out=st[:, t:t + 1]))
                ch.wait()
                ts(st[:, 2:4], st[:, 0:2], 1.0 / D, EPS, ALU.mult, ALU.add).then_inc(var_ok, 1)
                dve.wait_ge(root_ok, n + 1)
                newton(st[:, 8:10], st[:, 6:8], st[:, 2:4], st[:, 10:12])
                for t in range(NT):
                    ts(xn[:, t, :], x[:, t, :], st[:, 8 + t:9 + t], None, ALU.mult).then_inc(xn_ok, 1)

            def norm_take(n, g0):
                for b in (0, 2):
                    dve.wait_ge(hT_ps, 4 * n + b + 1)
                    for k in (2 * b, 2 * b + 1):
                        ts(hT[:, k, :], bank[b][:, 256 * (k % 2):256 * (k % 2) + 256], vT[:, g0 + k:g0 + k + 1], None, ALU.mult).then_inc(hT_v, 1)

            def residual(n):
                for t in range(NT):
                    for h in range(2):
                        tt(x[:, t, 512 * h:512 * h + 512], x[:, t, 512 * h:512 * h + 512], bank[2 * t + h][:, :], ALU.add).then_inc(x_new, 1)
                dve.wait_ge(x_new, 4 * n + 4)

            v_.memset(zeros[:, :], 0.0)
            v_.memset(ones[:, :], 1.0)
            ch.put(v_.memset(aT[:, :, :, :], 0.0))
            dve.wait_ge(in_x, 16)
            norm(0)
            dve.wait_ge(vec_ps, 1)
            v_.tensor_copy(vT[:, 0:180], bank[7][:, 0:180]).then_inc(vec_ok, 1)
            dve.wait_ge(vec_ok, 1)
            l0, l1 = vT[:, V_LB:V_LB + 4], vT[:, V_LB + 4:V_LB + 8]
            ch.link(tt(lbv[:, 16:20], l0, l1, ALU.max))
            ch.put(tt(lbv[:, 0:4], l0, lbv[:, 16:20], ALU.subtract))
            tt(lbv[:, 4:8], l1, lbv[:, 16:20], ALU.subtract).then_inc(lb_in, 1)
            norm_take(0, V_MIX)
            dve.wait_ge(lb_ex, 1)
            ch.link(tt(lbv[:, 20:24], lbv[:, 8:12], lbv[:, 12:16], ALU.add))
            ch.link(v_.reciprocal(lbv[:, 24:28], lbv[:, 20:24]))
            ch.link(tt(lbv[:, 28:32], lbv[:, 8:12], lbv[:, 24:28], ALU.mult))
            ch.link(ts(lbv[:, 32:36], lbv[:, 28:32], -1.0, 1.0, ALU.mult, ALU.add))

            dve.wait_ge(e_out, 3)
            dve.wait_ge(in_even, 32)
            sq = ro[:, :, 0:10, :]
            for t in range(NT):
                ch.put(tt(ro[:, t, 0:10, :], rb[:, t, 0:10, :], rb[:, t, 0:10, :], ALU.mult))
            ch.wait()
            ch.link(v_.tensor_reduce(st[:, 16:36].rearrange("p (a h) -> p a h", a=2), sq, AX.X, ALU.add))
            ts(st[:, 16:36], st[:, 16:36], 1.0 / 64, EPS, ALU.mult, ALU.add).then_inc(qk_var, 1)
            dve.wait_ge(qk_root, 1)
            dve.wait_ge(qk_var, 1)
            rs = rt[:, 0, 0:20]
            newton(rs, st[:, 36:56], st[:, 16:36], rt[:, 1, 0:20])
            for t in range(NT):
                h10 = rb[:, t, 0:10, :]
                ch.link(tt(h10, h10, bc(rs[:, 10 * t:10 * t + 10].unsqueeze(2), [P, 10, 64]), ALU.mult))
                ch.put(tt(rb[:, t, 0:8, :], rb[:, t, 0:8, :], bc(qkn[:, 0:1, :], [P, 8, 64]), ALU.mult))
                ch.link(tt(rb[:, t, 8:10, :], rb[:, t, 8:10, :], bc(qkn[:, 1:2, :], [P, 2, 64]), ALU.mult))
            for t in range(NT):
                a1, a2 = rb[:, t, :, 0:32], rb[:, t, :, 32:64]
                cos, sin = bc(cs[:, t:t + 1, 0:32], [P, 16, 32]), bc(cs[:, t:t + 1, 32:64], [P, 16, 32])
                r = lambda n: rt[:, n, :].rearrange("p (h d) -> p h d", h=16)
                ch.put(tt(r(0), a1, cos, ALU.mult))
                ch.put(tt(r(1), a2, sin, ALU.mult))
                ch.put(tt(r(2), a2, cos, ALU.mult))
                ch.link(tt(r(3), a1, sin, ALU.mult))
                ch.put(tt(ro[:, t, :, 0:32], r(0), r(1), ALU.subtract))
                ch.wait()
                tt(ro[:, t, :, 32:64], r(2), r(3), ALU.add).then_inc(rot_ok, 1)
                dve.wait_ge(rot_ok, t + 1)
            dve.wait_ge(e_out, 4)
            for h in range(HG):
                last = ts(lb_[:, h, :], lb_[:, h, :], lbv[:, 32 + h:33 + h], lbv[:, 28 + h:29 + h], ALU.mult, ALU.add)
            last.then_inc(f_lin, 1)
            for h in range(HG):
                last = ts(kk[:, h, :], kk[:, h, :], lbv[:, 32 + h:33 + h], None, ALU.mult)
            last.then_inc(k_ok, 1)
            ch.put(ts(iw[:, :, :], iw[:, :, :], 0.125, None, ALU.mult))
            ch.wait()
            for t in range(NT):
                n = P * (t + 1)
                dve.wait_ge(ix_rel, t + 1)
                s_ = sc[:, t, 0:n]
                ch.link(ts(s_, rl[:, 0, 0:n], iw[:, t, 0:1], None, ALU.mult))
                for h in range(1, 4):
                    ch.link(stt(s_, rl[:, h, 0:n], iw[:, t, h:h + 1], s_, ALU.mult, ALU.add))
                tt(wk[:, t, 0:n], s_, adm[:, t, 0:n], ALU.add).then_inc(ix_ok, 1)
            dve.wait_ge(f_log, 1)
            for h in range(HG):
                last = v_.tensor_tensor_scan(bb[:, h, :], ones[:, :], lb_[:, h, :], 0.0, ALU.mult, ALU.add)
            last.then_inc(b_ok, 1)

            def top_keys(t):
                dve.wait_ge(ix_ok, t + 1)
                w = wk[:, t, 0:P * (t + 1)]
                for r in range(TOPK // 8):
                    ch.link(v_.max(mx8[:, t, :], w))
                    ch.link(v_.match_replace(w, mx8[:, t, :], w, GONE))
                ch.link(ts(sc[:, t, 0:P * (t + 1)], w, GONE, NEG, ALU.not_equal, ALU.mult))
            def take_level(v):
                pair = PAIR["level", v]
                dve.wait_ge(lv_ps, v + 1)
                if v == 8:
                    v_.tensor_copy(aX[:, :, :], bank[pair[0]][:, :]).then_inc(lv_ok, 1)
                    return
                for t in range(NT):
                    ins = v_.copy_predicated(aT[:, t, :, :], lvl[:, v:v + 1, :].to_broadcast([P, HG, P]),
                                             bank[pair[t]][:, :].rearrange("p (h t) -> p h t", h=HG))
                ins.then_inc(lv_ok, 1)
                dve.wait_ge(lv_ok, v + 1)

            def attend(b):
                t, heads = BATCHES[b]
                n, nh = P * (t + 1), len(heads)
                dve.wait_ge(ql_ps, b + 1)
                for m, h in enumerate(heads):
                    o = m % (nh // 2)
                    ch.put(v_.tensor_tensor_reduce(out=pr[:, n * m:n * m + n], in0=bank[4 + h // 4][:, n * o:n * o + n], in1=sc[:, t, 0:n],
                                                   scale=0.125, scalar=-3.0e38, op0=ALU.add, op1=ALU.max, accum_out=sm[:, b, m:m + 1]))
                ch.wait()
                ts(sm[:, b, 8:8 + nh], sm[:, b, 0:nh], -1.0, None, ALU.mult).then_inc(at_max, 1)
                dve.wait_ge(at_exp, b + 1)
                ch.link(v_.reciprocal(sm[:, b, 24:24 + nh], sm[:, b, 16:16 + nh]))
                dve.wait_ge(pv_ps, b + 1)
                dst = xn[:, t, 512:1024].rearrange("p (v h d) -> p v h d", v=2, h=4)[:, :, heads[0]:heads[0] + nh // 2, :]
                tt(dst, bank[4][:, 0:64 * nh].rearrange("p (v h d) -> p v h d", v=2, h=nh // 2),
                   bc(sm[:, b, 24:24 + nh].rearrange("p (v h) -> p v h", v=2).unsqueeze(3), [P, 2, nh // 2, 64]), ALU.mult).then_inc(at_o, 1)
            for kind, n in DVE_ORDER:
                {"level": take_level, "keys": top_keys, "attend": attend}[kind](n)
            ov = lb_[:, :, :].rearrange("p h t -> p (h t)").rearrange("p (a n) -> p a n", a=2)
            sqv = kk[:, :, :].rearrange("p h t -> p (h t)").rearrange("p (a n) -> p a n", a=2)
            for t in range(NT):
                dve.wait_ge(ho_ps, t + 1)
                ch.put(v_.tensor_copy(ov[:, t, :], bank[2 + t][:, :]))
            ch.wait()
            ch.link(tt(sqv, ov, ov, ALU.mult))
            ch.link(v_.tensor_reduce(st[:, 24:32], sqv.rearrange("p a (h d) -> p (a h) d", h=4), AX.X, ALU.add))
            ts(st[:, 16:24], st[:, 24:32], 1.0 / P, EPS, ALU.mult, ALU.add).then_inc(ho_var, 1)
            dve.wait_ge(e_out, 7)
            ch.link(tt(ov, ov, gg[:, :, :], ALU.mult))
            dve.wait_ge(ho_root, 1)
            newton(st[:, 44:52], st[:, 36:44], st[:, 16:24], st[:, 52:60])
            for t in range(NT):
                ins = tt(xn[:, t, 0:512].rearrange("p (h d) -> p h d", h=4), ov[:, t, :].rearrange("p (h d) -> p h d", h=4),
                         bc(st[:, 44 + 4 * t:48 + 4 * t].unsqueeze(2), [P, 4, P]), ALU.mult)
            ins.then_inc(on_ok, 1)
            dve.wait_ge(mixed[0], 9)
            residual(0)

            def moe(layer, n):
                m = M[layer]
                norm(n)
                for a in (gp[:, :, 0:8], gp[:, :, 12:16], ep[:, :, 0:8], m8[:, 1, :, :], m8[:, 3, :, :]):
                    ch.put(v_.memset(a, NEG))
                norm_take(n, V_FFN + 8 * layer)
                dve.wait_ge(m["rt_ps"], 1)
                dve.wait_ge(in_rb, 64)
                ch.wait()
                for t in range(NT):
                    ch.put(tt(lg[:, t, :], bank[4][:, 36 * t:36 * t + 36], br[:, layer, :], ALU.add))
                ch.wait()
                ch.link(v_.tensor_copy(gp[:, :, 8:12], lg[:, :, 0:4]))
                for t in range(NT):
                    ch.link(v_.max(m8[:, 0, t, :], gp[:, t, :]))
                    ch.link(v_.tensor_copy(m8[:, 1, t, 0:1], m8[:, 0, t, 0:1]))
                    ch.link(v_.match_replace(gr[:, t, :], m8[:, 1, t, :], gp[:, t, :], MARK))
                ch.link(ts(g4[:, 0, :, :], gr[:, :, 8:12], MARK, None, ALU.is_equal))
                ch.link(ts(g4[:, 1, :, :], g4[:, 0, :, :], 1.0, -NEG, ALU.subtract, ALU.mult))
                for t in range(NT):
                    el = lg[:, t, 4:36].rearrange("p (g e) -> p g e", g=4)
                    e_ = ep[:, t, 8:40].rearrange("p (g e) -> p g e", g=4)
                    ch.link(tt(e_, el, bc(g4[:, 0, t, :].unsqueeze(2), [P, 4, 8]), ALU.mult))
                    ch.link(tt(e_, e_, bc(g4[:, 1, t, :].unsqueeze(2), [P, 4, 8]), ALU.add))
                    ch.link(v_.max(m8[:, 2, t, :], ep[:, t, :]))
                    ch.link(v_.tensor_copy(m8[:, 3, t, 0:2], m8[:, 2, t, 0:2]))
                    ch.link(v_.match_replace(er[:, t, :], m8[:, 3, t, :], ep[:, t, :], MARK))
                    ch.put(ts(arg[:, t, 0:4], lg[:, t, 0:4], m8[:, 0, t, 0:1], None, ALU.subtract))
                    ts(arg[:, t, 4:36], ep[:, t, 8:40], m8[:, 2, t, 0:1], None, ALU.subtract).then_inc(m["rt_in"], 1)
                ts(s32[:, 0, :, :], er[:, :, 8:40], MARK, None, ALU.is_equal).then_inc(m["rt_sel"], 1)
                dve.wait_ge(m["rt_sel"], 1)
                dve.wait_ge(m["rt_ex"], 1)
                red = lambda o, a: ch.link(v_.tensor_reduce(o, a, AX.X, ALU.add))
                red(st[:, 16:18], arg[:, :, 0:4])
                red(st[:, 18:20], arg[:, :, 4:36])
                ch.link(v_.reciprocal(st[:, 20:24], st[:, 16:20]))
                for t in range(NT):
                    ch.put(stt(s32[:, 1, t, :], arg[:, t, 4:36], st[:, 22 + t:23 + t], s32[:, 0, t, :], ALU.mult, ALU.mult))
                ch.wait()
                red(st[:, 24:26], s32[:, 1, :, :])
                ch.link(v_.reciprocal(st[:, 26:28], st[:, 24:26]))
                ch.link(tt(st[:, 28:30], st[:, 26:28], st[:, 20:22], ALU.mult))
                for t in range(NT):
                    ch.put(ts(s32[:, 2, t, :], s32[:, 1, t, :], st[:, 28 + t:29 + t], None, ALU.mult))
                ch.wait()
                dve.wait_ge(m["rk_ps"], 1)
                rk = s32[:, 3, :, :]
                ch.link(stt(rk, bank[5][:, 0:64].rearrange("p (a e) -> p a e", a=2), 1.0, s32[:, 0, :, :], ALU.add, ALU.mult))
                ch.link(v_.tensor_reduce(rr[:, 0:1], bank[5][:, 64:96], AX.X, ALU.max))
                ch.link(ts(rr[:, 8:16], thr, rr[:, 0:1], None, ALU.is_lt))
                ch.link(v_.tensor_reduce(rr[:, 1:2], rr[:, 8:16], AX.X, ALU.add))
                ch.link(ts(rr[:, 2:3], rr[:, 1:2], float(NGROUPS), -1.0, ALU.mult, ALU.add))
                ch.put(v_.tensor_copy(rounds[:, layer:layer + 1], rr[:, 1:2]))
                ch.put(v_.tensor_copy(rounds[:, 2 + layer:3 + layer], rr[:, 2:3]))
                step = lambda tab, r: tab[:, NGROUPS * r:NGROUPS * (r + 1), :].rearrange("p g (a e) -> p a g e", a=2)
                by_group = lambda a: a.rearrange("p a (g e) -> p a g e", g=NGROUPS)
                for r in range(ROUNDS):
                    ch.put(ts(step(rtab, r), by_group(rk), -1.0 - CAP * r, None, ALU.add))
                    last = v_.tensor_copy(step(gtab, r), by_group(s32[:, 2, :, :]))
                last.then_inc(m["rt_ok"], 1)
                dve.wait_ge(m["rt_ok"], 1)
                ch.wait()
                nr = dve.value_load(rounds[0:1, layer:layer + 1], min_val=1, max_val=ROUNDS)
                with dve.Fori(0, nr * NGROUPS) as i:
                    tt(sel[:, :, :], bc(rtab[:, bass.ds(i, 1), :].rearrange("p a e -> p (a e)").unsqueeze(2), [P, 8, CAP]),
                       bc(iota.unsqueeze(1), [P, 8, CAP]), ALU.is_equal).then_inc(m["s_ok"], 1)
                    dve.wait_ge(m["s_ok"], i + 1)
                    for t in range(NT):
                        gt = gtab[:, bass.ds(i, 1), 4 * t:4 * t + 4].rearrange("p a e -> p (a e)").unsqueeze(2).unsqueeze(3)
                        ins = tt(pg[:, t, :, :, :], bc(sel[:, 4 * t:4 * t + 4, :].unsqueeze(2), [P, GROUP, 4, CAP]), bc(gt, [P, GROUP, 4, CAP]), ALU.mult)
                    ins.then_inc(m["pg_ok"], 1)
                    dve.wait_ge(m["ga_ps"], i + 1)
                    for b in range(2):
                        g0 = V_FFN + 8 * layer + 4 * b
                        tt(xT[:, 4 * b:4 * b + 4, :], bank[6 + b][:, :].rearrange("p (k c) -> p k c", k=4),
                           bc(vT[:, g0:g0 + 4].unsqueeze(2), [P, 4, P]), ALU.mult).then_inc(m["xt_ok"], 1)

                    def gate(e):
                        dve.wait_ge(m["si_ok"], i * 4 + e + 1)
                        tt(he[:, e % 2, :], sg[:, e % 2, :], bank[4 + e % 2][:, P:2 * P], ALU.mult).then_inc(m["he_ok"], 1)

                    def turned(e):
                        dve.wait_ge(m["ht_ps"], i * 4 + e + 1)
                        v_.tensor_copy(heT[:, e % 2, :], bank[6][:, 0:P]).then_inc(m["ht_ok"], 1)

                    def take(e):
                        dve.wait_ge(used[layer], i * STEP_UNITS + finished(e, 2))
                        if e >= 2:
                            dve.wait_ge(m["scat"], i * 4 + e - 1)
                        v_.tensor_copy(ys[:, e % 2, 0:512], bank[6][:, :]).then_inc(m["yv_ok"], 1)

                    gate(0); turned(0); gate(1); take(0)
                    turned(1); gate(2); take(1)
                    turned(2); gate(3); take(2)
                    turned(3); take(3)
                dve.wait_ge(m["acc"], 1)
                residual(n)

            moe(0, 1)

            norm(2)
            for s_ in range(3):
                ch.put(v_.memset(cv[:, s_, 0:3], 0.0))
            norm_take(2, V_MIX + 8)
            dve.wait_ge(in_odd, 48)
            dve.wait_ge(mixed[1], 1)
            ch.link(ts(dtmp[:, 0, :], bank[4][0:32, 0:S], dts[:, 0:1], None, ALU.add))
            ch.link(ts(dtmp[:, 5, :], dtmp[:, 0, :], -1.0, None, ALU.mult))
            ts(dtmp[:, 6, :], dtmp[:, 0, :], 0.0, None, ALU.max).then_inc(al_in, 1)
            tt(dtmp[:, 1, :], dtmp[:, 0, :], dtmp[:, 5, :], ALU.min).then_inc(dt_b, 1)
            dve.wait_ge(al_ex, 1)
            ch.link(ts(dts[:, 3:4], dts[:, 2:3], -1.0, None, ALU.mult))
            dve.wait_ge(dt_e, 1)
            ts(dtmp[:, 3, :], dtmp[:, 2, :], 1.0, None, ALU.add).then_inc(dt_b, 1)
            dve.wait_ge(dt_b, 2)
            ch.link(ts(dtmp[:, 5, :], dtmp[:, 3, :], 1.0, None, ALU.subtract))
            ch.link(tt(dtmp[:, 5, :], dtmp[:, 2, :], dtmp[:, 5, :], ALU.subtract))
            ch.link(v_.reciprocal(dtmp[:, 7, :], dtmp[:, 3, :]))
            ch.link(tt(dtmp[:, 5, :], dtmp[:, 5, :], dtmp[:, 7, :], ALU.mult))
            dve.wait_ge(al_in, 1)
            ch.link(tt(dtmp[:, 6, :], dtmp[:, 6, :], dtmp[:, 5, :], ALU.add))
            dve.wait_ge(dt_l, 1)
            ch.link(tt(dtT[:, :], dtmp[:, 6, :], dtmp[:, 4, :], ALU.add))
            ch.link(ts(dtmp[:, 7, :], dtT[:, :], dts[:, 3:4], None, ALU.mult))
            v_.tensor_tensor_scan(cumT[:, :], ones[0:32, :], dtmp[:, 7, :], 0.0, ALU.mult, ALU.add).then_inc(dt_ok, 1)

            def conv(c):
                dve.wait_ge(raw_in, c + 1)
                if c >= 3:
                    dve.wait_ge(act_ok, c - 2)
                src, dst = cv[:, c % 3, :], ca[:, c % 3, :]
                w = lambda j: vT[:, V_CW + 24 * j + ct(c):V_CW + 24 * j + ct(c) + 1]
                ch.link(ts(dst, src[:, 3:259], w(3), vT[:, V_CB + ct(c):V_CB + ct(c) + 1], ALU.mult, ALU.add))
                ch.link(stt(dst, src[:, 2:258], w(2), dst, ALU.mult, ALU.add))
                ch.link(stt(dst, src[:, 1:257], w(1), dst, ALU.mult, ALU.add))
                stt(dst, src[:, 0:256], w(0), dst, ALU.mult, ALU.add).then_inc(cv_ok, 1)

            def ct(c):
                return 16 + c if c < 8 else c - 8

            def xs_take(u):
                dve.wait_ge(xs_ps, u + 1)
                pb = (4, 5) if u % 2 == 0 else (6, 7)
                for t in range(NT):
                    src = bank[pb[t]][:, :].rearrange("p (h d) -> p h d", h=8)
                    ch.put(tt(xd[:, t, 512 * u:512 * u + 512].rearrange("p (h d) -> p h d", h=8), src,
                              bc(dnat[:, t, 0, 8 * u:8 * u + 8].unsqueeze(2), [P, 8, 64]), ALU.mult))
                    ch.wait()
                    tt(xs[:, t, 512 * u:512 * u + 512].rearrange("p (h d) -> p h d", h=8), src,
                       bc(dsk[:, 8 * u:8 * u + 8].unsqueeze(2), [P, 8, 64]), ALU.mult).then_inc(xs_ok, 1)

            for c in range(24):
                conv(c)
                if c == 3:
                    dve.wait_ge(dn_ps, 1)
                    v_.tensor_copy(dnat[:, :, :, :], bank[5][:, 0:128].rearrange("p (a w h) -> p a w h", a=2, w=2)).then_inc(dn_ok, 1)
                    dve.wait_ge(dn_ok, 1)
                if c in (15, 19, 23):
                    xs_take(c // 4 - 3)
            xs_take(3)
            dve.wait_ge(xs_ok, 8)
            for g in range(SSM_G):
                dve.wait_ge(cb_ps, g + 1)
                tt(cbm[:, g, :], bank[4 + g][:, 0:384], mask3, ALU.mult).then_inc(cb_ok, 1)
            dve.wait_ge(cb_ok, 4)

            def decay(h):
                dve.wait_ge(cu_ps, h + 1)
                if h >= 3:
                    dve.wait_ge(yy_ps, h - 2)
                l_, b = lw[:, h % 3, :], bank[4 + h % 4]
                ch.put(ts(l_[:, 0:S], b[:, 0:S], dnat[:, 0, 1, h:h + 1], 0.0, ALU.subtract, ALU.min))
                ch.wait()
                ts(l_[:, S:S + P], b[:, P:S], dnat[:, 1, 1, h:h + 1], 0.0, ALU.subtract, ALU.min).then_inc(cu_ok, 1)

            def weigh(h):
                dve.wait_ge(lx_ok, h + 1)
                tt(lw[:, h % 3, :], lw[:, h % 3, :], cbm[:, h // 8, :], ALU.mult).then_inc(lm_ok, 1)

            def y_take(g):
                dve.wait_ge(yy_ps, 8 * g + 8)
                for t in range(NT):
                    yv = xs[:, t, 512 * g:512 * g + 512]
                    tt(yv, yv, bank[2 * (g % 2) + t][:, :], ALU.add).then_inc(yy_ok, 1)
                dve.wait_ge(yy_ok, 2 * g + 2)
                yv = xs[:, :, 512 * g:512 * g + 512]
                ch.link(tt(yv, yv, zz[:, :, 512 * g:512 * g + 512], ALU.mult))
                for t in range(NT):
                    ch.put(v_.tensor_tensor_reduce(out=zz[:, t, 512 * g:512 * g + 512], in0=xs[:, t, 512 * g:512 * g + 512],
                                                   in1=xs[:, t, 512 * g:512 * g + 512], scale=1.0, scalar=0.0, op0=ALU.mult, op1=ALU.add,
                                                   accum_out=st[:, 24 + 4 * t + g:25 + 4 * t + g]))

            decay(0)
            decay(1)
            for h in range(SSM_H):
                if h + 2 < SSM_H:
                    decay(h + 2)
                weigh(h)
                if h % 8 == 1 and h > 8:
                    y_take(h // 8 - 1)
            y_take(SSM_G - 1)
            ch.wait()
            ts(st[:, 16:24], st[:, 24:32], 1.0 / 512, EPS, ALU.mult, ALU.add).then_inc(o_var, 1)
            dve.wait_ge(o_root, 1)
            newton(st[:, 44:52], st[:, 36:44], st[:, 16:24], st[:, 52:60])
            for t in range(NT):
                for g in range(SSM_G):
                    ins = ts(xs[:, t, 512 * g:512 * g + 512], xs[:, t, 512 * g:512 * g + 512], st[:, 44 + 4 * t + g:45 + 4 * t + g], None, ALU.mult)
            ins.then_inc(yn_ok, 1)
            dve.wait_ge(mixed[1], 15)
            residual(2)
            moe(1, 3)


_INPUTS = ["x", "mix_norm", "ffn_norm", "ev_w_in", "hg_lb_logits", "hg_out_norm", "at_q_norm", "at_k_norm", "ev_w_out", "od_w_in",
           "od_conv_w", "od_conv_b", "od_dt_bias", "od_A_log", "od_D", "od_out_norm", "od_w_out", "moe_wg", "moe_bg", "moe_we",
           "moe_be", "moe_w1", "moe_w3", "moe_w2"]


def constants():
    p = np.arange(P)
    con = np.zeros((P, C_END), np.float32)
    con[:, C_ID:C_ID + P] = np.eye(P)
    upto = (p[:, None] <= p[None, :]).astype(np.float32)
    con[:, C_M3:C_M3 + 384] = np.concatenate([upto, np.ones((P, P)), upto], 1)
    con[:, C_STRICT:C_STRICT + P] = p[:, None] < p[None, :]
    for t in range(NT):
        q_chunk, k_chunk = (P * t + p) // 64, np.arange(S) // 64
        con[:, C_ADM + S * t:C_ADM + S * (t + 1)] = np.where(k_chunk[None, :] <= q_chunk[:, None], 0.0, NEG)
        inv = np.exp(np.float32(-np.log(10000.0)) * np.arange(32, dtype=np.float32) / np.float32(32)).astype(np.float32)
        ang = (P * t + p).astype(np.float32)[:, None] * inv[None, :]
        con[:, C_CS + 64 * t:C_CS + 64 * t + 32] = np.cos(ang)
        con[:, C_CS + 64 * t + 32:C_CS + 64 * t + 64] = np.sin(ang)
    con[:, C_IOTA:C_IOTA + 32] = np.arange(32)
    con[:, C_THR:C_THR + 8] = CAP * np.arange(8)
    lvl = np.zeros((P, 8, P), np.int32)
    lvl[:, 0, :] = np.eye(P)
    for v in range(1, 8):
        half = 64 >> (v - 1)
        s_, t_ = p[:, None], p[None, :]
        lvl[:, v, :] = (s_ // (2 * half) == t_ // (2 * half)) & (s_ // half % 2 == 0) & (t_ // half % 2 == 1)
    return con, lvl


def kernel(**inputs):
    import concourse.bacc as bacc
    from concourse import mybir
    from concourse.bass_utils import run_bass_kernel_spmd

    nc = bacc.Bacc("TRN2", target_bir_lowering=False, num_devices=1)
    con, lvl = constants()
    arrays, A = {}, {}
    for name, a in [(n, inputs[n]) for n in _INPUTS] + [("con", con), ("lvl", lvl)]:
        a = np.ascontiguousarray(a)
        arrays["in_" + name] = a
        A[name] = nc.dram_tensor("in_" + name, a.shape, mybir.dt.from_np(a.dtype), kind="ExternalInput").ap()
    out = nc.dram_tensor("out", (1, S, D), mybir.dt.float32, kind="ExternalOutput").ap()
    build(nc, A, out)
    r = run_bass_kernel_spmd(nc, [arrays], core_ids=[0])
    return r.results[0]["out"]
```

```python
import numpy as np

D, S, P = 1024, 256, 128
KT = D // P
NT = S // P
RING = 6
UNIT = 4096
EPS = 1e-6
NEG = -1.0e30
GONE = -3.0e38
MARK = 3.0e38
HG = 4
TOPK = 64
EXPERTS, GROUP, CAP, FF = 32, 4, 32, 512
NGROUPS = EXPERTS // GROUP
ROUNDS = S // CAP
MIX_UNITS = (9, 15)
STEP_UNITS = 3 * GROUP
SSM_H, SSM_G = 32, 4
NL, AHEAD = 5, 3
ORDER = [(0, 0), (0, 1), (1, 0), (1, 1), (1 - 1, 2), (2, 0), (2, 1), (1, 2), (3, 0), (3, 1), (2, 2), (3, 2)]
C_ID, C_M3, C_STRICT, C_ADM, C_CS, C_IOTA, C_THR = 0, 128, 512, 640, 1152, 1280, 1312
C_END = 1320
V_MIX, V_FFN, V_HG, V_LB, V_OD, V_CB, V_CW = 0, 16, 32, 36, 44, 60, 84
E_Q, E_F, E_I, E_G, E_AQ, E_AK, E_AV, E_IQ, E_IK = 0, 512, 1024, 1536, 2048, 2560, 2688, 2816, 3072


BATCHES = [(0, list(range(8))), (1, [0, 1, 4, 5]), (1, [2, 3, 6, 7])]
PE_ORDER = [("level", 0), ("unit", 5), ("score", 0), ("level", 1), ("level", 2), ("unit", 6), ("turn", 0), ("value", 0),
            ("score", 1), ("level", 3), ("level", 4), ("level", 5), ("turn", 1), ("value", 1),
            ("score", 2), ("level", 6), ("level", 7), ("level", 8), ("turn", 2), ("sum", 0), ("value", 2)]
DVE_ORDER = [("level", 0), ("keys", 0), ("mix", 1), ("mix", 2), ("score", 0), ("level", 1), ("mix", 3), ("level", 2), ("mix", 4),
             ("keys", 1), ("value", 0), ("score", 1), ("level", 3), ("mix", 5), ("level", 4), ("mix", 6), ("level", 5), ("mix", 7),
             ("value", 1), ("score", 2), ("level", 6), ("mix", 8), ("level", 7), ("level", 8), ("sum", 0), ("value", 2)]
ACT_ORDER = [("level", 1), ("unit", 5), ("level", 2), ("score", 0), ("level", 3), ("level", 4), ("unit", 6), ("turn", 0),
             ("score", 1), ("level", 5), ("level", 6), ("level", 7), ("turn", 1), ("score", 2), ("level", 8), ("turn", 2)]
OUT_BLOCKS = [[1, 0], [0, 1, 2, 3]]
PAIRED = [("unit", 3), ("unit", 4)] + [x for x in PE_ORDER if x[0] in ("level", "unit")]
PAIR = {x: ((2, 3), (0, 1))[n % 2] for n, x in enumerate(PAIRED)}


def finished(expert, part):
    return ORDER.index((expert, part)) + 1


def slot_of(layer, unit):
    return (unit + 3 * layer) % RING


def build(nc, A, out):
    import concourse.bass as bass
    from concourse import mybir
    from contextlib import ExitStack

    f32, i32 = mybir.dt.float32, mybir.dt.int32
    ALU, ACT, AX = mybir.AluOpType, mybir.ActivationFunctionType, mybir.AxisListType
    ctx = ExitStack()
    with ctx:
        def sb(name, shape, dt=f32, c=ctx):
            return c.enter_context(nc.sbuf_tensor(name, shape, dt))

        def sem(name):
            return ctx.enter_context(nc.semaphore(name))

        class Chain:

            def __init__(self, eng, s, base=0):
                self.eng, self.s, self.base, self.n = eng, s, base, 0

            def put(self, ins):
                self.n += 1
                ins.then_inc(self.s, 1)

            def wait(self):
                self.eng.wait_ge(self.s, self.base + self.n)

            def link(self, ins):
                self.put(ins)
                self.wait()

        ring = sb("ring", [P, RING, UNIT])
        con = sb("con", [P, C_END])
        lvl = sb("lvl", [P, 8, P], i32)
        ones = sb("ones", [P, 256])
        zeros = sb("zeros", [P, 256])
        zero_b = zeros[:, :].bitcast(mybir.dt.bfloat16)
        x = sb("x", [P, NT, D])
        xn = sb("xn", [P, NT, D])
        hT = sb("hT", [P, KT, S])
        vrow = sb("vrow", [96, 256])
        vT = sb("vT", [P, 184])
        wr = sb("wr", [P, 2, KT, 36])
        br = sb("br", [P, 2, 36])
        st = sb("st", [P, 64])
        rounds = sb("rounds", [P, 4], i32)
        ident = con[:, C_ID:C_ID + P]
        mask3 = con[:, C_M3:C_M3 + 384]
        strict = con[:, C_STRICT:C_STRICT + P]
        adm = con[:, C_ADM:C_ADM + 512].rearrange("p (a s) -> p a s", a=2)
        cs = con[:, C_CS:C_CS + 128].rearrange("p (a s) -> p a s", a=2)
        iota = con[:, C_IOTA:C_IOTA + 32]
        thr = con[:, C_THR:C_THR + 8]
        bank = [ctx.enter_context(nc.psum_tensor(f"bank{i}", [P, 512], f32)) for i in range(8)]

        def half(v):
            return P if v == 8 else 64 >> (v - 1)

        def halves(a, v):
            return a.rearrange("p h (n w t) -> p (h n) w t", w=2, t=half(v))

        with ExitStack() as c:
            rb = sb("rb", [P, NT, 16, 64], c=c)
            ro = sb("ro", [P, NT, 16, 64], c=c)
            rt = sb("rt", [P, 4, 512], c=c)
            tt_ = sb("tt_", [P, 8, S], c=c)
            av = sb("av", [P, NT, P], c=c)
            iw = sb("iw", [P, NT, 4], c=c)
            sc = sb("sc", [P, NT, S], c=c)
            wk = sb("wk", [P, NT, S], c=c)
            mx8 = sb("mx8", [P, NT, 8], c=c)
            pr = sb("pr", [P, 1024], c=c)
            sm = sb("sm", [P, 3, 32], c=c)
            qT = sb("qT", [P, HG, S], c=c)
            kk = sb("kk", [P, HG, S], c=c)
            lb_ = sb("lb_", [P, HG, S], c=c)
            bb = sb("bb", [P, HG, S], c=c)
            vv = sb("vv", [P, NT, 512], c=c)
            gg = sb("gg", [P, NT, 512], c=c)
            aT = sb("aT", [P, NT, HG, P], c=c)
            aX = sb("aX", [P, HG, P], c=c)
            lbv = sb("lbv", [P, 40], c=c)
            qkn = sb("qkn", [P, 2, 64], c=c)
        xe = rb[:, :, :, :].rearrange("p a h d -> p (a h d)").rearrange("p (n h t) -> p n h t", n=2, h=HG)
        ee = ro[:, :, :, :].rearrange("p a h d -> p (a h d)").rearrange("p (n h t) -> p n h t", n=2, h=HG)
        pT = rt[:, 0:2, :].rearrange("p a n -> p (a n)")
        rl = rt[:, :, 0:256]
        with ExitStack() as c:
            zz = sb("zz", [P, NT, 2048], c=c)
            xs = sb("xs", [P, NT, 2048], c=c)
            xd = sb("xd", [P, NT, 2048], c=c)
            bT = sb("bT", [P, SSM_G, S], c=c)
            cT = sb("cT", [P, SSM_G, S], c=c)
            cv = sb("cv", [P, 3, 260], c=c)
            ca = sb("ca", [P, 3, S], c=c)
            dts = sb("dts", [32, 8], c=c)
            dnat = sb("dnat", [P, NT, 2, 32], c=c)
            dsk = sb("dsk", [P, 32], c=c)
            cumT = sb("cumT", [P, S], c=c)
            dtT = sb("dtT", [32, S], c=c)
        dtmp = zz[0:32, 0, :].rearrange("p (n t) -> p n t", n=8)
        xsT = xn[:, :, :].rearrange("p a d -> p (a d)").rearrange("p (n t) -> p n t", n=8)
        lw = xn[:, :, :].rearrange("p a d -> p (a d)")[:, 0:384 * NL].rearrange("p (n t) -> p n t", n=NL)
        cbm = hT[:, :, :].rearrange("p k t -> p (k t)")[:, 0:1536].rearrange("p (g t) -> p g t", g=SSM_G)
        yT = xd[:, :, :].rearrange("p a d -> p (a d)").rearrange("p (k t) -> p k t", k=16)
        with ExitStack() as c:
            sel = sb("sel", [P, 8, CAP], c=c)
            pg = sb("pg", [P, NT, GROUP, 4, CAP], c=c)
            xT = sb("xT", [P, KT, P], c=c)
            pgT = sb("pgT", [P, GROUP, NT, P], c=c)
            sg = sb("sg", [P, 2, P], c=c)
            he = sb("he", [P, 2, P], c=c)
            heT = sb("heT", [P, 2, P], c=c)
            ys = sb("ys", [P, 2, D], c=c)
            rtab = sb("rtab", [P, ROUNDS * NGROUPS, 8], c=c)
            gtab = sb("gtab", [P, ROUNDS * NGROUPS, 8], c=c)
            lg = sb("lg", [P, NT, 36], c=c)
            gp = sb("gp", [P, NT, 16], c=c)
            gr = sb("gr", [P, NT, 16], c=c)
            ep = sb("ep", [P, NT, 40], c=c)
            er = sb("er", [P, NT, 40], c=c)
            m8 = sb("m8", [P, 4, NT, 8], c=c)
            arg = sb("arg", [P, NT, 36], c=c)
            g4 = sb("g4", [P, 4, NT, 4], c=c)
            s32 = sb("s32", [P, 4, NT, 32], c=c)
            rr = sb("rr", [P, 32], c=c)

        in_con, in_lvl, in_vec = sem("in_con"), sem("in_lvl"), sem("in_vec")
        in_x = [sem(f"in_x{t}") for t in range(NT)]
        in_small, in_rb, in_even, in_odd, vec_ps, vec_ok = sem("in_small"), sem("in_rb"), sem("in_even"), sem("in_odd"), sem("vec_ps"), sem("vec_ok")
        full = [[sem(f"full{l}_{s}") for s in range(RING)] for l in range(2)]
        mixed = [sem(f"mixed{l}") for l in range(2)]
        used = [sem(f"used{l}") for l in range(2)]
        var_ok, root_ok, xn_ok, hT_ps, hT_v, hT_a = (sem(n) for n in ("var_ok", "root_ok", "xn_ok", "hT_ps", "hT_v", "hT_a"))
        sq_ok = sem("sq_ok")
        x_new = sem("x_new")
        dch, ach, pch = sem("dch"), sem("ach"), sem("pch")
        e_out = sem("e_out")
        rot_ok, rot_ps, rot_t = sem("rot_ok"), sem("rot_ps"), sem("rot_t")
        ix_ps, ix_rel, ix_ok, lb_in, lb_ex = sem("ix_ps"), sem("ix_rel"), sem("ix_ok"), sem("lb_in"), sem("lb_ex")
        qk_var, qk_root = sem("qk_var"), sem("qk_root")
        ql_ps, at_max, at_exp, at_tps, at_t, pv_ps, at_o = (sem(n) for n in
            ("ql_ps", "at_max", "at_exp", "at_tps", "at_t", "pv_ps", "at_o"))
        lb_ok, f_lin, f_log, k_ok, b_ok = sem("lb_ok"), sem("f_lin"), sem("f_log"), sem("k_ok"), sem("b_ok")
        ex_in, ex_out, lv_x, lv_ps, lv_ok = sem("ex_in"), sem("ex_out"), sem("lv_x"), sem("lv_ps"), sem("lv_ok")
        ov_ok, ho_ps, ho_var, ho_root, on_ok = sem("ov_ok"), sem("ho_ps"), sem("ho_var"), sem("ho_root"), sem("on_ok")
        mo_ps = [sem(f"mo_ps{l}") for l in range(2)]
        mo_acc = [sem(f"mo_acc{l}") for l in range(2)]
        mo_t = [sem(f"mo_t{l}") for l in range(2)]
        mp_ok = [sem(f"mp_ok{l}") for l in range(2)]
        dt_b, dt_e, dt_l, dt_ok, dn_ps, dn_ok = (sem(n) for n in ("dt_b", "dt_e", "dt_l", "dt_ok", "dn_ps", "dn_ok"))
        raw_in, cv_ok, act_ok, xs_ps, xs_ok, z_ok = (sem(n) for n in ("raw_in", "cv_ok", "act_ok", "xs_ps", "xs_ok", "z_ok"))
        cb_ps, cb_ok, cu_ps, cu_ok, lx_ok, lm_ok, yy_ps, yy_ok = (sem(n) for n in
            ("cb_ps", "cb_ok", "cu_ps", "cu_ok", "lx_ok", "lm_ok", "yy_ps", "yy_ok"))
        o_var, o_root, yn_ok, al_in, al_ex = sem("o_var"), sem("o_root"), sem("yn_ok"), sem("al_in"), sem("al_ex")
        names = ("rt_ps", "rt_in", "rt_ex", "rt_sel", "rk_ps", "rt_ok", "s_ok", "pg_ok", "ga_ps", "xt_ok",
                 "pt_ps", "pt_ok", "si_ok", "he_ok", "ht_ps", "ht_ok", "yv_ok", "ya_ok", "scat", "acc", "mdc")
        M = [{n: sem(f"{n}{l}") for n in names} for l in range(2)]
        stored = sem("stored")

        w1v = A["moe_w1"].rearrange("l e (k p) f -> l e p k f", p=P)
        w3v = A["moe_w3"].rearrange("l e (k p) f -> l e p k f", p=P)
        w2v = A["moe_w2"].rearrange("l e (k p) n -> l e p k n", p=P)
        evin = A["ev_w_in"][0].rearrange("(k p) n -> p k n", p=P)
        evout = A["ev_w_out"][0].rearrange("(k p) n -> p k n", p=P)
        odin = A["od_w_in"][0].rearrange("(k p) n -> p k n", p=P)
        odout = A["od_w_out"][0].rearrange("(k p) n -> p k n", p=P)
        EVEN = [(E_AK, 512), (E_IK, 68), (E_AQ, 512), (E_F, 512), (E_Q, 512), (E_I, 512), (E_G, 512)]
        ODD = [(5120, 32), (4096, 512), (4608, 512)] + [(2048 + 512 * u, 512) for u in range(4)] + \
              [(512 * u, 512) for u in range(4)]

        def wslot(layer, unit, n):
            return ring[:, slot_of(layer, unit), 0:(UNIT // 512 if n <= 512 else 4) * n].rearrange("p (k n) -> p k n", n=n)

        def full_at(layer, unit):
            return 32 * (unit // RING + 1)

        block = ctx.enter_context(nc.Block())

        @block.sync
        def _(sp):
            def load(layer, unit, halves):
                for dst, src in halves:
                    sp.dma_start(dst, src).then_inc(full[layer][slot_of(layer, unit)], 16)

            def in_unit(layer, unit, w, c0, n):
                d = wslot(layer, unit, n)
                load(layer, unit, [(d[:, 4 * h:4 * h + 4, :], w[:, 4 * h:4 * h + 4, c0:c0 + n]) for h in range(2)])

            def out_unit(layer, unit, w, k0):
                d = wslot(layer, unit, 1024)
                load(layer, unit, [(d[:, 2 * h:2 * h + 2, :], w[:, k0 + 2 * h:k0 + 2 * h + 2, :]) for h in range(2)])

            def moe_unit(layer, j, e):
                unit = MIX_UNITS[layer] + j
                d, part = ring[:, slot_of(layer, unit), :], j % 3
                if part < 2:
                    d = d.rearrange("p (k w f) -> p k w f", k=4, w=2)
                    pairs = [(d[:, :, w, :], v[layer, bass.ds(e, 1), :, 4 * part:4 * part + 4, :]
                              .rearrange("e p k f -> (e p) k f")) for w, v in enumerate((w1v, w3v))]
                else:
                    d = d.rearrange("p (k n) -> p k n", k=4)
                    pairs = [(d[:, 2 * h:2 * h + 2, :], w2v[layer, bass.ds(e, 1), :, 2 * h:2 * h + 2, :]
                              .rearrange("e p k n -> (e p) k n")) for h in range(2)]
                load(layer, unit, pairs)

            for t in range(NT):
                sp.dma_start(x[:, t, :], A["x"][0, P * t:P * t + P, :]).then_inc(in_x[t], 16)
            sp.dma_start(con[:, :], A["con"]).then_inc(in_con, 16)
            rows = lambda a: a.rearrange("(r c) -> r c", c=P)
            sp.dma_start(vrow[0:16, 0:P], A["mix_norm"].rearrange("l (r c) -> (l r) c", c=P)).then_inc(in_vec, 16)
            sp.dma_start(vrow[16:32, 0:P], A["ffn_norm"].rearrange("l (r c) -> (l r) c", c=P)).then_inc(in_vec, 16)
            sp.dma_start(vrow[32:36, 0:P], rows(A["hg_out_norm"][0])).then_inc(in_vec, 16)
            sp.dma_start(vrow[36:44, 0:P], A["hg_lb_logits"].rearrange("l (r c) -> (l r) c", c=P)).then_inc(in_vec, 16)
            sp.dma_start(vrow[44:60, 0:P], rows(A["od_out_norm"][0])).then_inc(in_vec, 16)
            sp.dma_start(vrow[0:96, P:2 * P], A["od_conv_w"][0].rearrange("j (r c) -> (j r) c", c=P)).then_inc(in_vec, 16)
            sp.dma_start(vrow[60:84, 0:P], rows(A["od_conv_b"][0])).then_inc(in_vec, 16)
            for layer in range(2):
                for v in range(MIX_UNITS[layer]):
                    if v >= RING:
                        sp.wait_ge(mixed[layer], v - RING + 1)
                    elif layer == 1:
                        j = v + RING
                        sp.wait_ge(used[0], last_step * STEP_UNITS + finished(j // 3, j % 3))
                    if layer == 0:
                        if v < len(EVEN):
                            in_unit(0, v, evin, *EVEN[v])
                        else:
                            out_unit(0, v, evout, 4 * OUT_BLOCKS[0][v - len(EVEN)])
                    else:
                        if v < len(ODD):
                            in_unit(1, v, odin, *ODD[v])
                        else:
                            out_unit(1, v, odout, 4 * OUT_BLOCKS[1][v - len(ODD)])
                for j in range(STEP_UNITS):
                    if j == RING - 1:
                        sp.wait_ge(mo_acc[layer], NT)
                    elif j < RING:
                        sp.wait_ge(mixed[layer], MIX_UNITS[layer] + j - RING + 1)
                    else:
                        sp.wait_ge(used[layer], finished((j - RING) // 3, (j - RING) % 3))
                    moe_unit(layer, j, j // 3)
                sp.wait_ge(M[layer]["rt_ok"], 1)
                last_step = sp.value_load(rounds[0:1, 2 + layer:3 + layer], min_val=NGROUPS - 1, max_val=ROUNDS * NGROUPS - 1)
                with sp.Fori(0, last_step) as i:
                    for j in range(STEP_UNITS):
                        q = (j + RING) % STEP_UNITS
                        sp.wait_ge(used[layer], (i + (0 if j < RING else 1)) * STEP_UNITS + finished(q // 3, q % 3))
                        moe_unit(layer, j, ((i + 1) % NGROUPS) * GROUP + j // 3)
            sp.wait_ge(x_new, 16)
            sp.dma_start(out[0].rearrange("(a p) d -> p a d", p=P), x[:, :, :]).then_inc(stored, 16)
            sp.wait_ge(stored, 16)

        @block.tensor
        def _(pe):
            mm, tr = nc.tensor.matmul, nc.tensor.transpose

            def loaded(layer, unit, extra=0):
                pe.wait_ge(full[layer][slot_of(layer, unit)], full_at(layer, unit) + extra)

            def norm_transposes(n):
                pe.wait_ge(x_new, 4 * n) if n else None
                for t in range(NT):
                    pe.wait_ge(xn_ok, 2 * n + t + 1)
                    for k in range(KT):
                        c0 = 256 * (k % 2) + P * t
                        last = tr(bank[k // 2][:, c0:c0 + P], xn[:, t, P * k:P * k + P], ident)
                        if t == 1 and k % 2:
                            last.then_inc(hT_ps, 1)

            def hT_ready(n):
                pe.wait_ge(hT_v, 4 * n + 4)
                pe.wait_ge(hT_a, 4 * n + 4)

            def rows_product(layer, unit, n, banks):
                w = wslot(layer, unit, n)
                for t in range(NT):
                    for k in range(KT):
                        last = mm(bank[banks[t]][:, 0:n], hT[:, k, P * t:P * t + P], w[:, k, :], start=(k == 0), stop=(k == KT - 1))
                last.then_inc(mixed[layer], 1)

            def cols_product(layer, unit, banks):
                w = wslot(layer, unit, 512)
                for c in range(4):
                    for k in range(KT):
                        last = mm(bank[banks[c // 2]][:, 256 * (c % 2):256 * (c % 2) + 256], w[:, k, P * c:P * c + P],
                                  hT[:, k, :], start=(k == 0), stop=(k == KT - 1))
                last.then_inc(mixed[layer], 1)

            def pair_free(kind, n):
                k, m = PAIRED[PAIRED.index((kind, n)) - 2]
                if k == "unit":
                    pe.wait_ge(e_out, m + 1)
                else:
                    pe.wait_ge(lv_ok, m + 1)

            pe.wait_ge(in_con, 16)
            pe.wait_ge(in_vec, 16 * 7)
            tr(bank[7][:, 0:84], vrow[0:84, 0:P], ident[0:84, 0:84])
            tr(bank[7][:, 84:180], vrow[0:96, P:2 * P], ident[0:96, 0:96]).then_inc(vec_ps, 1)

            norm_transposes(0)
            hT_ready(0)
            for u in range(4):
                loaded(0, u)
                if u >= 2:
                    pe.wait_ge(e_out, u - 1)
                if u == 3:
                    cols_product(0, u, (2, 3))
                else:
                    rows_product(0, u, EVEN[u][1], ((0, 1), (2, 3))[u % 2])
            pe.wait_ge(rot_ok, 2)
            pe.wait_ge(vec_ok, 1)
            for s_ in range(8):
                for t in range(NT):
                    src = ro[:, t, 2 * s_:2 * s_ + 2, :].rearrange("p h d -> p (h d)")
                    last = tr(bank[4 + s_ // 2][:, 256 * (s_ % 2) + P * t:256 * (s_ % 2) + P * t + P], src, ident)
                if s_ % 2:
                    last.then_inc(rot_ps, 1)
            loaded(0, 4)
            pe.wait_ge(e_out, 3)
            cols_product(0, 4, PAIR["unit", 4])
            pe.wait_ge(rot_t, 4)
            for t in range(NT):
                n = P * (t + 1)
                for h in range(4):
                    r0 = 64 * (h % 2)
                    last = mm(bank[4 + 2 * t + h % 2][:, n * (h // 2):n * (h // 2) + n], tt_[r0:r0 + 64, 5 + h // 2, P * t:P * t + P],
                              tt_[r0:r0 + 64, 7, 0:n], start=True, stop=True)
                last.then_inc(ix_ps, 1)

            def unit(u):
                loaded(0, u)
                pair_free("unit", u)
                rows_product(0, u, 512, PAIR["unit", u])

            def score(b):
                t, heads = BATCHES[b]
                n = P * (t + 1)
                pe.wait_ge(ix_rel, 2)
                if b:
                    pe.wait_ge(at_o, b)
                for m, h in enumerate(heads):
                    r0, o = 64 * (h // 4), m % (len(heads) // 2)
                    last = mm(bank[4 + h // 4][:, n * o:n * o + n], tt_[r0:r0 + 64, h % 4, P * t:P * t + P],
                              tt_[r0:r0 + 64, 4, 0:n], start=True, stop=True)
                last.then_inc(ql_ps, 1)

            def turn(b):
                pe.wait_ge(at_exp, b + 1)
                for j in range(8):
                    last = tr(bank[6 + j // 4][:, P * (j % 4):P * (j % 4) + P], pr[:, P * j:P * j + P], ident)
                    if j % 4 == 3:
                        last.then_inc(at_tps, 1)

            def value(b):
                t, heads = BATCHES[b]
                pe.wait_ge(at_t, 2 * (b + 1))
                for m, h in enumerate(heads):
                    for s_ in range(t + 1):
                        j = m * (t + 1) + s_
                        last = mm(bank[4][:, 64 * m:64 * m + 64], pT[:, P * j:P * j + P], av[:, s_, 64 * (h // 4):64 * (h // 4) + 64],
                                  start=(s_ == 0), stop=(s_ == t))
                last.then_inc(pv_ps, 1)

            def level(v):
                if v == 0:
                    pe.wait_ge(k_ok, 1)
                    pe.wait_ge(e_out, 5)
                else:
                    pe.wait_ge(lv_x, v)
                pair_free("level", v)
                for t in range(NT if v < 8 else 1):
                    for h in range(HG):
                        o = bank[PAIR["level", v][t]][:, P * h:P * h + P]
                        if v == 0:
                            last = mm(o, kk[:, h, P * t:P * t + P], qT[:, h, P * t:P * t + P], start=True, stop=True)
                        else:
                            e, tq = xe[:, v % 2, h, :], t if v < 8 else 1
                            last = mm(o, e[:, P * t:P * t + P], e[:, P * tq:P * tq + P], start=True, stop=True)
                last.then_inc(lv_ps, 1)

            def hgrn_sum(_):
                pe.wait_ge(e_out, 7)
                pe.wait_ge(lv_ok, 9)
                for t in range(NT):
                    for h in range(HG):
                        for s_ in range(t + 1):
                            w = aX[:, h, :] if s_ < t else aT[:, t, h, :]
                            last = mm(bank[2 + t][:, P * h:P * h + P], w, vv[:, s_, P * h:P * h + P], start=(s_ == 0), stop=(s_ == t))
                    last.then_inc(ho_ps, 1)

            for kind, n in PE_ORDER:
                {"level": level, "unit": unit, "score": score, "turn": turn, "value": value, "sum": hgrn_sum}[kind](n)

            def out_projection(layer, src, dst, ready, banks_read):
                blocks = OUT_BLOCKS[layer]

                def transposes(u):
                    pe.wait_ge(*ready[u])
                    for b in (2 * u, 2 * u + 1):
                        if b >= 4:
                            pe.wait_ge(mo_t[layer], b - 3)
                        for i in range(2):
                            for t in range(NT):
                                k, c0 = 4 * blocks[u] + 2 * (b % 2) + i, 256 * i + P * t
                                last = tr(bank[4 + b % 4][:, c0:c0 + P], src[:, t, P * k:P * k + P], ident)
                        last.then_inc(mo_ps[layer], 1)

                def product(u):
                    unit = MIX_UNITS[layer] - len(blocks) + u
                    loaded(layer, unit)
                    pe.wait_ge(mo_t[layer], 2 * u + 2)
                    w = wslot(layer, unit, 1024)
                    end = u == len(blocks) - 1
                    for t in range(NT):
                        for k in range(4):
                            for h in range(2):
                                last = mm(bank[2 * t + h][:, :], dst[:, 4 * blocks[u] + k, P * t:P * t + P], w[:, k, 512 * h:512 * h + 512],
                                          start=(u == 0 and k == 0), stop=(end and k == 3))
                        if end:
                            last.then_inc(mo_acc[layer], 1)
                    if not end:
                        last.then_inc(mixed[layer], 1)

                transposes(0)
                pe.wait_ge(*banks_read)
                for u in range(1, len(blocks)):
                    if u > 1 or len(blocks) > 2:
                        transposes(u)
                        product(u - 1)
                    else:
                        product(u - 1)
                        transposes(u)
                product(len(blocks) - 1)

            out_projection(0, xn, hT, [(at_o, 3), (on_ok, 1)], (ov_ok, 2))

            def moe(layer, n):
                m = M[layer]
                norm_transposes(n)
                hT_ready(n)
                pe.wait_ge(in_small, 16 * 4)
                for t in range(NT):
                    for k in range(KT):
                        last = mm(bank[4][:, 36 * t:36 * t + 36], hT[:, k, P * t:P * t + P], wr[:, layer, k, :], start=(k == 0), stop=(k == KT - 1))
                last.then_inc(m["rt_ps"], 1)
                for a in range(4):
                    mm(bank[a][:, :], zero_b[:, 0:P], zero_b, start=True, stop=False)
                pe.wait_ge(m["rt_sel"], 1)
                for t in range(NT):
                    for s_ in range(t + 1):
                        mm(bank[5][:, 32 * t:32 * t + 32], strict if s_ == t else ones[:, 0:P], s32[:, 0, s_, :], start=(s_ == 0), stop=(s_ == t))
                for s_ in range(NT):
                    last = mm(bank[5][:, 64:96], ones[:, 0:P], s32[:, 0, s_, :], start=(s_ == 0), stop=(s_ == NT - 1))
                last.then_inc(m["rk_ps"], 1)
                pe.wait_ge(m["rt_ok"], 1)
                nr = pe.value_load(rounds[0:1, layer:layer + 1], min_val=1, max_val=ROUNDS)
                base = MIX_UNITS[layer]
                with pe.Fori(0, nr * NGROUPS) as i:
                    pe.wait_ge(m["s_ok"], i + 1)
                    for k in range(KT):
                        for t in range(NT):
                            last = mm(bank[6 + k // 4][:, P * (k % 4):P * (k % 4) + P], xn[:, t, P * k:P * k + P],
                                      sel[:, 4 * t:4 * t + 4, :].rearrange("p e c -> p (e c)"), start=(t == 0), stop=(t == NT - 1))
                    last.then_inc(m["ga_ps"], 1)
                    pe.wait_ge(m["pg_ok"], i + 1)
                    for e in range(GROUP):
                        for t in range(NT):
                            c0 = 256 * (e % 2) + P * t
                            last = tr(bank[4 + e // 2][:, c0:c0 + P], pg[:, t, e, :, :].rearrange("p j c -> p (j c)"), ident)
                    last.then_inc(m["pt_ps"], 1)

                    def up(e):
                        for part in range(2):
                            u = base + 3 * e + part
                            loaded(layer, u, i * 64)
                            w = ring[:, slot_of(layer, u), :].rearrange("p (k w f) -> p k w f", k=4, w=2)
                            for k in range(4):
                                for j in range(4):
                                    last = mm(bank[4 + e % 2][32 * j:32 * j + 32, 0:256], xT[:, 4 * part + k, CAP * e:CAP * e + CAP],
                                              w[:, k, :, P * j:P * j + P], start=(part == 0 and k == 0), stop=(part == 1 and k == 3))
                            last.then_inc(used[layer], 1)

                    def turn(e):
                        pe.wait_ge(m["he_ok"], i * 4 + e + 1)
                        if e:
                            pe.wait_ge(m["yv_ok"], i * 4 + e)
                        tr(bank[6][:, 0:P], he[:, e % 2, :], ident).then_inc(m["ht_ps"], 1)

                    def down(e):
                        u = base + 3 * e + 2
                        loaded(layer, u, i * 64)
                        pe.wait_ge(m["ht_ok"], i * 4 + e + 1)
                        if e:
                            pe.wait_ge(m["ya_ok"], i * 4 + e)
                        w = ring[:, slot_of(layer, u), :].rearrange("p (k n) -> p k n", k=4)
                        for h in range(2):
                            for j in range(4):
                                last = mm(bank[6 + h][32 * j:32 * j + 32, :], heT[:, e % 2, CAP * j:CAP * j + CAP],
                                          w[:, j, 512 * h:512 * h + 512], start=True, stop=True)
                        last.then_inc(used[layer], 1)

                    def scatter(e):
                        pe.wait_ge(m["yv_ok"], i * 4 + e + 1)
                        pe.wait_ge(m["ya_ok"], i * 4 + e + 1)
                        for t in range(NT):
                            for h in range(2):
                                last = mm(bank[2 * t + h][:, :], pgT[:, e, t, :], ys[:, e % 2, 512 * h:512 * h + 512], start=False, stop=False)
                        last.then_inc(m["scat"], 1)

                    pe.wait_ge(m["xt_ok"], i * 2 + 2)
                    pe.wait_ge(m["pt_ok"], i * 2 + 2)
                    up(0); up(1); turn(0); down(0)
                    up(2); turn(1); down(1); scatter(0)
                    up(3); turn(2); down(2); scatter(1)
                    turn(3); down(3); scatter(2); scatter(3)
                for t in range(NT):
                    for h in range(2):
                        last = mm(bank[2 * t + h][:, :], zero_b[:, 0:P], zero_b, start=False, stop=True)
                    last.then_inc(m["acc"], 1)

            moe(0, 1)

            norm_transposes(2)
            hT_ready(2)
            loaded(1, 0)
            w = wslot(1, 0, 32)
            for k in range(KT):
                last = mm(bank[4][0:32, 0:S], w[:, k, :], hT[:, k, :], start=(k == 0), stop=(k == KT - 1))
            last.then_inc(mixed[1], 1)

            def dt_rows():
                pe.wait_ge(dt_ok, 1)
                for t in range(NT):
                    mm(bank[5][:, 64 * t:64 * t + 32], dtT[:, P * t:P * t + P], ident[0:32, 0:32], start=True, stop=True)
                    last = mm(bank[5][:, 64 * t + 32:64 * t + 64], cumT[0:32, P * t:P * t + P], ident[0:32, 0:32], start=True, stop=True)
                last.then_inc(dn_ps, 1)

            def xs_rows(u):
                pe.wait_ge(act_ok, 8 + 4 * u + 4)
                pb = (4, 5) if u % 2 == 0 else (6, 7)
                if u >= 2:
                    pe.wait_ge(xs_ok, 2 * (u - 1))
                for t in range(NT):
                    for c in range(4):
                        last = tr(bank[pb[t]][:, P * c:P * c + P], xsT[:, (4 * u + c) % 8, P * t:P * t + P], ident)
                last.then_inc(xs_ps, 1)

            for u in range(1, 7):
                loaded(1, u)
                if u >= 3:
                    pe.wait_ge(raw_in, 4 * (u - 2))
                cols_product(1, u, ((2, 3), (0, 1))[u % 2])
                if u == 1:
                    dt_rows()
                if u == 3:
                    pe.wait_ge(dn_ok, 1)
                if u >= 4:
                    xs_rows(u - 4)
            for u in range(7, 11):
                loaded(1, u)
                pe.wait_ge(raw_in, 4 * min(u - 2, 6))
                if u >= 9:
                    pe.wait_ge(z_ok, 2 * (u - 8))
                rows_product(1, u, 512, ((2, 3), (0, 1))[u % 2])
                if u == 7:
                    xs_rows(3)
            pe.wait_ge(xs_ok, 8)
            for g in range(SSM_G):
                mm(bank[4 + g][:, 0:S], bT[:, g, 0:P], cT[:, g, :], start=True, stop=True)
                mm(bank[4 + g][:, S:S + P], bT[:, g, P:S], cT[:, g, P:S], start=True, stop=True).then_inc(cb_ps, 1)
            pe.wait_ge(z_ok, 8)

            def cum_rows(h):
                if h >= 4:
                    pe.wait_ge(cu_ok, h - 3)
                else:
                    pe.wait_ge(cb_ok, 4)
                mm(bank[4 + h % 4][:, 0:S], ident[:, h:h + 1].to_broadcast([P, P]), cumT[:, :], start=True, stop=True).then_inc(cu_ps, 1)

            def y_head(h):
                g, o = h // 8, 64 * (h % 8)
                pe.wait_ge(lm_ok, h + 1)
                if h % 8 == 0 and g >= 2:
                    pe.wait_ge(yy_ok, 2 * (g - 1))
                b = 2 * (g % 2)
                l_ = lw[:, h % NL, :]
                mm(bank[b][:, o:o + 64], l_[:, 0:P], xd[:, 0, 64 * h:64 * h + 64], start=True, stop=True)
                mm(bank[b + 1][:, o:o + 64], l_[:, P:2 * P], xd[:, 0, 64 * h:64 * h + 64], start=True, stop=False)
                mm(bank[b + 1][:, o:o + 64], l_[:, 2 * P:3 * P], xd[:, 1, 64 * h:64 * h + 64], start=False, stop=True).then_inc(yy_ps, 1)

            for h in range(4):
                cum_rows(h)
            for h in range(SSM_H):
                y_head(h)
                if h + 4 < SSM_H:
                    cum_rows(h + 4)
            out_projection(1, xs, yT, [(yn_ok, 2 * g + 2) for g in range(SSM_G)], (yy_ok, 8))
            moe(1, 3)

        @block.scalar
        def _(act):
            fn = nc.scalar.activation
            ch = Chain(act, ach)
            act.dma_start(lvl[:, :, :], A["lvl"]).then_inc(in_lvl, 16)
            act.dma_start(qkn[:, 0, :], A["at_q_norm"].to_broadcast([P, 64])).then_inc(in_even, 16)
            act.dma_start(qkn[:, 1, :], A["at_k_norm"].to_broadcast([P, 64])).then_inc(in_even, 16)

            def norm_root(n):
                for t in range(NT):
                    act.wait_ge(var_ok, 2 * n + t + 1)
                    ch.link(fn(st[:, 4 + t:5 + t], st[:, 2 + t:3 + t], ACT.Ln))
                    fn(st[:, 6 + t:7 + t], st[:, 4 + t:5 + t], ACT.Exp, scale=-0.5).then_inc(root_ok, 1)

            def norm_take(n, g0):
                for b in (1, 3):
                    act.wait_ge(hT_ps, 4 * n + b + 1)
                    for k in (2 * b, 2 * b + 1):
                        fn(hT[:, k, :], bank[b][:, 256 * (k % 2):256 * (k % 2) + 256], ACT.Copy, scale=vT[:, g0 + k:g0 + k + 1]).then_inc(hT_a, 1)

            norm_root(0)
            act.wait_ge(lb_in, 1)
            fn(lbv[:, 8:16], lbv[:, 0:8], ACT.Exp).then_inc(lb_ex, 1)
            act.wait_ge(vec_ok, 1)
            norm_take(0, V_MIX)
            act.wait_ge(mixed[0], 1)
            for t in range(NT):
                fn(rb[:, t, 8:10, :], bank[t][:, 0:128], ACT.Copy)
                fn(av[:, t, :], bank[t][:, 128:256], ACT.Copy)
                last = fn(rb[:, t, 10:14, :], bank[t][:, 256:512], ACT.Copy)
            last.then_inc(e_out, 1)
            act.wait_ge(mixed[0], 2)
            for t in range(NT):
                fn(rb[:, t, 14, :], bank[2 + t][:, 0:64], ACT.Copy)
                fn(rb[:, t, 15, :], bank[2 + t][:, 0:64], ACT.Copy)
                last = fn(iw[:, t, :], bank[2 + t][:, 64:68], ACT.Copy)
            last.then_inc(e_out, 1)
            act.wait_ge(mixed[0], 3)
            for t in range(NT):
                last = fn(rb[:, t, 0:8, :].rearrange("p (i v) d -> p v i d", v=2), bank[t][:, :].rearrange("p (v i d) -> p v i d", v=2, i=4), ACT.Copy)
            last.then_inc(e_out, 1)
            act.wait_ge(qk_var, 1)
            ch.link(fn(st[:, 36:56], st[:, 16:36], ACT.Ln))
            fn(st[:, 36:56], st[:, 36:56], ACT.Exp, scale=-0.5).then_inc(qk_root, 1)
            act.wait_ge(mixed[0], 4)
            for c in range(2):
                fn(lb_[:, 2 * c:2 * c + 2, :], bank[2 + c][:, :], ACT.Sigmoid)
                last = fn(kk[:, 2 * c:2 * c + 2, :], bank[2 + c][:, :], ACT.Sigmoid, scale=-1.0)
            last.then_inc(e_out, 1)
            for b in range(4):
                act.wait_ge(rot_ps, b + 1)
                fn(tt_[:, 2 * b:2 * b + 2, :], bank[4 + b][:, :], ACT.Copy).then_inc(rot_t, 1)
            act.wait_ge(mixed[0], 5)
            for c in range(2):
                last = fn(qT[:, 2 * c:2 * c + 2, :], bank[PAIR["unit", 4][c]][:, :], ACT.Copy)
            last.then_inc(e_out, 1)
            act.wait_ge(rot_ok, 2)
            for t in range(NT):
                act.wait_ge(ix_ps, t + 1)
                if t:
                    act.wait_ge(ix_ok, 1)
                n = P * (t + 1)
                for r in range(2):
                    last = fn(rl[:, r:4:2, 0:n], bank[4 + 2 * t + r][:, 0:2 * n].rearrange("p (h s) -> p h s", h=2), ACT.Relu)
                last.then_inc(ix_rel, 1)
            act.wait_ge(f_lin, 1)
            fn(lb_[:, :, :], lb_[:, :, :], ACT.Ln).then_inc(f_log, 1)

            def unit(u):
                act.wait_ge(mixed[0], u + 1)
                for t in range(NT):
                    last = fn((vv, gg)[u - 5][:, t, :], bank[PAIR["unit", u][t]][:, :], (ACT.Copy, ACT.Silu)[u - 5])
                last.then_inc(e_out, 1)

            def level(v):
                act.wait_ge(ex_in, v)
                fn(ee[:, v % 2, :, :], ee[:, v % 2, :, :], ACT.Exp).then_inc(ex_out, 1)

            def score(b):
                t, heads = BATCHES[b]
                n = P * (t + 1)
                act.wait_ge(at_max, b + 1)
                for m in range(len(heads)):
                    last = fn(pr[:, n * m:n * m + n], pr[:, n * m:n * m + n], ACT.Exp, bias=sm[:, b, 8 + m:9 + m], accum_out=sm[:, b, 16 + m:17 + m])
                last.then_inc(at_exp, 1)

            def turn(b):
                for j in range(2):
                    act.wait_ge(at_tps, 2 * b + j + 1)
                    fn(pT[:, 512 * j:512 * j + 512], bank[6 + j][:, :], ACT.Copy).then_inc(at_t, 1)

            for kind, n in ACT_ORDER:
                {"level": level, "unit": unit, "score": score, "turn": turn}[kind](n)
            act.wait_ge(ho_var, 1)
            ch.link(fn(st[:, 36:44], st[:, 16:24], ACT.Ln))
            fn(st[:, 36:44], st[:, 36:44], ACT.Exp, scale=-0.5).then_inc(ho_root, 1)

            def out_take(layer, kts, dst, gain):
                for b in range(kts // 2):
                    act.wait_ge(mo_ps[layer], b + 1)
                    for i in range(2):
                        k = 4 * OUT_BLOCKS[layer][b // 2] + 2 * (b % 2) + i
                        g = gain(k)
                        last = fn(dst[:, k, :], bank[4 + b % 4][:, 256 * i:256 * i + 256], ACT.Copy,
                                  scale=1.0 if g is None else vT[:, g:g + 1])
                    last.then_inc(mo_t[layer], 1)

            out_take(0, 8, hT, lambda k: V_HG + k if k < 4 else None)

            def moe(layer, n):
                m = M[layer]
                norm_root(n)
                norm_take(n, V_FFN + 8 * layer)
                act.wait_ge(m["rt_in"], 2)
                fn(arg[:, :, :], arg[:, :, :], ACT.Exp).then_inc(m["rt_ex"], 1)
                act.wait_ge(m["rt_ok"], 1)
                nr = act.value_load(rounds[0:1, layer:layer + 1], min_val=1, max_val=ROUNDS)
                with act.Fori(0, nr * NGROUPS) as i:
                    act.wait_ge(m["pt_ps"], i + 1)
                    for b in range(2):
                        fn(pgT[:, 2 * b:2 * b + 2, :, :], bank[4 + b][:, :], ACT.Copy).then_inc(m["pt_ok"], 1)

                    def silu(e):
                        act.wait_ge(used[layer], i * STEP_UNITS + finished(e, 1))
                        fn(sg[:, e % 2, :], bank[4 + e % 2][:, 0:P], ACT.Silu).then_inc(m["si_ok"], 1)

                    def take(e):
                        act.wait_ge(used[layer], i * STEP_UNITS + finished(e, 2))
                        if e >= 2:
                            act.wait_ge(m["scat"], i * 4 + e - 1)
                        fn(ys[:, e % 2, 512:1024], bank[7][:, :], ACT.Copy).then_inc(m["ya_ok"], 1)

                    silu(0); silu(1); take(0); silu(2); take(1); silu(3); take(2); take(3)

            moe(0, 1)
            act.wait_ge(x_new, 5)
            act.dma_start(dts[:, 0:1], A["od_dt_bias"].rearrange("a h -> h a")).then_inc(in_odd, 16)
            act.dma_start(dts[:, 1:2], A["od_A_log"].rearrange("a h -> h a")).then_inc(in_odd, 16)
            act.dma_start(dsk[:, :], A["od_D"].to_broadcast([P, SSM_H])).then_inc(in_odd, 16)
            norm_root(2)
            norm_take(2, V_MIX + 8)
            act.wait_ge(in_odd, 48)
            fn(dts[:, 2:3], dts[:, 1:2], ACT.Exp).then_inc(al_ex, 1)
            act.wait_ge(dt_b, 1)
            fn(dtmp[:, 2, :], dtmp[:, 1, :], ACT.Exp).then_inc(dt_e, 1)
            act.wait_ge(dt_b, 2)
            fn(dtmp[:, 4, :], dtmp[:, 3, :], ACT.Ln).then_inc(dt_l, 1)

            def raw(c):
                u, q = 1 + c // 4, c % 4
                act.wait_ge(mixed[1], u + 1)
                if c >= 3:
                    act.wait_ge(cv_ok, c - 2)
                b = ((2, 3), (0, 1))[u % 2][q // 2]
                fn(cv[:, c % 3, 3:259], bank[b][:, 256 * (q % 2):256 * (q % 2) + 256], ACT.Copy).then_inc(raw_in, 1)

            def conv_silu(c):
                act.wait_ge(cv_ok, c + 1)
                if c >= 16:
                    act.wait_ge(xs_ps, (c - 8) // 4 - 1)
                dst = bT[:, c, :] if c < 4 else cT[:, c - 4, :] if c < 8 else xsT[:, c % 8, :]
                fn(dst, ca[:, c % 3, :], ACT.Silu).then_inc(act_ok, 1)

            for c in range(24):
                raw(c)
                if c:
                    conv_silu(c - 1)
            conv_silu(23)
            for u in range(4):
                act.wait_ge(mixed[1], 8 + u)
                for t in range(NT):
                    b = ((2, 3), (0, 1))[(u + 7) % 2][t]
                    fn(zz[:, t, 512 * u:512 * u + 512], bank[b][:, :], ACT.Silu).then_inc(z_ok, 1)

            def y_root(g):
                act.wait_ge(o_var, g + 1)
                a = 36 + 2 * g
                ch.link(fn(st[:, a:a + 2], st[:, a - 20:a - 18], ACT.Ln))
                fn(st[:, a:a + 2], st[:, a:a + 2], ACT.Exp, scale=-0.5).then_inc(o_root, 1)

            for h in range(SSM_H):
                act.wait_ge(cu_ok, h + 1)
                fn(lw[:, h % NL, :], lw[:, h % NL, :], ACT.Exp).then_inc(lx_ok, 1)
                if h % 8 == 5 and h > 8:
                    y_root(h // 8 - 1)
            y_root(SSM_G - 1)
            out_take(1, 16, yT, lambda k: V_OD + k)
            moe(1, 3)

        @block.gpsimd
        def _(pool):
            g = nc.gpsimd
            ch = Chain(pool, pch)
            for l in range(2):
                pool.dma_start(wr[:, l, :, 0:4], A["moe_wg"][l].rearrange("(k p) n -> p k n", p=P)).then_inc(in_small, 16)
                pool.dma_start(wr[:, l, :, 4:36], A["moe_we"][l].rearrange("(k p) n -> p k n", p=P)).then_inc(in_small, 16)
                pool.dma_start(br[:, l, 0:4], A["moe_bg"][l:l + 1, :].to_broadcast([P, 4])).then_inc(in_rb, 16)
                pool.dma_start(br[:, l, 4:36], A["moe_be"][l:l + 1, :].to_broadcast([P, 32])).then_inc(in_rb, 16)
            pool.wait_ge(b_ok, 1)
            pool.wait_ge(rot_ps, 4)
            for v in range(1, 9):
                if v >= 3:
                    pool.wait_ge(lv_x, v - 2)
                b_, e_ = halves(bb[:, :, :], v), halves(ee[:, v % 2, :, :], v)
                ref = b_[:, :, 0, half(v) - 1:half(v)].to_broadcast([P, b_.shape[1], half(v)])
                g.tensor_tensor(e_[:, :, 0, :], ref, b_[:, :, 0, :], ALU.subtract)
                g.tensor_tensor(e_[:, :, 1, :], b_[:, :, 1, :], ref, ALU.subtract).then_inc(ex_in, 1)

        @block.vector
        def _(dve):
            v_ = nc.vector
            ch = Chain(dve, dch)
            tt, ts, stt = v_.tensor_tensor, v_.tensor_scalar, v_.scalar_tensor_tensor
            bc = lambda a, shape: a.to_broadcast(shape)

            def newton(y, y0, var, tmp):
                ch.link(tt(tmp, y0, y0, ALU.mult))
                ch.link(tt(tmp, tmp, var, ALU.mult))
                ch.link(ts(tmp, tmp, -0.5, 1.5, ALU.mult, ALU.add))
                ch.link(tt(y, y0, tmp, ALU.mult))

            def norm(n, t):
                v_.tensor_tensor_reduce(out=xn[:, t, :], in0=x[:, t, :], in1=x[:, t, :], scale=1.0, scalar=0.0,
                                        op0=ALU.mult, op1=ALU.add, accum_out=st[:, t:t + 1]).then_inc(sq_ok, 1)
                dve.wait_ge(sq_ok, 2 * n + t + 1)
                ts(st[:, 2 + t:3 + t], st[:, t:t + 1], 1.0 / D, EPS, ALU.mult, ALU.add).then_inc(var_ok, 1)

            def norm_end(n, t):
                dve.wait_ge(var_ok, 2 * n + t + 1)
                dve.wait_ge(root_ok, 2 * n + t + 1)
                newton(st[:, 8 + t:9 + t], st[:, 6 + t:7 + t], st[:, 2 + t:3 + t], st[:, 10 + t:11 + t])
                ts(xn[:, t, :], x[:, t, :], st[:, 8 + t:9 + t], None, ALU.mult).then_inc(xn_ok, 1)

            def norm_take(n, g0):
                for b in (0, 2):
                    dve.wait_ge(hT_ps, 4 * n + b + 1)
                    for k in (2 * b, 2 * b + 1):
                        ts(hT[:, k, :], bank[b][:, 256 * (k % 2):256 * (k % 2) + 256], vT[:, g0 + k:g0 + k + 1], None, ALU.mult).then_inc(hT_v, 1)

            def residual(n, ready):
                for t in range(NT):
                    dve.wait_ge(ready, t + 1)
                    for h in range(2):
                        tt(x[:, t, 512 * h:512 * h + 512], x[:, t, 512 * h:512 * h + 512], bank[2 * t + h][:, :], ALU.add).then_inc(x_new, 1)
                    if n < 3:
                        dve.wait_ge(x_new, 4 * n + 2 * t + 2)
                        norm(n + 1, t)
                for t in range(NT if n < 3 else 0):
                    norm_end(n + 1, t)

            v_.memset(zeros[:, :], 0.0)
            v_.memset(ones[:, :], 1.0)
            ch.put(v_.memset(aT[:, :, :, :], 0.0))
            for t in range(NT):
                dve.wait_ge(in_x[t], 16)
                norm(0, t)
            for t in range(NT):
                norm_end(0, t)
            dve.wait_ge(vec_ps, 1)
            v_.tensor_copy(vT[:, 0:180], bank[7][:, 0:180]).then_inc(vec_ok, 1)
            dve.wait_ge(vec_ok, 1)
            l0, l1 = vT[:, V_LB:V_LB + 4], vT[:, V_LB + 4:V_LB + 8]
            ch.link(tt(lbv[:, 16:20], l0, l1, ALU.max))
            ch.put(tt(lbv[:, 0:4], l0, lbv[:, 16:20], ALU.subtract))
            tt(lbv[:, 4:8], l1, lbv[:, 16:20], ALU.subtract).then_inc(lb_in, 1)
            norm_take(0, V_MIX)
            dve.wait_ge(lb_ex, 1)
            ch.link(tt(lbv[:, 20:24], lbv[:, 8:12], lbv[:, 12:16], ALU.add))
            ch.link(v_.reciprocal(lbv[:, 24:28], lbv[:, 20:24]))
            ch.link(tt(lbv[:, 28:32], lbv[:, 8:12], lbv[:, 24:28], ALU.mult))
            ch.link(ts(lbv[:, 32:36], lbv[:, 28:32], -1.0, 1.0, ALU.mult, ALU.add))

            dve.wait_ge(e_out, 3)
            dve.wait_ge(in_even, 32)
            dve.wait_ge(in_con, 16)
            dve.wait_ge(in_lvl, 16)
            sq = ro[:, :, 0:10, :]
            for t in range(NT):
                ch.put(tt(ro[:, t, 0:10, :], rb[:, t, 0:10, :], rb[:, t, 0:10, :], ALU.mult))
            ch.wait()
            ch.link(v_.tensor_reduce(st[:, 16:36].rearrange("p (a h) -> p a h", a=2), sq, AX.X, ALU.add))
            ts(st[:, 16:36], st[:, 16:36], 1.0 / 64, EPS, ALU.mult, ALU.add).then_inc(qk_var, 1)
            dve.wait_ge(qk_root, 1)
            dve.wait_ge(qk_var, 1)
            rs = rt[:, 0, 0:20]
            newton(rs, st[:, 36:56], st[:, 16:36], rt[:, 1, 0:20])
            for t in range(NT):
                h10 = rb[:, t, 0:10, :]
                ch.link(tt(h10, h10, bc(rs[:, 10 * t:10 * t + 10].unsqueeze(2), [P, 10, 64]), ALU.mult))
                ch.put(tt(rb[:, t, 0:8, :], rb[:, t, 0:8, :], bc(qkn[:, 0:1, :], [P, 8, 64]), ALU.mult))
                ch.link(tt(rb[:, t, 8:10, :], rb[:, t, 8:10, :], bc(qkn[:, 1:2, :], [P, 2, 64]), ALU.mult))
            for t in range(NT):
                a1, a2 = rb[:, t, :, 0:32], rb[:, t, :, 32:64]
                cos, sin = bc(cs[:, t:t + 1, 0:32], [P, 16, 32]), bc(cs[:, t:t + 1, 32:64], [P, 16, 32])
                r = lambda n: rt[:, n, :].rearrange("p (h d) -> p h d", h=16)
                ch.put(tt(r(0), a1, cos, ALU.mult))
                ch.put(tt(r(1), a2, sin, ALU.mult))
                ch.put(tt(r(2), a2, cos, ALU.mult))
                ch.link(tt(r(3), a1, sin, ALU.mult))
                ch.put(tt(ro[:, t, :, 0:32], r(0), r(1), ALU.subtract))
                ch.wait()
                tt(ro[:, t, :, 32:64], r(2), r(3), ALU.add).then_inc(rot_ok, 1)
                dve.wait_ge(rot_ok, t + 1)
            dve.wait_ge(e_out, 4)
            for h in range(HG):
                last = ts(lb_[:, h, :], lb_[:, h, :], lbv[:, 32 + h:33 + h], lbv[:, 28 + h:29 + h], ALU.mult, ALU.add)
            last.then_inc(f_lin, 1)
            for h in range(HG):
                last = ts(kk[:, h, :], kk[:, h, :], lbv[:, 32 + h:33 + h], None, ALU.mult)
            last.then_inc(k_ok, 1)
            ch.put(ts(iw[:, :, :], iw[:, :, :], 0.125, None, ALU.mult))
            ch.wait()
            for t in range(NT):
                n = P * (t + 1)
                dve.wait_ge(ix_rel, t + 1)
                s_ = sc[:, t, 0:n]
                ch.link(ts(s_, rl[:, 0, 0:n], iw[:, t, 0:1], None, ALU.mult))
                for h in range(1, 4):
                    ch.link(stt(s_, rl[:, h, 0:n], iw[:, t, h:h + 1], s_, ALU.mult, ALU.add))
                tt(wk[:, t, 0:n], s_, adm[:, t, 0:n], ALU.add).then_inc(ix_ok, 1)
            dve.wait_ge(f_log, 1)
            for h in range(HG):
                last = v_.tensor_tensor_scan(bb[:, h, :], ones[:, :], lb_[:, h, :], 0.0, ALU.mult, ALU.add)
            last.then_inc(b_ok, 1)

            def top_keys(t):
                dve.wait_ge(ix_ok, t + 1)
                w = wk[:, t, 0:P * (t + 1)]
                for r in range(TOPK // 8):
                    ch.link(v_.max(mx8[:, t, :], w))
                    ch.link(v_.match_replace(w, mx8[:, t, :], w, GONE))
                ch.link(ts(sc[:, t, 0:P * (t + 1)], w, GONE, NEG, ALU.not_equal, ALU.mult))
            def take_level(v):
                pair = PAIR["level", v]
                dve.wait_ge(lv_ps, v + 1)
                if v == 8:
                    v_.tensor_copy(aX[:, :, :], bank[pair[0]][:, :]).then_inc(lv_ok, 1)
                    return
                for t in range(NT):
                    ins = v_.copy_predicated(aT[:, t, :, :], lvl[:, v:v + 1, :].to_broadcast([P, HG, P]),
                                             bank[pair[t]][:, :].rearrange("p (h t) -> p h t", h=HG))
                ins.then_inc(lv_ok, 1)
                dve.wait_ge(lv_ok, v + 1)

            def mix(v):
                dve.wait_ge(ex_out, v)
                if v == 1:
                    dve.wait_ge(e_out, 5)
                    dve.wait_ge(k_ok, 1)
                if v >= 3:
                    dve.wait_ge(lv_ps, v - 1)
                e_, x_ = halves(ee[:, v % 2, :, :], v), halves(xe[:, v % 2, :, :], v)
                tt(x_[:, :, 0, :], halves(kk[:, :, :], v)[:, :, 0, :], e_[:, :, 0, :], ALU.mult)
                tt(x_[:, :, 1, :], halves(qT[:, :, :], v)[:, :, 1, :], e_[:, :, 1, :], ALU.mult).then_inc(lv_x, 1)

            def score(b):
                t, heads = BATCHES[b]
                n, nh = P * (t + 1), len(heads)
                dve.wait_ge(ql_ps, b + 1)
                for m, h in enumerate(heads):
                    o = m % (nh // 2)
                    ch.put(v_.tensor_tensor_reduce(out=pr[:, n * m:n * m + n], in0=bank[4 + h // 4][:, n * o:n * o + n], in1=sc[:, t, 0:n],
                                                   scale=0.125, scalar=-3.0e38, op0=ALU.add, op1=ALU.max, accum_out=sm[:, b, m:m + 1]))
                ch.wait()
                ts(sm[:, b, 8:8 + nh], sm[:, b, 0:nh], -1.0, None, ALU.mult).then_inc(at_max, 1)

            def value(b):
                t, heads = BATCHES[b]
                nh = len(heads)
                dve.wait_ge(at_exp, b + 1)
                ch.link(v_.reciprocal(sm[:, b, 24:24 + nh], sm[:, b, 16:16 + nh]))
                dve.wait_ge(pv_ps, b + 1)
                dst = xn[:, t, 512:1024].rearrange("p (v h d) -> p v h d", v=2, h=4)[:, :, heads[0]:heads[0] + nh // 2, :]
                tt(dst, bank[4][:, 0:64 * nh].rearrange("p (v h d) -> p v h d", v=2, h=nh // 2),
                   bc(sm[:, b, 24:24 + nh].rearrange("p (v h) -> p v h", v=2).unsqueeze(3), [P, 2, nh // 2, 64]), ALU.mult).then_inc(at_o, 1)

            ov = lb_[:, :, :].rearrange("p h t -> p (h t)").rearrange("p (a n) -> p a n", a=2)

            def hgrn_sum(_):
                for t in range(NT):
                    dve.wait_ge(ho_ps, t + 1)
                    v_.tensor_copy(ov[:, t, :], bank[2 + t][:, :]).then_inc(ov_ok, 1)

            for kind, n in DVE_ORDER:
                {"level": take_level, "mix": mix, "keys": top_keys, "score": score, "value": value, "sum": hgrn_sum}[kind](n)
            sqv = kk[:, :, :].rearrange("p h t -> p (h t)").rearrange("p (a n) -> p a n", a=2)
            dve.wait_ge(ov_ok, 2)
            ch.link(tt(sqv, ov, ov, ALU.mult))
            ch.link(v_.tensor_reduce(st[:, 24:32], sqv.rearrange("p a (h d) -> p (a h) d", h=4), AX.X, ALU.add))
            ts(st[:, 16:24], st[:, 24:32], 1.0 / P, EPS, ALU.mult, ALU.add).then_inc(ho_var, 1)
            dve.wait_ge(e_out, 7)
            ch.link(tt(ov, ov, gg[:, :, :], ALU.mult))
            dve.wait_ge(ho_root, 1)
            newton(st[:, 44:52], st[:, 36:44], st[:, 16:24], st[:, 52:60])
            for t in range(NT):
                ins = tt(xn[:, t, 0:512].rearrange("p (h d) -> p h d", h=4), ov[:, t, :].rearrange("p (h d) -> p h d", h=4),
                         bc(st[:, 44 + 4 * t:48 + 4 * t].unsqueeze(2), [P, 4, P]), ALU.mult)
            ins.then_inc(on_ok, 1)
            residual(0, mo_acc[0])

            def moe(layer, n):
                m = M[layer]
                for a in (gp[:, :, 0:8], gp[:, :, 12:16], ep[:, :, 0:8], m8[:, 1, :, :], m8[:, 3, :, :]):
                    ch.put(v_.memset(a, NEG))
                norm_take(n, V_FFN + 8 * layer)
                dve.wait_ge(m["rt_ps"], 1)
                dve.wait_ge(in_rb, 64)
                ch.wait()
                for t in range(NT):
                    ch.put(tt(lg[:, t, :], bank[4][:, 36 * t:36 * t + 36], br[:, layer, :], ALU.add))
                ch.wait()
                ch.link(v_.tensor_copy(gp[:, :, 8:12], lg[:, :, 0:4]))
                for t in range(NT):
                    ch.link(v_.max(m8[:, 0, t, :], gp[:, t, :]))
                    ch.link(v_.tensor_copy(m8[:, 1, t, 0:1], m8[:, 0, t, 0:1]))
                    ch.link(v_.match_replace(gr[:, t, :], m8[:, 1, t, :], gp[:, t, :], MARK))
                ch.link(ts(g4[:, 0, :, :], gr[:, :, 8:12], MARK, None, ALU.is_equal))
                ch.link(ts(g4[:, 1, :, :], g4[:, 0, :, :], 1.0, -NEG, ALU.subtract, ALU.mult))
                for t in range(NT):
                    el = lg[:, t, 4:36].rearrange("p (g e) -> p g e", g=4)
                    e_ = ep[:, t, 8:40].rearrange("p (g e) -> p g e", g=4)
                    ch.link(tt(e_, el, bc(g4[:, 0, t, :].unsqueeze(2), [P, 4, 8]), ALU.mult))
                    ch.link(tt(e_, e_, bc(g4[:, 1, t, :].unsqueeze(2), [P, 4, 8]), ALU.add))
                    ch.link(v_.max(m8[:, 2, t, :], ep[:, t, :]))
                    ch.link(v_.tensor_copy(m8[:, 3, t, 0:2], m8[:, 2, t, 0:2]))
                    ch.link(v_.match_replace(er[:, t, :], m8[:, 3, t, :], ep[:, t, :], MARK))
                    ch.put(ts(arg[:, t, 0:4], lg[:, t, 0:4], m8[:, 0, t, 0:1], None, ALU.subtract))
                    ts(arg[:, t, 4:36], ep[:, t, 8:40], m8[:, 2, t, 0:1], None, ALU.subtract).then_inc(m["rt_in"], 1)
                ts(s32[:, 0, :, :], er[:, :, 8:40], MARK, None, ALU.is_equal).then_inc(m["rt_sel"], 1)
                dve.wait_ge(m["rt_sel"], 1)
                dve.wait_ge(m["rt_ex"], 1)
                red = lambda o, a: ch.link(v_.tensor_reduce(o, a, AX.X, ALU.add))
                red(st[:, 16:18], arg[:, :, 0:4])
                red(st[:, 18:20], arg[:, :, 4:36])
                ch.link(v_.reciprocal(st[:, 20:24], st[:, 16:20]))
                for t in range(NT):
                    ch.put(stt(s32[:, 1, t, :], arg[:, t, 4:36], st[:, 22 + t:23 + t], s32[:, 0, t, :], ALU.mult, ALU.mult))
                ch.wait()
                red(st[:, 24:26], s32[:, 1, :, :])
                ch.link(v_.reciprocal(st[:, 26:28], st[:, 24:26]))
                ch.link(tt(st[:, 28:30], st[:, 26:28], st[:, 20:22], ALU.mult))
                for t in range(NT):
                    ch.put(ts(s32[:, 2, t, :], s32[:, 1, t, :], st[:, 28 + t:29 + t], None, ALU.mult))
                ch.wait()
                dve.wait_ge(m["rk_ps"], 1)
                rk = s32[:, 3, :, :]
                ch.link(stt(rk, bank[5][:, 0:64].rearrange("p (a e) -> p a e", a=2), 1.0, s32[:, 0, :, :], ALU.add, ALU.mult))
                ch.link(v_.tensor_reduce(rr[:, 0:1], bank[5][:, 64:96], AX.X, ALU.max))
                ch.link(ts(rr[:, 8:16], thr, rr[:, 0:1], None, ALU.is_lt))
                ch.link(v_.tensor_reduce(rr[:, 1:2], rr[:, 8:16], AX.X, ALU.add))
                ch.link(ts(rr[:, 2:3], rr[:, 1:2], float(NGROUPS), -1.0, ALU.mult, ALU.add))
                ch.put(v_.tensor_copy(rounds[:, layer:layer + 1], rr[:, 1:2]))
                ch.put(v_.tensor_copy(rounds[:, 2 + layer:3 + layer], rr[:, 2:3]))
                step = lambda tab, r: tab[:, NGROUPS * r:NGROUPS * (r + 1), :].rearrange("p g (a e) -> p a g e", a=2)
                by_group = lambda a: a.rearrange("p a (g e) -> p a g e", g=NGROUPS)
                for r in range(ROUNDS):
                    ch.put(ts(step(rtab, r), by_group(rk), -1.0 - CAP * r, None, ALU.add))
                    last = v_.tensor_copy(step(gtab, r), by_group(s32[:, 2, :, :]))
                last.then_inc(m["rt_ok"], 1)
                dve.wait_ge(m["rt_ok"], 1)
                ch.wait()
                nr = dve.value_load(rounds[0:1, layer:layer + 1], min_val=1, max_val=ROUNDS)
                with dve.Fori(0, nr * NGROUPS) as i:
                    tt(sel[:, :, :], bc(rtab[:, bass.ds(i, 1), :].rearrange("p a e -> p (a e)").unsqueeze(2), [P, 8, CAP]),
                       bc(iota.unsqueeze(1), [P, 8, CAP]), ALU.is_equal).then_inc(m["s_ok"], 1)
                    dve.wait_ge(m["s_ok"], i + 1)
                    for t in range(NT):
                        gt = gtab[:, bass.ds(i, 1), 4 * t:4 * t + 4].rearrange("p a e -> p (a e)").unsqueeze(2).unsqueeze(3)
                        ins = tt(pg[:, t, :, :, :], bc(sel[:, 4 * t:4 * t + 4, :].unsqueeze(2), [P, GROUP, 4, CAP]), bc(gt, [P, GROUP, 4, CAP]), ALU.mult)
                    ins.then_inc(m["pg_ok"], 1)
                    dve.wait_ge(m["ga_ps"], i + 1)
                    for b in range(2):
                        g0 = V_FFN + 8 * layer + 4 * b
                        tt(xT[:, 4 * b:4 * b + 4, :], bank[6 + b][:, :].rearrange("p (k c) -> p k c", k=4),
                           bc(vT[:, g0:g0 + 4].unsqueeze(2), [P, 4, P]), ALU.mult).then_inc(m["xt_ok"], 1)

                    def gate(e):
                        dve.wait_ge(m["si_ok"], i * 4 + e + 1)
                        tt(he[:, e % 2, :], sg[:, e % 2, :], bank[4 + e % 2][:, P:2 * P], ALU.mult).then_inc(m["he_ok"], 1)

                    def turned(e):
                        dve.wait_ge(m["ht_ps"], i * 4 + e + 1)
                        v_.tensor_copy(heT[:, e % 2, :], bank[6][:, 0:P]).then_inc(m["ht_ok"], 1)

                    def take(e):
                        dve.wait_ge(used[layer], i * STEP_UNITS + finished(e, 2))
                        if e >= 2:
                            dve.wait_ge(m["scat"], i * 4 + e - 1)
                        v_.tensor_copy(ys[:, e % 2, 0:512], bank[6][:, :]).then_inc(m["yv_ok"], 1)

                    gate(0); turned(0); gate(1); take(0)
                    turned(1); gate(2); take(1)
                    turned(2); gate(3); take(2)
                    turned(3); take(3)
                residual(n, m["acc"])

            moe(0, 1)

            ch.put(v_.memset(cumT[:, :], 0.0))
            for s_ in range(3):
                ch.put(v_.memset(cv[:, s_, 0:3], 0.0))
            norm_take(2, V_MIX + 8)
            dve.wait_ge(in_odd, 48)
            dve.wait_ge(mixed[1], 1)
            ch.link(ts(dtmp[:, 0, :], bank[4][0:32, 0:S], dts[:, 0:1], None, ALU.add))
            ch.link(ts(dtmp[:, 5, :], dtmp[:, 0, :], -1.0, None, ALU.mult))
            ts(dtmp[:, 6, :], dtmp[:, 0, :], 0.0, None, ALU.max).then_inc(al_in, 1)
            tt(dtmp[:, 1, :], dtmp[:, 0, :], dtmp[:, 5, :], ALU.min).then_inc(dt_b, 1)
            dve.wait_ge(al_ex, 1)
            ch.link(ts(dts[:, 3:4], dts[:, 2:3], -1.0, None, ALU.mult))
            dve.wait_ge(dt_e, 1)
            ts(dtmp[:, 3, :], dtmp[:, 2, :], 1.0, None, ALU.add).then_inc(dt_b, 1)
            dve.wait_ge(dt_b, 2)
            ch.link(ts(dtmp[:, 5, :], dtmp[:, 3, :], 1.0, None, ALU.subtract))
            ch.link(tt(dtmp[:, 5, :], dtmp[:, 2, :], dtmp[:, 5, :], ALU.subtract))
            ch.link(v_.reciprocal(dtmp[:, 7, :], dtmp[:, 3, :]))
            ch.link(tt(dtmp[:, 5, :], dtmp[:, 5, :], dtmp[:, 7, :], ALU.mult))
            dve.wait_ge(al_in, 1)
            ch.link(tt(dtmp[:, 6, :], dtmp[:, 6, :], dtmp[:, 5, :], ALU.add))
            dve.wait_ge(dt_l, 1)
            ch.link(tt(dtT[:, :], dtmp[:, 6, :], dtmp[:, 4, :], ALU.add))
            ch.link(ts(dtmp[:, 7, :], dtT[:, :], dts[:, 3:4], None, ALU.mult))
            v_.tensor_tensor_scan(cumT[0:32, :], ones[0:32, :], dtmp[:, 7, :], 0.0, ALU.mult, ALU.add).then_inc(dt_ok, 1)

            def conv(c):
                dve.wait_ge(raw_in, c + 1)
                if c >= 3:
                    dve.wait_ge(act_ok, c - 2)
                src, dst = cv[:, c % 3, :], ca[:, c % 3, :]
                w = lambda j: vT[:, V_CW + 24 * j + ct(c):V_CW + 24 * j + ct(c) + 1]
                ch.link(ts(dst, src[:, 3:259], w(3), vT[:, V_CB + ct(c):V_CB + ct(c) + 1], ALU.mult, ALU.add))
                ch.link(stt(dst, src[:, 2:258], w(2), dst, ALU.mult, ALU.add))
                ch.link(stt(dst, src[:, 1:257], w(1), dst, ALU.mult, ALU.add))
                stt(dst, src[:, 0:256], w(0), dst, ALU.mult, ALU.add).then_inc(cv_ok, 1)

            def ct(c):
                return 16 + c if c < 8 else c - 8

            def xs_take(u):
                dve.wait_ge(xs_ps, u + 1)
                pb = (4, 5) if u % 2 == 0 else (6, 7)
                for t in range(NT):
                    src = bank[pb[t]][:, :].rearrange("p (h d) -> p h d", h=8)
                    ch.put(tt(xd[:, t, 512 * u:512 * u + 512].rearrange("p (h d) -> p h d", h=8), src,
                              bc(dnat[:, t, 0, 8 * u:8 * u + 8].unsqueeze(2), [P, 8, 64]), ALU.mult))
                    ch.wait()
                    tt(xs[:, t, 512 * u:512 * u + 512].rearrange("p (h d) -> p h d", h=8), src,
                       bc(dsk[:, 8 * u:8 * u + 8].unsqueeze(2), [P, 8, 64]), ALU.mult).then_inc(xs_ok, 1)

            for c in range(24):
                conv(c)
                if c == 3:
                    dve.wait_ge(dn_ps, 1)
                    v_.tensor_copy(dnat[:, :, :, :], bank[5][:, 0:128].rearrange("p (a w h) -> p a w h", a=2, w=2)).then_inc(dn_ok, 1)
                    dve.wait_ge(dn_ok, 1)
                if c in (15, 19, 23):
                    xs_take(c // 4 - 3)
            xs_take(3)
            dve.wait_ge(xs_ok, 8)
            for g in range(SSM_G):
                dve.wait_ge(cb_ps, g + 1)
                tt(cbm[:, g, :], bank[4 + g][:, 0:384], mask3, ALU.mult).then_inc(cb_ok, 1)
            dve.wait_ge(cb_ok, 4)

            def decay(h):
                dve.wait_ge(cu_ps, h + 1)
                if h >= NL:
                    dve.wait_ge(yy_ps, h - NL + 1)
                l_, b = lw[:, h % NL, :], bank[4 + h % 4]
                ch.put(ts(l_[:, 0:S], b[:, 0:S], dnat[:, 0, 1, h:h + 1], 0.0, ALU.subtract, ALU.min))
                ch.wait()
                ts(l_[:, S:S + P], b[:, P:S], dnat[:, 1, 1, h:h + 1], 0.0, ALU.subtract, ALU.min).then_inc(cu_ok, 1)

            def weigh(h):
                dve.wait_ge(lx_ok, h + 1)
                tt(lw[:, h % NL, :], lw[:, h % NL, :], cbm[:, h // 8, :], ALU.mult).then_inc(lm_ok, 1)

            def y_take(g):
                dve.wait_ge(yy_ps, 8 * g + 8)
                for t in range(NT):
                    yv = xs[:, t, 512 * g:512 * g + 512]
                    tt(yv, yv, bank[2 * (g % 2) + t][:, :], ALU.add).then_inc(yy_ok, 1)
                dve.wait_ge(yy_ok, 2 * g + 2)
                yv = xs[:, :, 512 * g:512 * g + 512]
                ch.link(tt(yv, yv, zz[:, :, 512 * g:512 * g + 512], ALU.mult))
                for t in range(NT):
                    ch.put(v_.tensor_tensor_reduce(out=zz[:, t, 512 * g:512 * g + 512], in0=xs[:, t, 512 * g:512 * g + 512],
                                                   in1=xs[:, t, 512 * g:512 * g + 512], scale=1.0, scalar=0.0, op0=ALU.mult, op1=ALU.add,
                                                   accum_out=st[:, 24 + 2 * g + t:25 + 2 * g + t]))
                ch.wait()
                ts(st[:, 16 + 2 * g:18 + 2 * g], st[:, 24 + 2 * g:26 + 2 * g], 1.0 / 512, EPS, ALU.mult, ALU.add).then_inc(o_var, 1)

            def y_norm(g):
                a = 2 * g
                dve.wait_ge(o_root, g + 1)
                newton(st[:, 44 + a:46 + a], st[:, 36 + a:38 + a], st[:, 16 + a:18 + a], st[:, 52 + a:54 + a])
                for t in range(NT):
                    yv = xs[:, t, 512 * g:512 * g + 512]
                    ts(yv, yv, st[:, 44 + a + t:45 + a + t], None, ALU.mult).then_inc(yn_ok, 1)

            for h in range(AHEAD):
                decay(h)
            for h in range(SSM_H):
                weigh(h)
                if h + AHEAD < SSM_H:
                    decay(h + AHEAD)
                if h % 8 == 1 and h > 8:
                    y_take(h // 8 - 1)
                if h % 8 == 4 and h > 8:
                    y_norm(h // 8 - 1)
            y_take(SSM_G - 1)
            y_norm(SSM_G - 1)
            residual(2, mo_acc[1])
            moe(1, 3)


_INPUTS = ["x", "mix_norm", "ffn_norm", "ev_w_in", "hg_lb_logits", "hg_out_norm", "at_q_norm", "at_k_norm", "ev_w_out", "od_w_in",
           "od_conv_w", "od_conv_b", "od_dt_bias", "od_A_log", "od_D", "od_out_norm", "od_w_out", "moe_wg", "moe_bg", "moe_we",
           "moe_be", "moe_w1", "moe_w3", "moe_w2"]


def constants():
    p = np.arange(P)
    con = np.zeros((P, C_END), np.float32)
    con[:, C_ID:C_ID + P] = np.eye(P)
    upto = (p[:, None] <= p[None, :]).astype(np.float32)
    con[:, C_M3:C_M3 + 384] = np.concatenate([upto, np.ones((P, P)), upto], 1)
    con[:, C_STRICT:C_STRICT + P] = p[:, None] < p[None, :]
    for t in range(NT):
        q_chunk, k_chunk = (P * t + p) // 64, np.arange(S) // 64
        con[:, C_ADM + S * t:C_ADM + S * (t + 1)] = np.where(k_chunk[None, :] <= q_chunk[:, None], 0.0, NEG)
        inv = np.exp(np.float32(-np.log(10000.0)) * np.arange(32, dtype=np.float32) / np.float32(32)).astype(np.float32)
        ang = (P * t + p).astype(np.float32)[:, None] * inv[None, :]
        con[:, C_CS + 64 * t:C_CS + 64 * t + 32] = np.cos(ang)
        con[:, C_CS + 64 * t + 32:C_CS + 64 * t + 64] = np.sin(ang)
    con[:, C_IOTA:C_IOTA + 32] = np.arange(32)
    con[:, C_THR:C_THR + 8] = CAP * np.arange(8)
    lvl = np.zeros((P, 8, P), np.int32)
    lvl[:, 0, :] = np.eye(P)
    for v in range(1, 8):
        half = 64 >> (v - 1)
        s_, t_ = p[:, None], p[None, :]
        lvl[:, v, :] = (s_ // (2 * half) == t_ // (2 * half)) & (s_ // half % 2 == 0) & (t_ // half % 2 == 1)
    return con, lvl


def kernel(**inputs):
    import concourse.bacc as bacc
    from concourse import mybir
    from concourse.bass_utils import run_bass_kernel_spmd

    nc = bacc.Bacc("TRN2", target_bir_lowering=False, num_devices=1)
    con, lvl = constants()
    arrays, A = {}, {}
    for name, a in [(n, inputs[n]) for n in _INPUTS] + [("con", con), ("lvl", lvl)]:
        a = np.ascontiguousarray(a)
        arrays["in_" + name] = a
        A[name] = nc.dram_tensor("in_" + name, a.shape, mybir.dt.from_np(a.dtype), kind="ExternalInput").ap()
    out = nc.dram_tensor("out", (1, S, D), mybir.dt.float32, kind="ExternalOutput").ap()
    build(nc, A, out)
    r = run_bass_kernel_spmd(nc, [arrays], core_ids=[0])
    return r.results[0]["out"]
```

```python
import numpy as np

D, S, P = 1024, 256, 128
KT = D // P
NT = S // P
RING = 6
UNIT = 4096
MOE_WORDS = 7920
EPS = 1e-6
NEG = -1.0e30
GONE = -3.0e38
MARK = 3.0e38
HG = 4
TOPK = 64
EXPERTS, GROUP, CAP, FF = 32, 4, 32, 512
NGROUPS = EXPERTS // GROUP
ROUNDS = S // CAP
MIX_UNITS = (9, 15)
STEP_UNITS = 3 * GROUP
SSM_H, SSM_G = 32, 4
NL, AHEAD = 5, 3
ORDER = [(0, 0), (0, 1), (1, 0), (0, 2), (1, 1), (2, 0), (1, 2), (2, 1), (3, 0), (2, 2), (3, 1), (3, 2)]
FIRST = [(0, 0), (0, 1), (0, 2), (1, 2), (1, 0), (1, 1), (2, 2), (3, 2), (2, 0), (2, 1), (3, 0), (3, 1)]
C_ID, C_M3, C_STRICT, C_ADM, C_CS, C_IOTA, C_THR = 0, 128, 512, 640, 1152, 1280, 1312
C_END = 1328
V_MIX, V_FFN, V_HG, V_LB, V_OD, V_CB, V_CW = 0, 16, 32, 36, 44, 60, 84
E_Q, E_F, E_I, E_G, E_AQ, E_AK, E_AV, E_IQ, E_IK = 0, 512, 1024, 1536, 2048, 2560, 2688, 2816, 3072


BATCHES = [(0, list(range(8))), (1, [0, 1, 4, 5]), (1, [2, 3, 6, 7])]
PE_ORDER = [("level", 0), ("unit", 5), ("score", 0), ("level", 1), ("level", 2), ("unit", 6), ("turn", 0), ("value", 0),
            ("score", 1), ("level", 3), ("level", 4), ("level", 5), ("turn", 1), ("value", 1),
            ("score", 2), ("level", 6), ("level", 7), ("level", 8), ("turn", 2), ("sum", 0), ("value", 2)]
DVE_ORDER = [("level", 0), ("keys", 0), ("mix", 1), ("mix", 2), ("score", 0), ("level", 1), ("mix", 3), ("level", 2), ("mix", 4),
             ("keys", 1), ("value", 0), ("score", 1), ("level", 3), ("mix", 5), ("level", 4), ("mix", 6), ("level", 5), ("mix", 7),
             ("value", 1), ("score", 2), ("level", 6), ("mix", 8), ("level", 7), ("level", 8), ("sum", 0), ("value", 2)]
ACT_ORDER = [("level", 1), ("unit", 5), ("level", 2), ("score", 0), ("level", 3), ("level", 4), ("unit", 6), ("turn", 0),
             ("score", 1), ("level", 5), ("level", 6), ("level", 7), ("turn", 1), ("score", 2), ("level", 8), ("turn", 2)]
OUT_BLOCKS = [[1, 0], [0, 1, 2, 3]]
PAIRED = [("unit", 3), ("unit", 4)] + [x for x in PE_ORDER if x[0] in ("level", "unit")]
PAIR = {x: ((2, 3), (0, 1))[n % 2] for n, x in enumerate(PAIRED)}

XS_BANKS = [(4, 5), (6, 7), (4, 5), (0, 1)]
CB_BANKS = (4, 5, 2, 3)
Z_STEPS, Z_FIRST = 2048 // 512 * NT * KT, 10


def z_head(j):
    return max((KT * (j + 1) - Z_FIRST + 1) // 2 - 1 + AHEAD, 0)


def finished(expert, part):
    return ORDER.index((expert, part)) + 1


def slot_of(layer, unit):
    return (unit + 3 * layer) % RING


def build(nc, A, out):
    import concourse.bass as bass
    from concourse import mybir
    from contextlib import ExitStack

    f32, i32 = mybir.dt.float32, mybir.dt.int32
    ALU, ACT, AX = mybir.AluOpType, mybir.ActivationFunctionType, mybir.AxisListType
    ctx = ExitStack()
    with ctx:
        def sb(name, shape, dt=f32, c=ctx):
            return c.enter_context(nc.sbuf_tensor(name, shape, dt))

        def sem(name):
            return ctx.enter_context(nc.semaphore(name))

        class Chain:

            def __init__(self, eng, s, base=0):
                self.eng, self.s, self.base, self.n = eng, s, base, 0

            def put(self, ins):
                self.n += 1
                ins.then_inc(self.s, 1)

            def wait(self):
                self.eng.wait_ge(self.s, self.base + self.n)

            def link(self, ins):
                self.put(ins)
                self.wait()

        ring = sb("ring", [P, RING, UNIT])
        con = sb("con", [P, C_END])
        lvl = sb("lvl", [P, 8, P], i32)
        ones = sb("ones", [P, 256])
        zeros = sb("zeros", [P, 256])
        zero_b = zeros[:, :].bitcast(mybir.dt.bfloat16)
        x = sb("x", [P, NT, D])
        xn = sb("xn", [P, NT, D])
        hT = sb("hT", [P, KT, S])
        vrow = sb("vrow", [96, 256])
        vT = sb("vT", [P, 184])
        wr = sb("wr", [P, 2, KT, 36])
        br = sb("br", [P, 2, 36])
        st = sb("st", [P, 64])
        rounds = sb("rounds", [P, 4], i32)
        ident = con[:, C_ID:C_ID + P]
        mask3 = con[:, C_M3:C_M3 + 384]
        strict = con[:, C_STRICT:C_STRICT + P]
        adm = con[:, C_ADM:C_ADM + 512].rearrange("p (a s) -> p a s", a=2)
        cs = con[:, C_CS:C_CS + 128].rearrange("p (a s) -> p a s", a=2)
        iota = con[:, C_IOTA:C_IOTA + 32]
        thr = con[:, C_THR:C_THR + 8]
        thr1 = con[:, C_THR + 8:C_THR + 16]
        bank = [ctx.enter_context(nc.psum_tensor(f"bank{i}", [P, 512], f32)) for i in range(8)]

        def half(v):
            return P if v == 8 else 64 >> (v - 1)

        def halves(a, v):
            return a.rearrange("p h (n w t) -> p (h n) w t", w=2, t=half(v))

        with ExitStack() as c:
            rb = sb("rb", [P, NT, 16, 64], c=c)
            ro = sb("ro", [P, NT, 16, 64], c=c)
            rt = sb("rt", [P, 4, 512], c=c)
            tt_ = sb("tt_", [P, 8, S], c=c)
            av = sb("av", [P, NT, P], c=c)
            iw = sb("iw", [P, NT, 4], c=c)
            sc = sb("sc", [P, NT, S], c=c)
            wk = sb("wk", [P, NT, S], c=c)
            mx8 = sb("mx8", [P, NT, 8], c=c)
            pr = sb("pr", [P, 1024], c=c)
            sm = sb("sm", [P, 3, 32], c=c)
            qT = sb("qT", [P, HG, S], c=c)
            kk = sb("kk", [P, HG, S], c=c)
            lb_ = sb("lb_", [P, HG, S], c=c)
            bb = sb("bb", [P, HG, S], c=c)
            vv = sb("vv", [P, NT, 512], c=c)
            gg = sb("gg", [P, NT, 512], c=c)
            aT = sb("aT", [P, NT, HG, P], c=c)
            aX = sb("aX", [P, HG, P], c=c)
            lbv = sb("lbv", [P, 40], c=c)
            qkn = sb("qkn", [P, 2, 64], c=c)
        xe = rb[:, :, :, :].rearrange("p a h d -> p (a h d)").rearrange("p (n h t) -> p n h t", n=2, h=HG)
        ee = ro[:, :, :, :].rearrange("p a h d -> p (a h d)").rearrange("p (n h t) -> p n h t", n=2, h=HG)
        pT = rt[:, 0:2, :].rearrange("p a n -> p (a n)")
        rl = rt[:, :, 0:256]
        with ExitStack() as c:
            zz = sb("zz", [P, NT, 2048], c=c)
            xs = sb("xs", [P, NT, 2048], c=c)
            xd = sb("xd", [P, NT, 2048], c=c)
            bT = sb("bT", [P, SSM_G, S], c=c)
            cT = sb("cT", [P, SSM_G, S], c=c)
            cbm = sb("cbm", [P, SSM_G, 3 * P], c=c)
            cv = sb("cv", [P, 3, 260], c=c)
            ca = sb("ca", [P, 3, S], c=c)
            dts = sb("dts", [32, 8], c=c)
            dnat = sb("dnat", [P, NT, 2, 32], c=c)
            dsk = sb("dsk", [P, 32], c=c)
            cumT = sb("cumT", [P, S], c=c)
            dtT = sb("dtT", [32, S], c=c)
        dtmp = zz[0:32, 0, :].rearrange("p (n t) -> p n t", n=8)
        xsT = xn[:, :, :].rearrange("p a d -> p (a d)").rearrange("p (n t) -> p n t", n=8)
        lw = xn[:, :, :].rearrange("p a d -> p (a d)")[:, 0:384 * NL].rearrange("p (n t) -> p n t", n=NL)
        yT = xd[:, :, :].rearrange("p a d -> p (a d)").rearrange("p (k t) -> p k t", k=16)
        with ExitStack() as c:
            extra1 = sb("extra1", [P, UNIT], c=c)
            sel = sb("sel", [P, 8, CAP], c=c)
            pg = sb("pg", [P, NT, GROUP, 4, CAP], c=c)
            xT = sb("xT", [P, KT, P], c=c)
            pgT = sb("pgT", [P, GROUP, NT, P], c=c)
            sg = sb("sg", [P, 2, P], c=c)
            he = sb("he", [P, 2, P], c=c)
            heT = sb("heT", [P, 2, P], c=c)
            ys = sb("ys", [P, 2, D], c=c)
            rtab = sb("rtab", [P, ROUNDS * NGROUPS, 8], c=c)
            gtab = sb("gtab", [P, ROUNDS * NGROUPS, 8], c=c)
            lg = sb("lg", [P, NT, 36], c=c)
            gp = sb("gp", [P, NT, 16], c=c)
            gr = sb("gr", [P, NT, 16], c=c)
            ep = sb("ep", [P, NT, 40], c=c)
            er = sb("er", [P, NT, 40], c=c)
            m8 = sb("m8", [P, 4, NT, 8], c=c)
            arg = sb("arg", [P, NT, 36], c=c)
            g4 = sb("g4", [P, 4, NT, 4], c=c)
            s32 = sb("s32", [P, 4, NT, 32], c=c)
            rr = sb("rr", [P, 32], c=c)
            sb("pad", [P, 2 * UNIT - MOE_WORDS], c=c)
            extra0 = sb("extra0", [P, UNIT], c=c)

        in_con, in_lvl, in_vec = sem("in_con"), sem("in_lvl"), sem("in_vec")
        in_x = [sem(f"in_x{t}") for t in range(NT)]
        in_small, in_rb, in_even, in_odd, vec_ps, vec_ok = sem("in_small"), sem("in_rb"), sem("in_even"), sem("in_odd"), sem("vec_ps"), sem("vec_ok")
        full = [[sem(f"full{l}_{s}") for s in range(RING + 2)] for l in range(2)]
        mixed = [sem(f"mixed{l}") for l in range(2)]
        used = [sem(f"used{l}") for l in range(2)]
        var_ok, root_ok, xn_ok, hT_ps, hT_v, hT_a = (sem(n) for n in ("var_ok", "root_ok", "xn_ok", "hT_ps", "hT_v", "hT_a"))
        sq_ok, rms_ok = sem("sq_ok"), sem("rms_ok")
        x_new = sem("x_new")
        dch, ach, pch = sem("dch"), sem("ach"), sem("pch")
        e_out = sem("e_out")
        rot_ok, rot_ps, rot_t = sem("rot_ok"), sem("rot_ps"), sem("rot_t")
        ix_ps, ix_rel, ix_ok, lb_in, lb_ex = sem("ix_ps"), sem("ix_rel"), sem("ix_ok"), sem("lb_in"), sem("lb_ex")
        qk_var, qk_root = sem("qk_var"), sem("qk_root")
        ql_ps, at_max, at_exp, at_tps, at_t, pv_ps, at_o = (sem(n) for n in
            ("ql_ps", "at_max", "at_exp", "at_tps", "at_t", "pv_ps", "at_o"))
        f_lin, f_log, k_ok, b_ok = sem("f_lin"), sem("f_log"), sem("k_ok"), sem("b_ok")
        ex_in, ex_out, lv_x, lv_ps, lv_ok = sem("ex_in"), sem("ex_out"), sem("lv_x"), sem("lv_ps"), sem("lv_ok")
        ov_ok, ho_ps, ho_var, ho_root, on_ok = sem("ov_ok"), sem("ho_ps"), sem("ho_var"), sem("ho_root"), sem("on_ok")
        mo_ps = [sem(f"mo_ps{l}") for l in range(2)]
        mo_acc = [sem(f"mo_acc{l}") for l in range(2)]
        mo_t = [sem(f"mo_t{l}") for l in range(2)]
        mp_ok = [sem(f"mp_ok{l}") for l in range(2)]
        dt_b, dt_e, dt_l, dt_ok, dn_ps, dn_ok = (sem(n) for n in ("dt_b", "dt_e", "dt_l", "dt_ok", "dn_ps", "dn_ok"))
        raw_in, cv_ok, act_ok, xs_ps, xs_ok, z_ps, z_ok = (sem(n) for n in ("raw_in", "cv_ok", "act_ok", "xs_ps", "xs_ok", "z_ps", "z_ok"))
        cb_ps, cb_ok, cu_ps, cu_ok, lx_ok, lm_ok, yy_ps, yy_ok = (sem(n) for n in
            ("cb_ps", "cb_ok", "cu_ps", "cu_ok", "lx_ok", "lm_ok", "yy_ps", "yy_ok"))
        o_var, o_root, yn_ok, al_in, al_ex = sem("o_var"), sem("o_root"), sem("yn_ok"), sem("al_in"), sem("al_ex")
        names = ("rt_ps", "rt_in", "rt_ex", "rt_sel", "rk_ps", "rt_ok", "s_ok", "pg_ok", "ga_ps", "xt_ok",
                 "pt_ps", "pt_ok", "si_ok", "he_ok", "ht_ps", "ht_ok", "yv_ok", "ya_ok", "scat", "acc", "lg_ok", "ga_ok", "tab_ok")
        M = [{n: sem(f"{n}{l}") for n in names} for l in range(2)]
        stored = sem("stored")

        w1v = A["moe_w1"].rearrange("l e (k p) f -> l e p k f", p=P)
        w3v = A["moe_w3"].rearrange("l e (k p) f -> l e p k f", p=P)
        w2v = A["moe_w2"].rearrange("l e (k p) n -> l e p k n", p=P)
        evin = A["ev_w_in"][0].rearrange("(k p) n -> p k n", p=P)
        evout = A["ev_w_out"][0].rearrange("(k p) n -> p k n", p=P)
        odin = A["od_w_in"][0].rearrange("(k p) n -> p k n", p=P)
        odout = A["od_w_out"][0].rearrange("(k p) n -> p k n", p=P)
        EVEN = [(E_AK, 512), (E_IK, 68), (E_AQ, 512), (E_F, 512), (E_Q, 512), (E_I, 512), (E_G, 512)]
        ODD = [(5120, 32), (4096, 512), (4608, 512)] + [(2048 + 512 * u, 512) for u in range(4)] + \
              [(512 * u, 512) for u in range(4)]

        def wslot(layer, unit, n):
            return ring[:, slot_of(layer, unit), 0:(UNIT // 512 if n <= 512 else 4) * n].rearrange("p (k n) -> p k n", n=n)

        def full_at(layer, unit):
            return 32 * (unit // RING + 1)

        def moe_slot(layer, e, part):
            if part == 2 and e < 2:
                return RING + e
            return slot_of(layer, MIX_UNITS[layer] + ((2 * e + part) % 4 if part < 2 else 2 + e))

        def moe_memory(layer, e, part):
            slot = moe_slot(layer, e, part)
            return (extra0, extra1)[slot - RING][:, :] if slot >= RING else ring[:, slot, :]

        def moe_full(layer, e, part):
            slot = moe_slot(layer, e, part)
            before = sum(slot_of(layer, v) == slot for v in range(MIX_UNITS[layer]))
            turn = (2 * e + part) // 4 if part < 2 else 0
            return 32 * (before + turn + 1), 64 if part < 2 else 32

        block = ctx.enter_context(nc.Block())

        @block.sync
        def _(sp):
            def load(loaded, halves):
                for dst, src in halves:
                    sp.dma_start(dst, src).then_inc(loaded, 16)

            def in_unit(layer, unit, w, c0, n):
                d = wslot(layer, unit, n)
                load(full[layer][slot_of(layer, unit)], [(d[:, 4 * h:4 * h + 4, :], w[:, 4 * h:4 * h + 4, c0:c0 + n]) for h in range(2)])

            def out_unit(layer, unit, w, k0):
                d = wslot(layer, unit, 1024)
                load(full[layer][slot_of(layer, unit)], [(d[:, 2 * h:2 * h + 2, :], w[:, k0 + 2 * h:k0 + 2 * h + 2, :]) for h in range(2)])

            def moe_unit(layer, x_, part, e):
                d = moe_memory(layer, x_, part)
                if part < 2:
                    d = d.rearrange("p (k w f) -> p k w f", k=4, w=2)
                    pairs = [(d[:, :, w, :], v[layer, bass.ds(e, 1), :, 4 * part:4 * part + 4, :]
                              .rearrange("e p k f -> (e p) k f")) for w, v in enumerate((w1v, w3v))]
                else:
                    d = d.rearrange("p (k n) -> p k n", k=4)
                    pairs = [(d[:, 2 * h:2 * h + 2, :], w2v[layer, bass.ds(e, 1), :, 2 * h:2 * h + 2, :]
                              .rearrange("e p k n -> (e p) k n")) for h in range(2)]
                load(full[layer][moe_slot(layer, x_, part)], pairs)

            for t in range(NT):
                sp.dma_start(x[:, t, :], A["x"][0, P * t:P * t + P, :]).then_inc(in_x[t], 16)
            sp.dma_start(con[:, :], A["con"]).then_inc(in_con, 16)
            rows = lambda a: a.rearrange("(r c) -> r c", c=P)
            sp.dma_start(vrow[0:16, 0:P], A["mix_norm"].rearrange("l (r c) -> (l r) c", c=P)).then_inc(in_vec, 16)
            sp.dma_start(vrow[16:32, 0:P], A["ffn_norm"].rearrange("l (r c) -> (l r) c", c=P)).then_inc(in_vec, 16)
            sp.dma_start(vrow[32:36, 0:P], rows(A["hg_out_norm"][0])).then_inc(in_vec, 16)
            sp.dma_start(vrow[36:44, 0:P], A["hg_lb_logits"].rearrange("l (r c) -> (l r) c", c=P)).then_inc(in_vec, 16)
            sp.dma_start(vrow[44:60, 0:P], rows(A["od_out_norm"][0])).then_inc(in_vec, 16)
            sp.dma_start(vrow[0:96, P:2 * P], A["od_conv_w"][0].rearrange("j (r c) -> (j r) c", c=P)).then_inc(in_vec, 16)
            sp.dma_start(vrow[60:84, 0:P], rows(A["od_conv_b"][0])).then_inc(in_vec, 16)
            for layer in range(2):
                for v in range(MIX_UNITS[layer]):
                    if v >= RING:
                        sp.wait_ge(mixed[layer], v - RING + 1)
                    elif layer == 1:
                        sp.wait_ge(used[0], last_step * STEP_UNITS + finished(*((2, 0), (2, 1), (3, 0), (3, 1), (2, 2), (3, 2))[v]))
                    if layer == 0:
                        if v < len(EVEN):
                            in_unit(0, v, evin, *EVEN[v])
                        else:
                            out_unit(0, v, evout, 4 * OUT_BLOCKS[0][v - len(EVEN)])
                    else:
                        if v < len(ODD):
                            in_unit(1, v, odin, *ODD[v])
                        else:
                            out_unit(1, v, odout, 4 * OUT_BLOCKS[1][v - len(ODD)])
                for e, part in FIRST:
                    if part < 2 and e < 2:
                        sp.wait_ge(mixed[layer], MIX_UNITS[layer] - 5 + 2 * e + part)
                    elif part < 2:
                        sp.wait_ge(used[layer], finished(e - 2, part))
                    elif e == 0:
                        sp.wait_ge(*((on_ok, 1), (lm_ok, SSM_H))[layer])
                    elif e == 1:
                        sp.wait_ge(*((on_ok, 1), (o_var, SSM_G))[layer])
                    elif e == 2:
                        sp.wait_ge(mixed[layer], MIX_UNITS[layer] - 1)
                    else:
                        sp.wait_ge(mo_acc[layer], NT)
                    moe_unit(layer, e, part, e)
                sp.wait_ge(M[layer]["rt_ok"], 1)
                last_step = sp.value_load(rounds[0:1, 2 + layer:3 + layer], min_val=NGROUPS - 1, max_val=ROUNDS * NGROUPS - 1)
                with sp.Fori(0, last_step) as i:
                    for e in range(GROUP):
                        for part in range(3):
                            if part < 2 and e >= 2:
                                sp.wait_ge(used[layer], (i + 1) * STEP_UNITS + finished(e - 2, part))
                            else:
                                sp.wait_ge(used[layer], i * STEP_UNITS + finished(e + 2 if part < 2 else e, part))
                            moe_unit(layer, e, part, ((i + 1) % NGROUPS) * GROUP + e)
            for t in range(NT):
                sp.wait_ge(x_new, 12 + 2 * t + 2)
                sp.dma_start(out[0, P * t:P * t + P, :], x[:, t, :]).then_inc(stored, 16)
            sp.wait_ge(stored, 16 * NT)

        @block.tensor
        def _(pe):
            mm, tr = nc.tensor.matmul, nc.tensor.transpose

            def loaded(layer, unit):
                pe.wait_ge(full[layer][slot_of(layer, unit)], full_at(layer, unit))

            def norm_transposes(n):
                if n == 0:
                    pe.wait_ge(vec_ok, 1)
                for t in range(NT):
                    if n % 2 == 0:
                        pe.wait_ge(xn_ok, 2 * n + t + 1)
                    else:
                        pe.wait_ge(x_new, 4 * (n - 1) + 2 * t + 2)
                    src = x if n % 2 else xn
                    for k in range(KT):
                        c0 = 256 * (k % 2) + P * t
                        last = tr(bank[4 + k // 2][:, c0:c0 + P], src[:, t, P * k:P * k + P], ident)
                        if t == 1 and k % 2:
                            last.then_inc(hT_ps, 1)

            def hT_ready(n):
                pe.wait_ge(hT_v, 4 * n + 4)
                pe.wait_ge(hT_a, 4 * n + 4)

            def rows_product(layer, unit, n, banks):
                w = wslot(layer, unit, n)
                for t in range(NT):
                    for k in range(KT):
                        last = mm(bank[banks[t]][:, 0:n], hT[:, k, P * t:P * t + P], w[:, k, :], start=(k == 0), stop=(k == KT - 1))
                last.then_inc(mixed[layer], 1)

            def cols_product(layer, unit, banks):
                w = wslot(layer, unit, 512)
                for c in range(4):
                    for k in range(KT):
                        last = mm(bank[banks[c // 2]][:, 256 * (c % 2):256 * (c % 2) + 256], w[:, k, P * c:P * c + P],
                                  hT[:, k, :], start=(k == 0), stop=(k == KT - 1))
                last.then_inc(mixed[layer], 1)

            def pair_free(kind, n):
                k, m = PAIRED[PAIRED.index((kind, n)) - 2]
                if k == "unit":
                    pe.wait_ge(e_out, m + 1)
                else:
                    pe.wait_ge(lv_ok, m + 1)

            pe.wait_ge(in_con, 16)
            pe.wait_ge(in_vec, 16 * 7)
            tr(bank[7][:, 0:84], vrow[0:84, 0:P], ident[0:84, 0:84])
            tr(bank[7][:, 84:180], vrow[0:96, P:2 * P], ident[0:96, 0:96]).then_inc(vec_ps, 1)

            norm_transposes(0)
            hT_ready(0)
            for u in range(4):
                loaded(0, u)
                if u >= 2:
                    pe.wait_ge(e_out, u - 1)
                if u == 3:
                    cols_product(0, u, (2, 3))
                else:
                    rows_product(0, u, EVEN[u][1], ((0, 1), (2, 3))[u % 2])
            pe.wait_ge(rot_ok, 2)
            pe.wait_ge(vec_ok, 1)
            for s_ in range(8):
                for t in range(NT):
                    src = ro[:, t, 2 * s_:2 * s_ + 2, :].rearrange("p h d -> p (h d)")
                    last = tr(bank[4 + s_ // 2][:, 256 * (s_ % 2) + P * t:256 * (s_ % 2) + P * t + P], src, ident)
                if s_ % 2:
                    last.then_inc(rot_ps, 1)
            loaded(0, 4)
            pe.wait_ge(e_out, 3)
            cols_product(0, 4, PAIR["unit", 4])
            pe.wait_ge(rot_t, 4)
            for t in range(NT):
                n = P * (t + 1)
                for h in range(4):
                    r0 = 64 * (h % 2)
                    last = mm(bank[4 + 2 * t + h % 2][:, n * (h // 2):n * (h // 2) + n], tt_[r0:r0 + 64, 5 + h // 2, P * t:P * t + P],
                              tt_[r0:r0 + 64, 7, 0:n], start=True, stop=True)
                last.then_inc(ix_ps, 1)

            def unit(u):
                loaded(0, u)
                pair_free("unit", u)
                rows_product(0, u, 512, PAIR["unit", u])

            def score(b):
                t, heads = BATCHES[b]
                n = P * (t + 1)
                pe.wait_ge(ix_rel, 2)
                if b:
                    pe.wait_ge(at_o, b)
                for m, h in enumerate(heads):
                    r0, o = 64 * (h // 4), m % (len(heads) // 2)
                    last = mm(bank[4 + h // 4][:, n * o:n * o + n], tt_[r0:r0 + 64, h % 4, P * t:P * t + P],
                              tt_[r0:r0 + 64, 4, 0:n], start=True, stop=True)
                last.then_inc(ql_ps, 1)

            def turn(b):
                pe.wait_ge(at_exp, b + 1)
                for j in range(8):
                    last = tr(bank[6 + j // 4][:, P * (j % 4):P * (j % 4) + P], pr[:, P * j:P * j + P], ident)
                    if j % 4 == 3:
                        last.then_inc(at_tps, 1)

            def value(b):
                t, heads = BATCHES[b]
                pe.wait_ge(at_t, 2 * (b + 1))
                for m, h in enumerate(heads):
                    for s_ in range(t + 1):
                        j = m * (t + 1) + s_
                        last = mm(bank[4][:, 64 * m:64 * m + 64], pT[:, P * j:P * j + P], av[:, s_, 64 * (h // 4):64 * (h // 4) + 64],
                                  start=(s_ == 0), stop=(s_ == t))
                last.then_inc(pv_ps, 1)

            def level(v):
                if v == 0:
                    pe.wait_ge(k_ok, 1)
                    pe.wait_ge(e_out, 5)
                else:
                    pe.wait_ge(lv_x, v)
                pair_free("level", v)
                for t in range(NT if v < 8 else 1):
                    for h in range(HG):
                        o = bank[PAIR["level", v][t]][:, P * h:P * h + P]
                        if v == 0:
                            last = mm(o, kk[:, h, P * t:P * t + P], qT[:, h, P * t:P * t + P], start=True, stop=True)
                        else:
                            e, tq = xe[:, v % 2, h, :], t if v < 8 else 1
                            last = mm(o, e[:, P * t:P * t + P], e[:, P * tq:P * tq + P], start=True, stop=True)
                last.then_inc(lv_ps, 1)

            def hgrn_sum(_):
                pe.wait_ge(e_out, 7)
                pe.wait_ge(lv_ok, 9)
                for t in range(NT):
                    for h in range(HG):
                        for s_ in range(t + 1):
                            w = aX[:, h, :] if s_ < t else aT[:, t, h, :]
                            last = mm(bank[2 + t][:, P * h:P * h + P], w, vv[:, s_, P * h:P * h + P], start=(s_ == 0), stop=(s_ == t))
                    last.then_inc(ho_ps, 1)

            for kind, n in PE_ORDER:
                {"level": level, "unit": unit, "score": score, "turn": turn, "value": value, "sum": hgrn_sum}[kind](n)

            def out_projection(layer, src, dst, ready, banks_read):
                blocks = OUT_BLOCKS[layer]

                def transposes(u):
                    pe.wait_ge(*ready[u])
                    for b in (2 * u, 2 * u + 1):
                        if b >= 4:
                            pe.wait_ge(mo_t[layer], b - 3)
                        for i in range(2):
                            for t in range(NT):
                                k, c0 = 4 * blocks[u] + 2 * (b % 2) + i, 256 * i + P * t
                                last = tr(bank[4 + b % 4][:, c0:c0 + P], src[:, t, P * k:P * k + P], ident)
                        last.then_inc(mo_ps[layer], 1)

                def product(u):
                    unit = MIX_UNITS[layer] - len(blocks) + u
                    loaded(layer, unit)
                    pe.wait_ge(mo_t[layer], 2 * u + 2)
                    w = wslot(layer, unit, 1024)
                    end = u == len(blocks) - 1
                    for t in range(NT):
                        for k in range(4):
                            for h in range(2):
                                last = mm(bank[2 * t + h][:, :], dst[:, 4 * blocks[u] + k, P * t:P * t + P], w[:, k, 512 * h:512 * h + 512],
                                          start=(u == 0 and k == 0), stop=(end and k == 3))
                        if end:
                            last.then_inc(mo_acc[layer], 1)
                    if not end:
                        last.then_inc(mixed[layer], 1)

                transposes(0)
                pe.wait_ge(*banks_read)
                for u in range(1, len(blocks)):
                    if u > 1 or len(blocks) > 2:
                        transposes(u)
                        product(u - 1)
                    else:
                        product(u - 1)
                        transposes(u)
                product(len(blocks) - 1)

            out_projection(0, xn, hT, [(at_o, 3), (on_ok, 1)], (ov_ok, 2))

            def moe(layer, n):
                m = M[layer]
                norm_transposes(n)
                hT_ready(n)
                pe.wait_ge(in_small, 16 * 4)
                for t in range(NT):
                    for k in range(KT):
                        last = mm(bank[0][:, 36 * t:36 * t + 36], hT[:, k, P * t:P * t + P], wr[:, layer, k, :], start=(k == 0), stop=(k == KT - 1))
                last.then_inc(m["rt_ps"], 1)
                for a in (1, 2, 3, 0):
                    if a == 0:
                        pe.wait_ge(m["lg_ok"], 2)
                    mm(bank[a][:, :], zero_b[:, 0:P], zero_b, start=True, stop=False)
                pe.wait_ge(m["rt_sel"], 1)
                for t in range(NT):
                    for s_ in range(t + 1):
                        mm(bank[5][:, 32 * t:32 * t + 32], strict if s_ == t else ones[:, 0:P], s32[:, 0, s_, :], start=(s_ == 0), stop=(s_ == t))
                for s_ in range(NT):
                    last = mm(bank[5][:, 64:96], ones[:, 0:P], s32[:, 0, s_, :], start=(s_ == 0), stop=(s_ == NT - 1))
                last.then_inc(m["rk_ps"], 1)
                pe.wait_ge(m["rt_ok"], 1)
                nr = pe.value_load(rounds[0:1, layer:layer + 1], min_val=1, max_val=ROUNDS)
                pe.wait_ge(xn_ok, 2 * n + 2)
                with pe.Fori(0, nr * NGROUPS) as i:
                    pe.wait_ge(m["s_ok"], i + 1)
                    for k in range(KT):
                        for t in range(NT):
                            last = mm(bank[6 + k // 4][:, P * (k % 4):P * (k % 4) + P], xn[:, t, P * k:P * k + P],
                                      sel[:, 4 * t:4 * t + 4, :].rearrange("p e c -> p (e c)"), start=(t == 0), stop=(t == NT - 1))
                        if k % 4 == 3:
                            last.then_inc(m["ga_ps"], 1)
                        if k == 3:
                            pe.wait_ge(m["pg_ok"], i + 1)
                            for e in range(GROUP):
                                for t in range(NT):
                                    c0 = 256 * (e % 2) + P * t
                                    last = tr(bank[4 + e // 2][:, c0:c0 + P], pg[:, t, e, :, :].rearrange("p j c -> p (j c)"), ident)
                            last.then_inc(m["pt_ps"], 1)

                    def up(e, part):
                        first, more = moe_full(layer, e, part)
                        pe.wait_ge(full[layer][moe_slot(layer, e, part)], i * more + first)
                        w = moe_memory(layer, e, part).rearrange("p (k w f) -> p k w f", k=4, w=2)
                        for k in range(4):
                            for j in range(4):
                                last = mm(bank[4 + e % 2][32 * j:32 * j + 32, 0:256], xT[:, 4 * part + k, CAP * e:CAP * e + CAP],
                                          w[:, k, :, P * j:P * j + P], start=(part == 0 and k == 0), stop=(part == 1 and k == 3))
                        last.then_inc(used[layer], 1)

                    def turn(e):
                        pe.wait_ge(m["he_ok"], i * 4 + e + 1)
                        if e:
                            pe.wait_ge(m["yv_ok"], i * 4 + e)
                        tr(bank[6][:, 0:P], he[:, e % 2, :], ident).then_inc(m["ht_ps"], 1)

                    def down(e):
                        first, more = moe_full(layer, e, 2)
                        pe.wait_ge(full[layer][moe_slot(layer, e, 2)], i * more + first)
                        pe.wait_ge(m["ht_ok"], i * 4 + e + 1)
                        if e:
                            pe.wait_ge(m["ya_ok"], i * 4 + e)
                        w = moe_memory(layer, e, 2).rearrange("p (k n) -> p k n", k=4)
                        for h in range(2):
                            for j in range(4):
                                last = mm(bank[6 + h][32 * j:32 * j + 32, :], heT[:, e % 2, CAP * j:CAP * j + CAP],
                                          w[:, j, 512 * h:512 * h + 512], start=True, stop=True)
                        last.then_inc(used[layer], 1)

                    def scatter(e):
                        pe.wait_ge(m["yv_ok"], i * 4 + e + 1)
                        pe.wait_ge(m["ya_ok"], i * 4 + e + 1)
                        for t in range(NT):
                            for h in range(2):
                                last = mm(bank[2 * t + h][:, :], pgT[:, e, t, :], ys[:, e % 2, 512 * h:512 * h + 512], start=False, stop=False)
                        last.then_inc(m["scat"], 1)

                    pe.wait_ge(m["xt_ok"], i * 2 + 2)
                    pe.wait_ge(m["pt_ok"], i * 2 + 2)
                    up(0, 0); up(0, 1); up(1, 0); turn(0); down(0); up(1, 1)
                    up(2, 0); turn(1); down(1); scatter(0); up(2, 1)
                    up(3, 0); turn(2); down(2); scatter(1); up(3, 1)
                    scatter(2); turn(3); down(3); scatter(3)
                for t in range(NT):
                    for h in range(2):
                        last = mm(bank[2 * t + h][:, :], zero_b[:, 0:P], zero_b, start=False, stop=True)
                    last.then_inc(m["acc"], 1)

            moe(0, 1)

            norm_transposes(2)
            hT_ready(2)
            loaded(1, 0)
            w = wslot(1, 0, 32)
            for k in range(KT):
                last = mm(bank[4][0:32, 0:S], w[:, k, :], hT[:, k, :], start=(k == 0), stop=(k == KT - 1))
            last.then_inc(mixed[1], 1)

            def dt_rows():
                pe.wait_ge(dt_ok, 1)
                for t in range(NT):
                    mm(bank[5][:, 64 * t:64 * t + 32], dtT[:, P * t:P * t + P], ident[0:32, 0:32], start=True, stop=True)
                    last = mm(bank[5][:, 64 * t + 32:64 * t + 64], cumT[0:32, P * t:P * t + P], ident[0:32, 0:32], start=True, stop=True)
                last.then_inc(dn_ps, 1)

            def xs_rows(u):
                pe.wait_ge(act_ok, 8 + 4 * u + 4)
                if u == 2:
                    pe.wait_ge(xs_ok, 2)
                if u == 3:
                    pe.wait_ge(raw_in, 20)
                for t in range(NT):
                    for c in range(4):
                        last = tr(bank[XS_BANKS[u][t]][:, P * c:P * c + P], xsT[:, (4 * u + c) % 8, P * t:P * t + P], ident)
                last.then_inc(xs_ps, 1)

            def z_product(n):
                u, t, k = n // (NT * KT), n // KT % NT, n % KT
                if k == 0:
                    if t == 0:
                        loaded(1, 7 + u)
                    if u:
                        pe.wait_ge(z_ok, 2 * u - 1 + t)
                    elif t == 0:
                        pe.wait_ge(xs_ok, 4)
                w = wslot(1, 7 + u, 512)
                last = mm(bank[6 + t][:, :], hT[:, k, P * t:P * t + P], w[:, k, :], start=(k == 0), stop=(k == KT - 1))
                if k == KT - 1:
                    last.then_inc(*((z_ps, 1) if t == 0 else (mixed[1], 1)))

            for u in range(1, 7):
                loaded(1, u)
                if u >= 3:
                    pe.wait_ge(raw_in, 4 * (u - 2))
                cols_product(1, u, ((2, 3), (0, 1))[u % 2])
                if u == 1:
                    dt_rows()
                if u == 3:
                    pe.wait_ge(dn_ok, 1)
                if u >= 4:
                    xs_rows(u - 4)
            for n in range(Z_FIRST):
                z_product(n)
            xs_rows(3)
            pe.wait_ge(raw_in, 24)
            pe.wait_ge(xs_ok, 6)
            for g in range(SSM_G):
                b = CB_BANKS[g]
                mm(bank[b][:, 0:S], bT[:, g, 0:P], cT[:, g, :], start=True, stop=True)
                mm(bank[b][:, S:S + P], bT[:, g, P:S], cT[:, g, P:S], start=True, stop=True).then_inc(cb_ps, 1)

            def cum_rows(p):
                if p >= 2:
                    pe.wait_ge(cu_ok, 2 * p - 2)
                else:
                    pe.wait_ge(cb_ok, 4)
                for w in range(2):
                    h = 2 * p + w
                    last = mm(bank[4 + p % 2][:, S * w:S * w + S], ident[:, h:h + 1].to_broadcast([P, P]), cumT[:, :], start=True, stop=True)
                last.then_inc(cu_ps, 1)

            def y_head(h):
                g, o = h // 8, 64 * (h % 8)
                pe.wait_ge(lm_ok, h + 1)
                if h == 0:
                    pe.wait_ge(xs_ok, 8)
                if h % 8 == 0 and g >= 2:
                    pe.wait_ge(yy_ok, 2 * (g - 1))
                b = 2 * (g % 2)
                l_ = lw[:, h % NL, :]
                mm(bank[b][:, o:o + 64], l_[:, 0:P], xd[:, 0, 64 * h:64 * h + 64], start=True, stop=True)
                mm(bank[b + 1][:, o:o + 64], l_[:, P:2 * P], xd[:, 0, 64 * h:64 * h + 64], start=True, stop=False)
                mm(bank[b + 1][:, o:o + 64], l_[:, 2 * P:3 * P], xd[:, 1, 64 * h:64 * h + 64], start=False, stop=True).then_inc(yy_ps, 1)

            for p in range(2):
                cum_rows(p)
            for h in range(SSM_H):
                y_head(h)
                if h % 2 == 0 and h + 4 < SSM_H:
                    cum_rows(h // 2 + 2)
                for n in range(Z_FIRST + 2 * h, min(Z_FIRST + 2 * h + 2, Z_STEPS)):
                    z_product(n)
            out_projection(1, xs, yT, [(yn_ok, 2 * g + 2) for g in range(SSM_G)], (yy_ok, 8))
            moe(1, 3)

        @block.scalar
        def _(act):
            fn = nc.scalar.activation
            ch = Chain(act, ach)
            act.dma_start(lvl[:, :, :], A["lvl"]).then_inc(in_lvl, 16)
            act.dma_start(qkn[:, 0, :], A["at_q_norm"].to_broadcast([P, 64])).then_inc(in_even, 16)
            act.dma_start(qkn[:, 1, :], A["at_k_norm"].to_broadcast([P, 64])).then_inc(in_even, 16)

            def norm_root(n):
                for t in range(NT):
                    act.wait_ge(var_ok, 2 * n + t + 1)
                    ch.link(fn(st[:, 4 + t:5 + t], st[:, 2 + t:3 + t], ACT.Ln))
                    fn(st[:, 6 + t:7 + t], st[:, 4 + t:5 + t], ACT.Exp, scale=-0.5).then_inc(root_ok, 1)

            def norm_root_both(n):
                act.wait_ge(var_ok, 2 * n + 2)
                ch.link(fn(st[:, 4:6], st[:, 2:4], ACT.Ln))
                fn(st[:, 6:8], st[:, 4:6], ACT.Exp, scale=-0.5).then_inc(root_ok, 2)

            def norm_take(n, g0):
                for b in (1, 3):
                    act.wait_ge(hT_ps, 4 * n + b + 1)
                    for k in (2 * b, 2 * b + 1):
                        fn(hT[:, k, :], bank[4 + b][:, 256 * (k % 2):256 * (k % 2) + 256], ACT.Copy, scale=vT[:, g0 + k:g0 + k + 1]).then_inc(hT_a, 1)

            norm_root(0)
            act.wait_ge(lb_in, 1)
            fn(lbv[:, 8:16], lbv[:, 0:8], ACT.Exp).then_inc(lb_ex, 1)
            act.wait_ge(vec_ok, 1)
            norm_take(0, V_MIX)
            act.wait_ge(mixed[0], 1)
            for t in range(NT):
                fn(rb[:, t, 8:10, :], bank[t][:, 0:128], ACT.Copy)
                fn(av[:, t, :], bank[t][:, 128:256], ACT.Copy)
                last = fn(rb[:, t, 10:14, :], bank[t][:, 256:512], ACT.Copy)
            last.then_inc(e_out, 1)
            act.wait_ge(mixed[0], 2)
            for t in range(NT):
                fn(rb[:, t, 14, :], bank[2 + t][:, 0:64], ACT.Copy)
                fn(rb[:, t, 15, :], bank[2 + t][:, 0:64], ACT.Copy)
                last = fn(iw[:, t, :], bank[2 + t][:, 64:68], ACT.Copy)
            last.then_inc(e_out, 1)
            act.wait_ge(mixed[0], 3)
            for t in range(NT):
                last = fn(rb[:, t, 0:8, :].rearrange("p (i v) d -> p v i d", v=2), bank[t][:, :].rearrange("p (v i d) -> p v i d", v=2, i=4), ACT.Copy)
            last.then_inc(e_out, 1)
            act.wait_ge(qk_var, 1)
            ch.link(fn(st[:, 36:56], st[:, 16:36], ACT.Ln))
            fn(st[:, 36:56], st[:, 36:56], ACT.Exp, scale=-0.5).then_inc(qk_root, 1)
            act.wait_ge(mixed[0], 4)
            for c in range(2):
                fn(lb_[:, 2 * c:2 * c + 2, :], bank[2 + c][:, :], ACT.Sigmoid)
                last = fn(kk[:, 2 * c:2 * c + 2, :], bank[2 + c][:, :], ACT.Sigmoid, scale=-1.0)
            last.then_inc(e_out, 1)
            for b in range(4):
                act.wait_ge(rot_ps, b + 1)
                fn(tt_[:, 2 * b:2 * b + 2, :], bank[4 + b][:, :], ACT.Copy).then_inc(rot_t, 1)
            act.wait_ge(mixed[0], 5)
            for c in range(2):
                last = fn(qT[:, 2 * c:2 * c + 2, :], bank[PAIR["unit", 4][c]][:, :], ACT.Copy)
            last.then_inc(e_out, 1)
            act.wait_ge(rot_ok, 2)
            for t in range(NT):
                act.wait_ge(ix_ps, t + 1)
                if t:
                    act.wait_ge(ix_ok, 1)
                n = P * (t + 1)
                for r in range(2):
                    last = fn(rl[:, r:4:2, 0:n], bank[4 + 2 * t + r][:, 0:2 * n].rearrange("p (h s) -> p h s", h=2), ACT.Relu)
                last.then_inc(ix_rel, 1)
            act.wait_ge(f_lin, 1)
            fn(lb_[:, :, :], lb_[:, :, :], ACT.Ln).then_inc(f_log, 1)

            def unit(u):
                act.wait_ge(mixed[0], u + 1)
                for t in range(NT):
                    last = fn((vv, gg)[u - 5][:, t, :], bank[PAIR["unit", u][t]][:, :], (ACT.Copy, ACT.Silu)[u - 5])
                last.then_inc(e_out, 1)

            def level(v):
                act.wait_ge(ex_in, v)
                fn(ee[:, v % 2, :, :], ee[:, v % 2, :, :], ACT.Exp).then_inc(ex_out, 1)

            def score(b):
                t, heads = BATCHES[b]
                n = P * (t + 1)
                act.wait_ge(at_max, b + 1)
                for m in range(len(heads)):
                    last = fn(pr[:, n * m:n * m + n], pr[:, n * m:n * m + n], ACT.Exp, bias=sm[:, b, 8 + m:9 + m], accum_out=sm[:, b, 16 + m:17 + m])
                last.then_inc(at_exp, 1)

            def turn(b):
                for j in range(2):
                    act.wait_ge(at_tps, 2 * b + j + 1)
                    fn(pT[:, 512 * j:512 * j + 512], bank[6 + j][:, :], ACT.Copy).then_inc(at_t, 1)

            for kind, n in ACT_ORDER:
                {"level": level, "unit": unit, "score": score, "turn": turn}[kind](n)
            act.wait_ge(ho_var, 1)
            ch.link(fn(st[:, 36:44], st[:, 16:24], ACT.Ln))
            fn(st[:, 36:44], st[:, 36:44], ACT.Exp, scale=-0.5).then_inc(ho_root, 1)

            def out_take(layer, parts, dst, gain):
                for b in parts:
                    act.wait_ge(mo_ps[layer], b + 1)
                    for i in range(2):
                        k = 4 * OUT_BLOCKS[layer][b // 2] + 2 * (b % 2) + i
                        g = gain(k)
                        last = fn(dst[:, k, :], bank[4 + b % 4][:, 256 * i:256 * i + 256], ACT.Copy,
                                  scale=1.0 if g is None else vT[:, g:g + 1])
                    last.then_inc(mo_t[layer], 1)

            out_take(0, range(4), hT, lambda k: V_HG + k if k < 4 else None)

            def moe(layer, n):
                m = M[layer]
                norm_take(n, V_FFN + 8 * layer)
                norm_root_both(n)
                act.wait_ge(rms_ok, layer + 1)
                for t in range(NT):
                    fn(xn[:, t, :], x[:, t, :], ACT.Copy, scale=st[:, 8 + t:9 + t]).then_inc(xn_ok, 1)
                act.wait_ge(m["rt_in"], 2)
                fn(arg[:, :, :], arg[:, :, :], ACT.Exp).then_inc(m["rt_ex"], 1)
                act.wait_ge(m["rt_ok"], 1)
                nr = act.value_load(rounds[0:1, layer:layer + 1], min_val=1, max_val=ROUNDS)
                with act.Fori(0, nr * NGROUPS) as i:
                    act.wait_ge(m["pt_ps"], i + 1)
                    for b in range(2):
                        fn(pgT[:, 2 * b:2 * b + 2, :, :], bank[4 + b][:, :], ACT.Copy).then_inc(m["pt_ok"], 1)

                    def silu(e):
                        act.wait_ge(used[layer], i * STEP_UNITS + finished(e, 1))
                        fn(sg[:, e % 2, :], bank[4 + e % 2][:, 0:P], ACT.Silu).then_inc(m["si_ok"], 1)

                    def take(e):
                        act.wait_ge(used[layer], i * STEP_UNITS + finished(e, 2))
                        if e >= 2:
                            act.wait_ge(m["scat"], i * 4 + e - 1)
                        fn(ys[:, e % 2, 512:1024], bank[7][:, :], ACT.Copy).then_inc(m["ya_ok"], 1)

                    for e in range(GROUP):
                        silu(e)
                        take(e)

            moe(0, 1)
            act.wait_ge(x_new, 5)
            act.dma_start(dts[:, 0:1], A["od_dt_bias"].rearrange("a h -> h a")).then_inc(in_odd, 16)
            act.dma_start(dts[:, 1:2], A["od_A_log"].rearrange("a h -> h a")).then_inc(in_odd, 16)
            act.dma_start(dsk[:, :], A["od_D"].to_broadcast([P, SSM_H])).then_inc(in_odd, 16)
            norm_root(2)
            norm_take(2, V_MIX + 8)
            act.wait_ge(in_odd, 48)
            fn(dts[:, 2:3], dts[:, 1:2], ACT.Exp).then_inc(al_ex, 1)
            act.wait_ge(dt_b, 1)
            fn(dtmp[:, 2, :], dtmp[:, 1, :], ACT.Exp).then_inc(dt_e, 1)
            act.wait_ge(dt_b, 2)
            fn(dtmp[:, 4, :], dtmp[:, 3, :], ACT.Ln).then_inc(dt_l, 1)

            def raw(c):
                u, q = 1 + c // 4, c % 4
                act.wait_ge(mixed[1], u + 1)
                if c >= 3:
                    act.wait_ge(cv_ok, c - 2)
                b = ((2, 3), (0, 1))[u % 2][q // 2]
                fn(cv[:, c % 3, 3:259], bank[b][:, 256 * (q % 2):256 * (q % 2) + 256], ACT.Copy).then_inc(raw_in, 1)

            def conv_silu(c):
                act.wait_ge(cv_ok, c + 1)
                if c >= 16:
                    act.wait_ge(xs_ps, (c - 8) // 4 - 1)
                dst = bT[:, c, :] if c < 4 else cT[:, c - 4, :] if c < 8 else xsT[:, c % 8, :]
                fn(dst, ca[:, c % 3, :], ACT.Silu).then_inc(act_ok, 1)

            for c in range(24):
                raw(c)
                if c:
                    conv_silu(c - 1)
            conv_silu(23)

            def z_take(j):
                u, t = j // 2, j % 2
                act.wait_ge(*((z_ps, u + 1) if t == 0 else (mixed[1], 8 + u)))
                fn(zz[:, t, 512 * u:512 * u + 512], bank[6 + t][:, :], ACT.Silu).then_inc(z_ok, 1)

            def y_root(g):
                act.wait_ge(o_var, g + 1)
                a = 36 + 2 * g
                ch.link(fn(st[:, a:a + 2], st[:, a - 20:a - 18], ACT.Ln))
                fn(st[:, a:a + 2], st[:, a:a + 2], ACT.Exp, scale=-0.5).then_inc(o_root, 1)

            for h in range(SSM_H):
                act.wait_ge(cu_ok, h + 1)
                fn(lw[:, h % NL, :], lw[:, h % NL, :], ACT.Exp).then_inc(lx_ok, 1)
                for j in range(2 * SSM_G):
                    if h == z_head(j):
                        z_take(j)
                if h % 8 == 6 and h > 8:
                    y_root(h // 8 - 1)
            out_take(1, range(4), yT, lambda k: V_OD + k)
            y_root(SSM_G - 1)
            out_take(1, range(4, 8), yT, lambda k: V_OD + k)
            moe(1, 3)

        @block.gpsimd
        def _(pool):
            g = nc.gpsimd
            ch = Chain(pool, pch)
            for l in range(2):
                pool.dma_start(wr[:, l, :, 0:4], A["moe_wg"][l].rearrange("(k p) n -> p k n", p=P)).then_inc(in_small, 16)
                pool.dma_start(wr[:, l, :, 4:36], A["moe_we"][l].rearrange("(k p) n -> p k n", p=P)).then_inc(in_small, 16)
                pool.dma_start(br[:, l, 0:4], A["moe_bg"][l:l + 1, :].to_broadcast([P, 4])).then_inc(in_rb, 16)
                pool.dma_start(br[:, l, 4:36], A["moe_be"][l:l + 1, :].to_broadcast([P, 32])).then_inc(in_rb, 16)
            pool.wait_ge(b_ok, 1)
            pool.wait_ge(rot_ps, 4)
            for v in range(1, 9):
                if v >= 3:
                    pool.wait_ge(lv_x, v - 2)
                b_, e_ = halves(bb[:, :, :], v), halves(ee[:, v % 2, :, :], v)
                ref = b_[:, :, 0, half(v) - 1:half(v)].to_broadcast([P, b_.shape[1], half(v)])
                g.tensor_tensor(e_[:, :, 0, :], ref, b_[:, :, 0, :], ALU.subtract)
                g.tensor_tensor(e_[:, :, 1, :], b_[:, :, 1, :], ref, ALU.subtract).then_inc(ex_in, 1)

            for m, layer in zip(M, range(2)):
                for source, tab in ((3, rtab), (2, gtab)):
                    pool.wait_ge(m["ga_ok"], 3)
                    for t in range(NT):
                        dst = tab[:, :, 4 * t:4 * t + 4].rearrange("p (r g) e -> p r g e", r=ROUNDS)
                        src = s32[:, source, t, :].rearrange("p (g e) -> p g e", g=NGROUPS).unsqueeze(1).to_broadcast([P, ROUNDS, NGROUPS, 4])
                        if source == 2:
                            g.tensor_copy(dst, src).then_inc(m["tab_ok"], 1)
                        else:
                            g.tensor_tensor(dst, src, thr1.unsqueeze(2).unsqueeze(3).to_broadcast([P, ROUNDS, NGROUPS, 4]), ALU.subtract).then_inc(m["tab_ok"], 1)

        @block.vector
        def _(dve):
            v_ = nc.vector
            ch = Chain(dve, dch)
            tt, ts, stt = v_.tensor_tensor, v_.tensor_scalar, v_.scalar_tensor_tensor
            bc = lambda a, shape: a.to_broadcast(shape)

            def newton(y, y0, var, tmp, done=None):
                ch.link(tt(tmp, y0, y0, ALU.mult))
                ch.link(tt(tmp, tmp, var, ALU.mult))
                ch.link(ts(tmp, tmp, -0.5, 1.5, ALU.mult, ALU.add))
                if done:
                    tt(y, y0, tmp, ALU.mult).then_inc(*done)
                else:
                    ch.link(tt(y, y0, tmp, ALU.mult))

            def norm(n, t):
                v_.tensor_tensor_reduce(out=xn[:, t, :], in0=x[:, t, :], in1=x[:, t, :], scale=1.0, scalar=0.0,
                                        op0=ALU.mult, op1=ALU.add, accum_out=st[:, t:t + 1]).then_inc(sq_ok, 1)
                dve.wait_ge(sq_ok, 2 * n + t + 1)
                ts(st[:, 2 + t:3 + t], st[:, t:t + 1], 1.0 / D, EPS, ALU.mult, ALU.add).then_inc(var_ok, 1)

            def norm_end(n, t):
                dve.wait_ge(var_ok, 2 * n + t + 1)
                dve.wait_ge(root_ok, 2 * n + t + 1)
                newton(st[:, 8 + t:9 + t], st[:, 6 + t:7 + t], st[:, 2 + t:3 + t], st[:, 10 + t:11 + t])
                ts(xn[:, t, :], x[:, t, :], st[:, 8 + t:9 + t], None, ALU.mult).then_inc(xn_ok, 1)

            def norm_take(n, g0):
                for b in (0, 2):
                    dve.wait_ge(hT_ps, 4 * n + b + 1)
                    for k in (2 * b, 2 * b + 1):
                        ts(hT[:, k, :], bank[4 + b][:, 256 * (k % 2):256 * (k % 2) + 256], vT[:, g0 + k:g0 + k + 1], None, ALU.mult).then_inc(hT_v, 1)

            def residual(n, ready):
                for t in range(NT):
                    dve.wait_ge(ready, t + 1)
                    for h in range(2):
                        tt(x[:, t, 512 * h:512 * h + 512], x[:, t, 512 * h:512 * h + 512], bank[2 * t + h][:, :], ALU.add).then_inc(x_new, 1)
                    if n == 1 or (n < 3 and t == 0):
                        dve.wait_ge(x_new, 4 * n + 2 * t + 2)
                        norm(n + 1, t)
                for t in range(NT if n == 1 else 0):
                    norm_end(n + 1, t)

            v_.memset(zeros[:, :], 0.0)
            v_.memset(ones[:, :], 1.0)
            ch.put(v_.memset(aT[:, :, :, :], 0.0))
            for t in range(NT):
                dve.wait_ge(in_x[t], 16)
                norm(0, t)
            for t in range(NT):
                norm_end(0, t)
            dve.wait_ge(vec_ps, 1)
            v_.tensor_copy(vT[:, 0:180], bank[7][:, 0:180]).then_inc(vec_ok, 1)
            dve.wait_ge(vec_ok, 1)
            l0, l1 = vT[:, V_LB:V_LB + 4], vT[:, V_LB + 4:V_LB + 8]
            ch.link(tt(lbv[:, 16:20], l0, l1, ALU.max))
            ch.put(tt(lbv[:, 0:4], l0, lbv[:, 16:20], ALU.subtract))
            tt(lbv[:, 4:8], l1, lbv[:, 16:20], ALU.subtract).then_inc(lb_in, 1)
            norm_take(0, V_MIX)
            dve.wait_ge(lb_ex, 1)
            ch.link(tt(lbv[:, 20:24], lbv[:, 8:12], lbv[:, 12:16], ALU.add))
            ch.link(v_.reciprocal(lbv[:, 24:28], lbv[:, 20:24]))
            ch.link(tt(lbv[:, 28:32], lbv[:, 8:12], lbv[:, 24:28], ALU.mult))
            ch.link(ts(lbv[:, 32:36], lbv[:, 28:32], -1.0, 1.0, ALU.mult, ALU.add))

            dve.wait_ge(e_out, 3)
            dve.wait_ge(in_even, 32)
            dve.wait_ge(in_con, 16)
            dve.wait_ge(in_lvl, 16)
            sq = ro[:, :, 0:10, :]
            for t in range(NT):
                ch.put(tt(ro[:, t, 0:10, :], rb[:, t, 0:10, :], rb[:, t, 0:10, :], ALU.mult))
            ch.wait()
            ch.link(v_.tensor_reduce(st[:, 16:36].rearrange("p (a h) -> p a h", a=2), sq, AX.X, ALU.add))
            ts(st[:, 16:36], st[:, 16:36], 1.0 / 64, EPS, ALU.mult, ALU.add).then_inc(qk_var, 1)
            dve.wait_ge(qk_root, 1)
            dve.wait_ge(qk_var, 1)
            rs = rt[:, 0, 0:20]
            newton(rs, st[:, 36:56], st[:, 16:36], rt[:, 1, 0:20])
            for t in range(NT):
                h10 = rb[:, t, 0:10, :]
                ch.link(tt(h10, h10, bc(rs[:, 10 * t:10 * t + 10].unsqueeze(2), [P, 10, 64]), ALU.mult))
                ch.put(tt(rb[:, t, 0:8, :], rb[:, t, 0:8, :], bc(qkn[:, 0:1, :], [P, 8, 64]), ALU.mult))
                ch.link(tt(rb[:, t, 8:10, :], rb[:, t, 8:10, :], bc(qkn[:, 1:2, :], [P, 2, 64]), ALU.mult))
            for t in range(NT):
                a1, a2 = rb[:, t, :, 0:32], rb[:, t, :, 32:64]
                cos, sin = bc(cs[:, t:t + 1, 0:32], [P, 16, 32]), bc(cs[:, t:t + 1, 32:64], [P, 16, 32])
                r = lambda n: rt[:, n, :].rearrange("p (h d) -> p h d", h=16)
                ch.put(tt(r(0), a1, cos, ALU.mult))
                ch.put(tt(r(1), a2, sin, ALU.mult))
                ch.put(tt(r(2), a2, cos, ALU.mult))
                ch.link(tt(r(3), a1, sin, ALU.mult))
                ch.put(tt(ro[:, t, :, 0:32], r(0), r(1), ALU.subtract))
                ch.wait()
                tt(ro[:, t, :, 32:64], r(2), r(3), ALU.add).then_inc(rot_ok, 1)
                dve.wait_ge(rot_ok, t + 1)
            dve.wait_ge(e_out, 4)
            for h in range(HG):
                last = ts(lb_[:, h, :], lb_[:, h, :], lbv[:, 32 + h:33 + h], lbv[:, 28 + h:29 + h], ALU.mult, ALU.add)
            last.then_inc(f_lin, 1)
            for h in range(HG):
                last = ts(kk[:, h, :], kk[:, h, :], lbv[:, 32 + h:33 + h], None, ALU.mult)
            last.then_inc(k_ok, 1)
            ch.put(ts(iw[:, :, :], iw[:, :, :], 0.125, None, ALU.mult))
            ch.wait()
            for t in range(NT):
                n = P * (t + 1)
                dve.wait_ge(ix_rel, t + 1)
                s_ = sc[:, t, 0:n]
                ch.link(ts(s_, rl[:, 0, 0:n], iw[:, t, 0:1], None, ALU.mult))
                for h in range(1, 4):
                    ch.link(stt(s_, rl[:, h, 0:n], iw[:, t, h:h + 1], s_, ALU.mult, ALU.add))
                tt(wk[:, t, 0:n], s_, adm[:, t, 0:n], ALU.add).then_inc(ix_ok, 1)
            dve.wait_ge(f_log, 1)
            for h in range(HG):
                last = v_.tensor_tensor_scan(bb[:, h, :], ones[:, :], lb_[:, h, :], 0.0, ALU.mult, ALU.add)
            last.then_inc(b_ok, 1)

            def top_keys(t):
                dve.wait_ge(ix_ok, t + 1)
                w = wk[:, t, 0:P * (t + 1)]
                for r in range(TOPK // 8):
                    ch.link(v_.max(mx8[:, t, :], w))
                    ch.link(v_.match_replace(w, mx8[:, t, :], w, GONE))
                ch.link(ts(sc[:, t, 0:P * (t + 1)], w, GONE, NEG, ALU.not_equal, ALU.mult))
            def take_level(v):
                pair = PAIR["level", v]
                dve.wait_ge(lv_ps, v + 1)
                if v == 8:
                    v_.tensor_copy(aX[:, :, :], bank[pair[0]][:, :]).then_inc(lv_ok, 1)
                    return
                for t in range(NT):
                    ins = v_.copy_predicated(aT[:, t, :, :], lvl[:, v:v + 1, :].to_broadcast([P, HG, P]),
                                             bank[pair[t]][:, :].rearrange("p (h t) -> p h t", h=HG))
                ins.then_inc(lv_ok, 1)
                dve.wait_ge(lv_ok, v + 1)

            def mix(v):
                dve.wait_ge(ex_out, v)
                if v == 1:
                    dve.wait_ge(e_out, 5)
                    dve.wait_ge(k_ok, 1)
                if v >= 3:
                    dve.wait_ge(lv_ps, v - 1)
                e_, x_ = halves(ee[:, v % 2, :, :], v), halves(xe[:, v % 2, :, :], v)
                tt(x_[:, :, 0, :], halves(kk[:, :, :], v)[:, :, 0, :], e_[:, :, 0, :], ALU.mult)
                tt(x_[:, :, 1, :], halves(qT[:, :, :], v)[:, :, 1, :], e_[:, :, 1, :], ALU.mult).then_inc(lv_x, 1)

            def score(b):
                t, heads = BATCHES[b]
                n, nh = P * (t + 1), len(heads)
                dve.wait_ge(ql_ps, b + 1)
                for m, h in enumerate(heads):
                    o = m % (nh // 2)
                    ch.put(v_.tensor_tensor_reduce(out=pr[:, n * m:n * m + n], in0=bank[4 + h // 4][:, n * o:n * o + n], in1=sc[:, t, 0:n],
                                                   scale=0.125, scalar=-3.0e38, op0=ALU.add, op1=ALU.max, accum_out=sm[:, b, m:m + 1]))
                ch.wait()
                ts(sm[:, b, 8:8 + nh], sm[:, b, 0:nh], -1.0, None, ALU.mult).then_inc(at_max, 1)

            def value(b):
                t, heads = BATCHES[b]
                nh = len(heads)
                dve.wait_ge(at_exp, b + 1)
                ch.link(v_.reciprocal(sm[:, b, 24:24 + nh], sm[:, b, 16:16 + nh]))
                dve.wait_ge(pv_ps, b + 1)
                dst = xn[:, t, 512:1024].rearrange("p (v h d) -> p v h d", v=2, h=4)[:, :, heads[0]:heads[0] + nh // 2, :]
                tt(dst, bank[4][:, 0:64 * nh].rearrange("p (v h d) -> p v h d", v=2, h=nh // 2),
                   bc(sm[:, b, 24:24 + nh].rearrange("p (v h) -> p v h", v=2).unsqueeze(3), [P, 2, nh // 2, 64]), ALU.mult).then_inc(at_o, 1)

            ov = lb_[:, :, :].rearrange("p h t -> p (h t)").rearrange("p (a n) -> p a n", a=2)

            def hgrn_sum(_):
                for t in range(NT):
                    dve.wait_ge(ho_ps, t + 1)
                    v_.tensor_copy(ov[:, t, :], bank[2 + t][:, :]).then_inc(ov_ok, 1)

            for kind, n in DVE_ORDER:
                {"level": take_level, "mix": mix, "keys": top_keys, "score": score, "value": value, "sum": hgrn_sum}[kind](n)
            sqv = kk[:, :, :].rearrange("p h t -> p (h t)").rearrange("p (a n) -> p a n", a=2)
            dve.wait_ge(ov_ok, 2)
            ch.link(tt(sqv, ov, ov, ALU.mult))
            ch.link(v_.tensor_reduce(st[:, 24:32], sqv.rearrange("p a (h d) -> p (a h) d", h=4), AX.X, ALU.add))
            ts(st[:, 16:24], st[:, 24:32], 1.0 / P, EPS, ALU.mult, ALU.add).then_inc(ho_var, 1)
            dve.wait_ge(e_out, 7)
            ch.link(tt(ov, ov, gg[:, :, :], ALU.mult))
            dve.wait_ge(ho_root, 1)
            newton(st[:, 44:52], st[:, 36:44], st[:, 16:24], st[:, 52:60])
            for t in range(NT):
                ins = tt(xn[:, t, 0:512].rearrange("p (h d) -> p h d", h=4), ov[:, t, :].rearrange("p (h d) -> p h d", h=4),
                         bc(st[:, 44 + 4 * t:48 + 4 * t].unsqueeze(2), [P, 4, P]), ALU.mult)
            ins.then_inc(on_ok, 1)
            residual(0, mo_acc[0])

            def moe(layer, n):
                m = M[layer]
                for a in (gp[:, :, 0:8], gp[:, :, 12:16], ep[:, :, 0:8], m8[:, 1, :, :], m8[:, 3, :, :]):
                    ch.put(v_.memset(a, NEG))
                norm_take(n, V_FFN + 8 * layer)
                dve.wait_ge(x_new, 4 * n)
                norm(n, 1)
                dve.wait_ge(var_ok, 2 * n + 2)
                dve.wait_ge(root_ok, 2 * n + 2)
                newton(st[:, 8:10], st[:, 6:8], st[:, 2:4], st[:, 10:12], (rms_ok, 1))
                dve.wait_ge(rms_ok, layer + 1)
                dve.wait_ge(m["rt_ps"], 1)
                dve.wait_ge(in_rb, 64)
                ch.wait()
                for t in range(NT):
                    stt(lg[:, t, :], bank[0][:, 36 * t:36 * t + 36], st[:, 8 + t:9 + t], br[:, layer, :], ALU.mult, ALU.add).then_inc(m["lg_ok"], 1)
                dve.wait_ge(m["lg_ok"], 2)
                ch.link(v_.tensor_copy(gp[:, :, 8:12], lg[:, :, 0:4]))
                for t in range(NT):
                    ch.put(v_.max(m8[:, 0, t, :], gp[:, t, :]))
                ch.wait()
                ch.link(v_.tensor_copy(m8[:, 1, :, 0:1], m8[:, 0, :, 0:1]))
                for t in range(NT):
                    ch.put(v_.match_replace(gr[:, t, :], m8[:, 1, t, :], gp[:, t, :], MARK))
                ch.wait()
                ch.link(ts(g4[:, 0, :, :], gr[:, :, 8:12], MARK, None, ALU.is_equal))
                ch.link(ts(g4[:, 1, :, :], g4[:, 0, :, :], 1.0, -NEG, ALU.subtract, ALU.mult))
                el = lg[:, :, 4:36].rearrange("p t (g e) -> p t g e", g=4)
                e_ = ep[:, :, 8:40].rearrange("p t (g e) -> p t g e", g=4)
                ch.link(tt(e_, el, bc(g4[:, 0, :, :].unsqueeze(3), [P, NT, 4, 8]), ALU.mult))
                ch.link(tt(e_, e_, bc(g4[:, 1, :, :].unsqueeze(3), [P, NT, 4, 8]), ALU.add))
                for t in range(NT):
                    ch.put(v_.max(m8[:, 2, t, :], ep[:, t, :]))
                ch.wait()
                ch.link(v_.tensor_copy(m8[:, 3, :, 0:2], m8[:, 2, :, 0:2]))
                for t in range(NT):
                    ch.put(v_.match_replace(er[:, t, :], m8[:, 3, t, :], ep[:, t, :], MARK))
                ch.wait()
                ts(s32[:, 0, :, :], er[:, :, 8:40], MARK, None, ALU.is_equal).then_inc(m["rt_sel"], 1)
                for t in range(NT):
                    ch.put(ts(arg[:, t, 0:4], lg[:, t, 0:4], m8[:, 0, t, 0:1], None, ALU.subtract))
                    ts(arg[:, t, 4:36], ep[:, t, 8:40], m8[:, 2, t, 0:1], None, ALU.subtract).then_inc(m["rt_in"], 1)
                dve.wait_ge(m["rt_sel"], 1)
                dve.wait_ge(m["rt_ex"], 1)
                red = lambda o, a: ch.link(v_.tensor_reduce(o, a, AX.X, ALU.add))
                red(st[:, 16:18], arg[:, :, 0:4])
                red(st[:, 18:20], arg[:, :, 4:36])
                ch.link(v_.reciprocal(st[:, 20:24], st[:, 16:20]))
                for t in range(NT):
                    ch.put(stt(s32[:, 1, t, :], arg[:, t, 4:36], st[:, 22 + t:23 + t], s32[:, 0, t, :], ALU.mult, ALU.mult))
                ch.wait()
                red(st[:, 24:26], s32[:, 1, :, :])
                ch.link(v_.reciprocal(st[:, 26:28], st[:, 24:26]))
                ch.link(tt(st[:, 28:30], st[:, 26:28], st[:, 20:22], ALU.mult))
                for t in range(NT):
                    ts(s32[:, 2, t, :], s32[:, 1, t, :], st[:, 28 + t:29 + t], None, ALU.mult).then_inc(m["ga_ok"], 1)
                dve.wait_ge(m["rk_ps"], 1)
                rk = s32[:, 3, :, :]
                stt(rk, bank[5][:, 0:64].rearrange("p (a e) -> p a e", a=2), 1.0, s32[:, 0, :, :], ALU.add, ALU.mult).then_inc(m["ga_ok"], 1)
                ch.link(v_.tensor_reduce(rr[:, 0:1], bank[5][:, 64:96], AX.X, ALU.max))
                ch.link(ts(rr[:, 8:16], thr, rr[:, 0:1], None, ALU.is_lt))
                ch.link(v_.tensor_reduce(rr[:, 1:2], rr[:, 8:16], AX.X, ALU.add))
                ch.link(ts(rr[:, 2:3], rr[:, 1:2], float(NGROUPS), -1.0, ALU.mult, ALU.add))
                ch.put(v_.tensor_copy(rounds[:, layer:layer + 1], rr[:, 1:2]))
                v_.tensor_copy(rounds[:, 2 + layer:3 + layer], rr[:, 2:3]).then_inc(m["rt_ok"], 1)
                dve.wait_ge(m["rt_ok"], 1)
                ch.wait()
                nr = dve.value_load(rounds[0:1, layer:layer + 1], min_val=1, max_val=ROUNDS)
                dve.wait_ge(m["tab_ok"], 2)
                with dve.Fori(0, nr * NGROUPS) as i:
                    tt(sel[:, :, :], bc(rtab[:, bass.ds(i, 1), :].rearrange("p a e -> p (a e)").unsqueeze(2), [P, 8, CAP]),
                       bc(iota.unsqueeze(1), [P, 8, CAP]), ALU.is_equal).then_inc(m["s_ok"], 1)
                    dve.wait_ge(m["s_ok"], i + 1)
                    dve.wait_ge(m["tab_ok"], 4)
                    for t in range(NT):
                        gt = gtab[:, bass.ds(i, 1), 4 * t:4 * t + 4].rearrange("p a e -> p (a e)").unsqueeze(2).unsqueeze(3)
                        ins = tt(pg[:, t, :, :, :], bc(sel[:, 4 * t:4 * t + 4, :].unsqueeze(2), [P, GROUP, 4, CAP]), bc(gt, [P, GROUP, 4, CAP]), ALU.mult)
                    ins.then_inc(m["pg_ok"], 1)
                    for b in range(2):
                        dve.wait_ge(m["ga_ps"], i * 2 + b + 1)
                        g0 = V_FFN + 8 * layer + 4 * b
                        tt(xT[:, 4 * b:4 * b + 4, :], bank[6 + b][:, :].rearrange("p (k c) -> p k c", k=4),
                           bc(vT[:, g0:g0 + 4].unsqueeze(2), [P, 4, P]), ALU.mult).then_inc(m["xt_ok"], 1)

                    def gate(e):
                        dve.wait_ge(m["si_ok"], i * 4 + e + 1)
                        tt(he[:, e % 2, :], sg[:, e % 2, :], bank[4 + e % 2][:, P:2 * P], ALU.mult).then_inc(m["he_ok"], 1)

                    def turned(e):
                        dve.wait_ge(m["ht_ps"], i * 4 + e + 1)
                        v_.tensor_copy(heT[:, e % 2, :], bank[6][:, 0:P]).then_inc(m["ht_ok"], 1)

                    def take(e):
                        dve.wait_ge(used[layer], i * STEP_UNITS + finished(e, 2))
                        if e >= 2:
                            dve.wait_ge(m["scat"], i * 4 + e - 1)
                        v_.tensor_copy(ys[:, e % 2, 0:512], bank[6][:, :]).then_inc(m["yv_ok"], 1)

                    for e in range(GROUP):
                        gate(e)
                        turned(e)
                        take(e)
                residual(n, m["acc"])

            moe(0, 1)

            ch.put(v_.memset(cumT[:, :], 0.0))
            for s_ in range(3):
                ch.put(v_.memset(cv[:, s_, 0:3], 0.0))
            norm_take(2, V_MIX + 8)
            dve.wait_ge(in_odd, 48)
            dve.wait_ge(mixed[1], 1)
            ch.link(ts(dtmp[:, 0, :], bank[4][0:32, 0:S], dts[:, 0:1], None, ALU.add))
            ch.link(ts(dtmp[:, 5, :], dtmp[:, 0, :], -1.0, None, ALU.mult))
            ts(dtmp[:, 6, :], dtmp[:, 0, :], 0.0, None, ALU.max).then_inc(al_in, 1)
            tt(dtmp[:, 1, :], dtmp[:, 0, :], dtmp[:, 5, :], ALU.min).then_inc(dt_b, 1)
            dve.wait_ge(al_ex, 1)
            ch.link(ts(dts[:, 3:4], dts[:, 2:3], -1.0, None, ALU.mult))
            dve.wait_ge(dt_e, 1)
            ts(dtmp[:, 3, :], dtmp[:, 2, :], 1.0, None, ALU.add).then_inc(dt_b, 1)
            dve.wait_ge(dt_b, 2)
            ch.link(ts(dtmp[:, 5, :], dtmp[:, 3, :], 1.0, None, ALU.subtract))
            ch.link(tt(dtmp[:, 5, :], dtmp[:, 2, :], dtmp[:, 5, :], ALU.subtract))
            ch.link(v_.reciprocal(dtmp[:, 7, :], dtmp[:, 3, :]))
            ch.link(tt(dtmp[:, 5, :], dtmp[:, 5, :], dtmp[:, 7, :], ALU.mult))
            dve.wait_ge(al_in, 1)
            ch.link(tt(dtmp[:, 6, :], dtmp[:, 6, :], dtmp[:, 5, :], ALU.add))
            dve.wait_ge(dt_l, 1)
            ch.link(tt(dtT[:, :], dtmp[:, 6, :], dtmp[:, 4, :], ALU.add))
            ch.link(ts(dtmp[:, 7, :], dtT[:, :], dts[:, 3:4], None, ALU.mult))
            v_.tensor_tensor_scan(cumT[0:32, :], ones[0:32, :], dtmp[:, 7, :], 0.0, ALU.mult, ALU.add).then_inc(dt_ok, 1)

            def conv(c):
                dve.wait_ge(raw_in, c + 1)
                if c >= 3:
                    dve.wait_ge(act_ok, c - 2)
                src, dst = cv[:, c % 3, :], ca[:, c % 3, :]
                w = lambda j: vT[:, V_CW + 24 * j + ct(c):V_CW + 24 * j + ct(c) + 1]
                ch.link(ts(dst, src[:, 3:259], w(3), vT[:, V_CB + ct(c):V_CB + ct(c) + 1], ALU.mult, ALU.add))
                ch.link(stt(dst, src[:, 2:258], w(2), dst, ALU.mult, ALU.add))
                ch.link(stt(dst, src[:, 1:257], w(1), dst, ALU.mult, ALU.add))
                stt(dst, src[:, 0:256], w(0), dst, ALU.mult, ALU.add).then_inc(cv_ok, 1)

            def ct(c):
                return 16 + c if c < 8 else c - 8

            def xs_take(u):
                dve.wait_ge(xs_ps, u + 1)
                for t in range(NT):
                    src = bank[XS_BANKS[u][t]][:, :].rearrange("p (h d) -> p h d", h=8)
                    ch.put(tt(xd[:, t, 512 * u:512 * u + 512].rearrange("p (h d) -> p h d", h=8), src,
                              bc(dnat[:, t, 0, 8 * u:8 * u + 8].unsqueeze(2), [P, 8, 64]), ALU.mult))
                    ch.wait()
                    tt(xs[:, t, 512 * u:512 * u + 512].rearrange("p (h d) -> p h d", h=8), src,
                       bc(dsk[:, 8 * u:8 * u + 8].unsqueeze(2), [P, 8, 64]), ALU.mult).then_inc(xs_ok, 1)

            for c in range(24):
                conv(c)
                if c == 3:
                    dve.wait_ge(dn_ps, 1)
                    v_.tensor_copy(dnat[:, :, :, :], bank[5][:, 0:128].rearrange("p (a w h) -> p a w h", a=2, w=2)).then_inc(dn_ok, 1)
                    dve.wait_ge(dn_ok, 1)
                if c in (15, 19, 23):
                    xs_take(c // 4 - 3)
            xs_take(3)
            dve.wait_ge(xs_ok, 8)
            for g in range(SSM_G):
                dve.wait_ge(cb_ps, g + 1)
                tt(cbm[:, g, :], bank[CB_BANKS[g]][:, 0:384], mask3, ALU.mult).then_inc(cb_ok, 1)
            dve.wait_ge(cb_ok, 4)

            def decay(h):
                dve.wait_ge(cu_ps, h // 2 + 1)
                if h >= NL:
                    dve.wait_ge(yy_ps, h - NL + 1)
                l_, b = lw[:, h % NL, :], bank[4 + h // 2 % 2][:, S * (h % 2):S * (h % 2) + S]
                ch.put(ts(l_[:, 0:S], b[:, 0:S], dnat[:, 0, 1, h:h + 1], 0.0, ALU.subtract, ALU.min))
                ch.wait()
                ts(l_[:, S:S + P], b[:, P:S], dnat[:, 1, 1, h:h + 1], 0.0, ALU.subtract, ALU.min).then_inc(cu_ok, 1)

            def weigh(h):
                dve.wait_ge(lx_ok, h + 1)
                tt(lw[:, h % NL, :], lw[:, h % NL, :], cbm[:, h // 8, :], ALU.mult).then_inc(lm_ok, 1)

            def y_add(g):
                dve.wait_ge(yy_ps, 8 * g + 8)
                for t in range(NT):
                    yv = xs[:, t, 512 * g:512 * g + 512]
                    tt(yv, yv, bank[2 * (g % 2) + t][:, :], ALU.add).then_inc(yy_ok, 1)

            def y_gate(g):
                dve.wait_ge(yy_ok, 2 * g + 2)
                dve.wait_ge(z_ok, 2 * g + 2)
                yv = xs[:, :, 512 * g:512 * g + 512]
                ch.link(tt(yv, yv, zz[:, :, 512 * g:512 * g + 512], ALU.mult))
                for t in range(NT):
                    ch.put(v_.tensor_tensor_reduce(out=zz[:, t, 512 * g:512 * g + 512], in0=xs[:, t, 512 * g:512 * g + 512],
                                                   in1=xs[:, t, 512 * g:512 * g + 512], scale=1.0, scalar=0.0, op0=ALU.mult, op1=ALU.add,
                                                   accum_out=st[:, 24 + 2 * g + t:25 + 2 * g + t]))
                ch.wait()
                ts(st[:, 16 + 2 * g:18 + 2 * g], st[:, 24 + 2 * g:26 + 2 * g], 1.0 / 512, EPS, ALU.mult, ALU.add).then_inc(o_var, 1)

            def y_norm(g):
                a = 2 * g
                dve.wait_ge(o_root, g + 1)
                newton(st[:, 44 + a:46 + a], st[:, 36 + a:38 + a], st[:, 16 + a:18 + a], st[:, 52 + a:54 + a])
                for t in range(NT):
                    yv = xs[:, t, 512 * g:512 * g + 512]
                    ts(yv, yv, st[:, 44 + a + t:45 + a + t], None, ALU.mult).then_inc(yn_ok, 1)

            for h in range(AHEAD):
                decay(h)
            for h in range(SSM_H):
                weigh(h)
                if h + AHEAD < SSM_H:
                    decay(h + AHEAD)
                if h > 8:
                    {1: y_add, 2: y_gate, 5: y_norm}.get(h % 8, lambda g: None)(h // 8 - 1)
            y_add(SSM_G - 1)
            y_gate(SSM_G - 1)
            y_norm(SSM_G - 1)
            residual(2, mo_acc[1])
            moe(1, 3)


_INPUTS = ["x", "mix_norm", "ffn_norm", "ev_w_in", "hg_lb_logits", "hg_out_norm", "at_q_norm", "at_k_norm", "ev_w_out", "od_w_in",
           "od_conv_w", "od_conv_b", "od_dt_bias", "od_A_log", "od_D", "od_out_norm", "od_w_out", "moe_wg", "moe_bg", "moe_we",
           "moe_be", "moe_w1", "moe_w3", "moe_w2"]


def constants():
    p = np.arange(P)
    con = np.zeros((P, C_END), np.float32)
    con[:, C_ID:C_ID + P] = np.eye(P)
    upto = (p[:, None] <= p[None, :]).astype(np.float32)
    con[:, C_M3:C_M3 + 384] = np.concatenate([upto, np.ones((P, P)), upto], 1)
    con[:, C_STRICT:C_STRICT + P] = p[:, None] < p[None, :]
    for t in range(NT):
        q_chunk, k_chunk = (P * t + p) // 64, np.arange(S) // 64
        con[:, C_ADM + S * t:C_ADM + S * (t + 1)] = np.where(k_chunk[None, :] <= q_chunk[:, None], 0.0, NEG)
        inv = np.exp(np.float32(-np.log(10000.0)) * np.arange(32, dtype=np.float32) / np.float32(32)).astype(np.float32)
        ang = (P * t + p).astype(np.float32)[:, None] * inv[None, :]
        con[:, C_CS + 64 * t:C_CS + 64 * t + 32] = np.cos(ang)
        con[:, C_CS + 64 * t + 32:C_CS + 64 * t + 64] = np.sin(ang)
    con[:, C_IOTA:C_IOTA + 32] = np.arange(32)
    con[:, C_THR:C_THR + 8] = CAP * np.arange(8)
    con[:, C_THR + 8:C_THR + 16] = CAP * np.arange(8) + 1
    lvl = np.zeros((P, 8, P), np.int32)
    lvl[:, 0, :] = np.eye(P)
    for v in range(1, 8):
        half = 64 >> (v - 1)
        s_, t_ = p[:, None], p[None, :]
        lvl[:, v, :] = (s_ // (2 * half) == t_ // (2 * half)) & (s_ // half % 2 == 0) & (t_ // half % 2 == 1)
    return con, lvl


def kernel(**inputs):
    import concourse.bacc as bacc
    from concourse import mybir
    from concourse.bass_utils import run_bass_kernel_spmd

    nc = bacc.Bacc("TRN2", target_bir_lowering=False, num_devices=1)
    con, lvl = constants()
    arrays, A = {}, {}
    for name, a in [(n, inputs[n]) for n in _INPUTS] + [("con", con), ("lvl", lvl)]:
        a = np.ascontiguousarray(a)
        arrays["in_" + name] = a
        A[name] = nc.dram_tensor("in_" + name, a.shape, mybir.dt.from_np(a.dtype), kind="ExternalInput").ap()
    out = nc.dram_tensor("out", (1, S, D), mybir.dt.float32, kind="ExternalOutput").ap()
    build(nc, A, out)
    r = run_bass_kernel_spmd(nc, [arrays], core_ids=[0])
    return r.results[0]["out"]
```
